# Optimizing a Trainium2 kernel written in Bass

```python
import math
import jax, jax.numpy as jnp
from jax import lax
import numpy as np

D_MODEL = 1024
BATCH = 1
SEQ = 512
DEPTH = 2

D_FF = 2816
EPS = 1e-6
FOURIER_GROUPS = 8
FOURIER_GROUP_DIM = 128
FOURIER_WIDTH = FOURIER_GROUPS * FOURIER_GROUP_DIM
DIL_PAIRS = ((128, 1), (512, 4), (2048, 16))
DIL_HEADS_PER_GROUP = 2
DIL_HEAD_DIM = 64
DIL_HEADS = DIL_HEADS_PER_GROUP * len(DIL_PAIRS)
DIL_WIDTH = DIL_HEADS * DIL_HEAD_DIM
DIL_OUT_WIDTH = DIL_HEADS_PER_GROUP * DIL_HEAD_DIM
DIFF_HEADS = 4
DIFF_HEAD_DIM = 64
DIFF_QK_WIDTH = DIFF_HEADS * 2 * DIFF_HEAD_DIM
DIFF_V_DIM = 2 * DIFF_HEAD_DIM
DIFF_V_WIDTH = DIFF_HEADS * DIFF_V_DIM
SUBLN_EPS = 1e-5
Q_BLOCK = 128
IN_WIDTH = FOURIER_WIDTH + 3 * DIL_WIDTH + 2 * DIFF_QK_WIDTH + DIFF_V_WIDTH
N_BRANCHES = 3
NUM_BUCKETS = 32
MAX_DISTANCE = 1024
N_BIAS_HEADS = DIL_HEADS + DIFF_HEADS
NEG_INF = -1e30


def rmsnorm(x, g, eps=EPS):
    xf = x.astype(jnp.float32)
    y = xf * lax.rsqrt(jnp.mean(xf * xf, axis=-1, keepdims=True) + eps)
    return (y * g.astype(jnp.float32)).astype(x.dtype)

def swiglu(h, w_gate, w_up, w_down):
    return (jax.nn.silu(h @ w_gate) * (h @ w_up)) @ w_down

def rel_bucket(rel):
    half = NUM_BUCKETS // 2
    max_exact = half // 2
    ret = jnp.where(rel > 0, half, 0)
    n = jnp.abs(rel)
    nf = jnp.maximum(n, 1).astype(jnp.float32)
    large = max_exact + (jnp.log(nf / max_exact) / math.log(MAX_DISTANCE / max_exact)
                         * (half - max_exact)).astype(jnp.int32)
    large = jnp.minimum(large, half - 1)
    return ret + jnp.where(n < max_exact, n, large)

def fourier_mix(a):
    Bsz, S, _ = a.shape
    ag = a.astype(jnp.float32).reshape(Bsz, S, FOURIER_GROUPS, FOURIER_GROUP_DIM)
    y = jnp.fft.fftn(ag, axes=(1, 3), norm="ortho").real
    return y.reshape(Bsz, S, FOURIER_WIDTH).astype(a.dtype)

def dilated_window_attention(q, k, v, bias_cols, window, dil):
    Bsz, S, H, dh = q.shape
    radius = window // (2 * dil)
    blk = radius
    L = S // dil
    nb = -(-L // blk)
    Lp = nb * blk

    def to_sub(t):
        t = t.reshape(Bsz, L, dil, H, dh).transpose(0, 2, 3, 1, 4)
        return jnp.pad(t, ((0, 0), (0, 0), (0, 0), (0, Lp - L), (0, 0)))

    def windows(t):
        tp = jnp.pad(to_sub(t), ((0, 0), (0, 0), (0, 0), (blk, blk), (0, 0)))
        tp = tp.reshape(Bsz, dil, H, nb + 2, blk, dh)
        return jnp.concatenate([tp[:, :, :, :-2], tp[:, :, :, 1:-1], tp[:, :, :, 2:]], axis=4)

    qs = to_sub(q).reshape(Bsz, dil, H, nb, blk, dh).astype(jnp.float32)
    kw = windows(k).astype(jnp.float32)
    vw = windows(v).astype(jnp.float32)

    i = jnp.arange(blk)[:, None]
    m = jnp.arange(3 * blk)[None, :]
    rel_t = m - blk - i
    bias = bias_cols[rel_bucket(rel_t * dil)].astype(jnp.float32)
    bias = jnp.transpose(bias, (2, 0, 1))
    tk = (jnp.arange(nb)[:, None, None] - 1) * blk + m[None]
    valid = (jnp.abs(rel_t) <= radius)[None] & (tk >= 0) & (tk < L)

    logits = jnp.einsum('bdhjqc,bdhjkc->bdhjqk', qs, kw) * (dh ** -0.5)
    logits = logits + bias[None, None, :, None]
    logits = jnp.where(valid, logits, NEG_INF)
    lse = jax.nn.logsumexp(logits, axis=-1)
    p = jnp.exp(logits - lse[..., None])
    o = jnp.einsum('bdhjqk,bdhjkc->bdhjqc', p, vw)

    o = o.reshape(Bsz, dil, H, Lp, dh)[:, :, :, :L].transpose(0, 3, 1, 2, 4).reshape(Bsz, S, H, dh)
    lse = lse.reshape(Bsz, dil, H, Lp)[:, :, :, :L].transpose(0, 3, 1, 2).reshape(Bsz, S, H)
    return o, lse

def dilated_mixture(qb, kb, vb, rel_bias):
    Bsz, S, _ = qb.shape
    q = qb.reshape(Bsz, S, DIL_HEADS, DIL_HEAD_DIM)
    k = kb.reshape(Bsz, S, DIL_HEADS, DIL_HEAD_DIM)
    v = vb.reshape(Bsz, S, DIL_HEADS, DIL_HEAD_DIM)
    outs, lses = [], []
    for g, (window, dil) in enumerate(DIL_PAIRS):
        hs = slice(g * DIL_HEADS_PER_GROUP, (g + 1) * DIL_HEADS_PER_GROUP)
        o, lse = dilated_window_attention(q[:, :, hs], k[:, :, hs], v[:, :, hs],
                                          rel_bias[:, hs], window, dil)
        outs.append(o)
        lses.append(lse)
    o = jnp.stack(outs, axis=0)
    w = jax.nn.softmax(jnp.stack(lses, axis=0), axis=0)
    y = jnp.sum(w[..., None] * o, axis=0)
    return y.reshape(Bsz, S, DIL_OUT_WIDTH).astype(qb.dtype)

def diff_attention(qc, kc, vc, bias_cols, lam, subln_g, lam_init):
    Bsz, S, _ = qc.shape
    H, dh = DIFF_HEADS, DIFF_HEAD_DIM
    nq = S // Q_BLOCK
    qb = qc.reshape(Bsz, nq, Q_BLOCK, H, 2, dh).transpose(1, 0, 2, 3, 4, 5).astype(jnp.float32)
    kf = kc.reshape(Bsz, S, H, 2, dh).astype(jnp.float32)
    vf = vc.reshape(Bsz, S, H, DIFF_V_DIM).astype(jnp.float32)
    kpos = jnp.arange(S)
    scale = dh ** -0.5

    def one_block(args):
        j, qj = args
        qpos = j * Q_BLOCK + jnp.arange(Q_BLOCK)
        bias = bias_cols[rel_bucket(kpos[None, :] - qpos[:, None])].astype(jnp.float32)
        bias = jnp.transpose(bias, (2, 0, 1))
        logits = jnp.einsum('bqhmc,bkhmc->bhmqk', qj, kf) * scale + bias[None, :, None]
        p = jax.nn.softmax(logits, axis=-1)
        a = p[:, :, 0] - lam * p[:, :, 1]
        return jnp.einsum('bhqk,bkhe->bqhe', a, vf)

    o = lax.map(one_block, (jnp.arange(nq), qb))
    o = o.transpose(1, 0, 2, 3, 4).reshape(Bsz, S, H, DIFF_V_DIM)
    o = rmsnorm(o, subln_g, SUBLN_EPS) * (1.0 - lam_init)
    return o.reshape(Bsz, S, DIFF_V_WIDTH).astype(qc.dtype)

def first_inputs(seed: int = 0) -> dict:
    key = jax.random.key(seed)
    ks = jax.random.split(key, 26)

    def nrm(k, shape, fan_in):
        return jax.random.normal(k, shape, jnp.float32) * (fan_in ** -0.5)

    def gain(k, shape):
        return 1.0 + 0.05 * jax.random.normal(k, shape, jnp.float32)

    L = DEPTH
    return {
        "x": jax.random.normal(ks[0], (BATCH, SEQ, D_MODEL), jnp.float32),
        "g_ffn1": gain(ks[1], (L, D_MODEL)),
        "w_ffn1_gate": nrm(ks[2], (L, D_MODEL, D_FF), D_MODEL),
        "w_ffn1_up": nrm(ks[3], (L, D_MODEL, D_FF), D_MODEL),
        "w_ffn1_down": nrm(ks[4], (L, D_FF, D_MODEL), D_FF),
        "g_mix": gain(ks[5], (L, D_MODEL)),
        "w_in": nrm(ks[6], (L, D_MODEL, IN_WIDTH), D_MODEL),
        "w_gate": nrm(ks[7], (L, D_MODEL, N_BRANCHES * D_MODEL), D_MODEL),
        "b_gate": 0.02 * jax.random.normal(ks[8], (L, N_BRANCHES * D_MODEL), jnp.float32),
        "w_br_a": nrm(ks[9], (L, FOURIER_WIDTH, D_MODEL), FOURIER_WIDTH),
        "w_br_b": nrm(ks[10], (L, DIL_OUT_WIDTH, D_MODEL), DIL_OUT_WIDTH),
        "w_br_c": nrm(ks[11], (L, DIFF_V_WIDTH, D_MODEL), DIFF_V_WIDTH),
        "w_out": nrm(ks[12], (L, D_MODEL, D_MODEL), D_MODEL),
        "lam_q1": 0.1 * jax.random.normal(ks[13], (L, DIFF_HEAD_DIM), jnp.float32),
        "lam_k1": 0.1 * jax.random.normal(ks[14], (L, DIFF_HEAD_DIM), jnp.float32),
        "lam_q2": 0.1 * jax.random.normal(ks[15], (L, DIFF_HEAD_DIM), jnp.float32),
        "lam_k2": 0.1 * jax.random.normal(ks[16], (L, DIFF_HEAD_DIM), jnp.float32),
        "subln_g": gain(ks[17], (L, DIFF_V_DIM)),
        "rel_bias": 0.5 * jax.random.normal(ks[18], (NUM_BUCKETS, N_BIAS_HEADS), jnp.float32),
        "g_ffn2": gain(ks[19], (L, D_MODEL)),
        "w_ffn2_gate": nrm(ks[20], (L, D_MODEL, D_FF), D_MODEL),
        "w_ffn2_up": nrm(ks[21], (L, D_MODEL, D_FF), D_MODEL),
        "w_ffn2_down": nrm(ks[22], (L, D_FF, D_MODEL), D_FF),
        "g_final": gain(ks[23], (D_MODEL,)),
    }

def first_block(x, g_ffn1, w_ffn1_gate, w_ffn1_up, w_ffn1_down, g_mix, w_in, w_gate, b_gate,
              w_br_a, w_br_b, w_br_c, w_out, lam_q1, lam_k1, lam_q2, lam_k2, subln_g,
              rel_bias, g_ffn2, w_ffn2_gate, w_ffn2_up, w_ffn2_down, g_final):
    Bsz, S, D = x.shape
    c0 = FOURIER_WIDTH
    c1 = c0 + DIL_WIDTH
    c2 = c1 + DIL_WIDTH
    c3 = c2 + DIL_WIDTH
    c4 = c3 + DIFF_QK_WIDTH
    c5 = c4 + DIFF_QK_WIDTH
    for l in range(DEPTH):
        x = x + 0.5 * swiglu(rmsnorm(x, g_ffn1[l]), w_ffn1_gate[l], w_ffn1_up[l], w_ffn1_down[l])

        u = rmsnorm(x, g_mix[l])
        p = u @ w_in[l]
        a_in = p[..., :c0]
        qb, kb, vb = p[..., c0:c1], p[..., c1:c2], p[..., c2:c3]
        qc, kc, vc = p[..., c3:c4], p[..., c4:c5], p[..., c5:]

        y_a = fourier_mix(a_in) @ w_br_a[l]
        y_b = dilated_mixture(qb, kb, vb, rel_bias[:, :DIL_HEADS]) @ w_br_b[l]
        lam_init = 0.8 - 0.6 * math.exp(-0.3 * l)
        lam = (jnp.exp(jnp.sum(lam_q1[l].astype(jnp.float32) * lam_k1[l].astype(jnp.float32)))
               - jnp.exp(jnp.sum(lam_q2[l].astype(jnp.float32) * lam_k2[l].astype(jnp.float32)))
               + lam_init)
        y_c = diff_attention(qc, kc, vc, rel_bias[:, DIL_HEADS:], lam, subln_g[l], lam_init) @ w_br_c[l]

        gates = jax.nn.sigmoid(u @ w_gate[l] + b_gate[l]).reshape(Bsz, S, N_BRANCHES, D)
        merged = gates[:, :, 0] * y_a + gates[:, :, 1] * y_b + gates[:, :, 2] * y_c
        x = x + merged @ w_out[l]

        x = x + 0.5 * swiglu(rmsnorm(x, g_ffn2[l]), w_ffn2_gate[l], w_ffn2_up[l], w_ffn2_down[l])
    return rmsnorm(x, g_final)


DEPTH_2 = 1

MEM_LEN = 256
ATTN_HEADS = 8
ATTN_KV_HEADS = 2
ATTN_HEAD_DIM = 64
ATTN_GROUP = ATTN_HEADS // ATTN_KV_HEADS
WINDOW = 128
ATTN_BLOCK = 128
ROPE_THETA = 10000.0
DN_HEADS = 4
DN_HEAD_K = 128
DN_HEAD_V = 128
DN_CONV = 5
DN_CHUNK = 64
N_DIRS = 2
CROSS_HEADS = 4
CROSS_HEAD_DIM = D_MODEL // CROSS_HEADS
D_FF_2 = -(-8 * D_MODEL // (3 * 256)) * 256
ATTN_WIDTH = ATTN_HEADS * ATTN_HEAD_DIM
DN_WIDTH = DN_HEADS * DN_HEAD_V
MIX_WIDTH = ATTN_WIDTH + DN_WIDTH
DN_QKV = DN_HEADS * (2 * DN_HEAD_K + DN_HEAD_V)
IN_SIZES = [ATTN_WIDTH, ATTN_KV_HEADS * ATTN_HEAD_DIM, ATTN_KV_HEADS * ATTN_HEAD_DIM,
            DN_QKV, DN_WIDTH, N_DIRS * DN_HEADS, N_DIRS * DN_HEADS]
IN_COLS = int(np.sum(IN_SIZES))
IN_SPLITS = [int(v) for v in np.cumsum(IN_SIZES)[:-1]]


def _rms_norm(x, gain):
    xf = x.astype(jnp.float32)
    y = xf * lax.rsqrt(jnp.mean(xf * xf, axis=-1, keepdims=True) + EPS)
    return (y * gain.astype(jnp.float32)).astype(x.dtype)

def _l2norm(x):
    return x * lax.rsqrt(jnp.sum(x * x, axis=-1, keepdims=True) + EPS)

def _rope(x, positions):
    half = x.shape[-1] // 2
    inv_freq = ROPE_THETA ** (-jnp.arange(half, dtype=jnp.float32) / half)
    ang = positions.astype(jnp.float32)[..., None] * inv_freq
    cos = jnp.cos(ang)[:, :, None, :]
    sin = jnp.sin(ang)[:, :, None, :]
    xf = x.astype(jnp.float32)
    x1, x2 = xf[..., :half], xf[..., half:]
    return jnp.concatenate([x1 * cos - x2 * sin, x2 * cos + x1 * sin], axis=-1)

def _window_attention(q, k, v, sink):
    b, s = q.shape[0], q.shape[1]
    nb = s // ATTN_BLOCK
    qb = q.reshape(b, nb, ATTN_BLOCK, ATTN_KV_HEADS, ATTN_GROUP, ATTN_HEAD_DIM)

    def band(t):
        tp = t.reshape(b, nb, ATTN_BLOCK, ATTN_KV_HEADS, ATTN_HEAD_DIM)
        tp = jnp.pad(tp, ((0, 0), (1, 1), (0, 0), (0, 0), (0, 0)))
        return jnp.concatenate([tp[:, :-2], tp[:, 1:-1], tp[:, 2:]], axis=2)

    kw, vw = band(k), band(v)
    scores = jnp.einsum('bnqhgd,bnkhd->bnhgqk', qb, kw) * (ATTN_HEAD_DIM ** -0.5)
    qi = jnp.arange(ATTN_BLOCK)[:, None]
    ki = jnp.arange(3 * ATTN_BLOCK)[None, :]
    in_band = jnp.abs(ki - ATTN_BLOCK - qi) <= WINDOW
    kpos = (jnp.arange(nb)[:, None] - 1) * ATTN_BLOCK + jnp.arange(3 * ATTN_BLOCK)[None, :]
    in_seq = (kpos >= 0) & (kpos < s)
    mask = in_band[None, :, :] & in_seq[:, None, :]
    scores = jnp.where(mask[None, :, None, None], scores, -jnp.inf)
    sk = sink.astype(jnp.float32).reshape(ATTN_KV_HEADS, ATTN_GROUP)[None, None, :, :, None, None]
    m = jnp.maximum(jnp.max(scores, axis=-1, keepdims=True), sk)
    p = jnp.exp(scores - m)
    denom = jnp.sum(p, axis=-1, keepdims=True) + jnp.exp(sk - m)
    o = jnp.einsum('bnhgqk,bnkhd->bnqhgd', p / denom, vw)
    return o.reshape(b, s, ATTN_WIDTH)

def _gated_delta_chunked(q, k, v, g, beta):
    b, h, s, dk = q.shape
    dv = v.shape[-1]
    c = DN_CHUNK
    n = s // c
    q = q.reshape(b, h, n, c, dk)
    k = k.reshape(b, h, n, c, dk)
    v = v.reshape(b, h, n, c, dv)
    g = jnp.cumsum(g.reshape(b, h, n, c), axis=-1)
    beta = beta.reshape(b, h, n, c)
    incl = jnp.tril(jnp.ones((c, c), dtype=bool))
    strict = jnp.tril(jnp.ones((c, c), dtype=bool), k=-1)
    decay = jnp.exp(jnp.where(incl, g[..., :, None] - g[..., None, :], -jnp.inf))
    kb = k * beta[..., None]
    lower = jnp.where(strict, jnp.einsum('bhnid,bhnjd->bhnij', kb, k) * decay, 0.0)
    tmat = lower + jnp.eye(c, dtype=jnp.float32)
    rhs = jnp.concatenate([v * beta[..., None], kb * jnp.exp(g)[..., None]], axis=-1)
    sol = lax.linalg.triangular_solve(tmat, rhs, left_side=True, lower=True, unit_diagonal=True)
    u, w = sol[..., :dv], sol[..., dv:]
    qk = jnp.einsum('bhnid,bhnjd->bhnij', q, k) * decay
    qg = q * jnp.exp(g)[..., None]
    kg = k * jnp.exp(g[..., -1:] - g)[..., None]
    g_last = jnp.exp(g[..., -1])

    def step(state, inp):
        qg_i, kg_i, u_i, w_i, qk_i, gl_i = inp
        v_new = u_i - jnp.einsum('bhck,bhkv->bhcv', w_i, state)
        o_i = jnp.einsum('bhck,bhkv->bhcv', qg_i, state) + jnp.einsum('bhij,bhjv->bhiv', qk_i, v_new)
        state = state * gl_i[..., None, None] + jnp.einsum('bhck,bhcv->bhkv', kg_i, v_new)
        return state, o_i

    xs = tuple(jnp.moveaxis(t, 2, 0) for t in (qg, kg, u, w, qk, g_last))
    state0 = jnp.zeros((b, h, dk, dv), jnp.float32)
    _, o = lax.scan(step, state0, xs)
    return jnp.moveaxis(o, 0, 2).reshape(b, h, s, dv)

def _gated_deltanet(qkv, gate, a, bt, conv_w, a_log, dt_bias, g_out):
    b, s = qkv.shape[0], qkv.shape[1]
    ch = qkv.shape[-1]
    pad = DN_CONV // 2
    conv = lax.conv_general_dilated(qkv, conv_w.reshape(DN_CONV, 1, ch).astype(qkv.dtype),
                                    window_strides=(1,), padding=[(pad, pad)],
                                    dimension_numbers=('NWC', 'WIO', 'NWC'), feature_group_count=ch)
    conv = jax.nn.silu(conv.astype(jnp.float32))
    nq = DN_HEADS * DN_HEAD_K
    q = conv[..., :nq].reshape(b, s, DN_HEADS, DN_HEAD_K)
    k = conv[..., nq:2 * nq].reshape(b, s, DN_HEADS, DN_HEAD_K)
    v = conv[..., 2 * nq:].reshape(b, s, DN_HEADS, DN_HEAD_V)
    q = (_l2norm(q) * (DN_HEAD_K ** -0.5)).transpose(0, 2, 1, 3)
    k = _l2norm(k).transpose(0, 2, 1, 3)
    v = v.transpose(0, 2, 1, 3)
    a = a.astype(jnp.float32).reshape(b, s, N_DIRS, DN_HEADS)
    bt = bt.astype(jnp.float32).reshape(b, s, N_DIRS, DN_HEADS)
    g = -jnp.exp(a_log.astype(jnp.float32)) * jax.nn.softplus(a + dt_bias.astype(jnp.float32))
    g = g.transpose(2, 0, 3, 1)
    beta = jax.nn.sigmoid(bt).transpose(2, 0, 3, 1)
    o_fwd = _gated_delta_chunked(q, k, v, g[0], beta[0])
    flip = lambda t: jnp.flip(t, axis=2)
    o_bwd = flip(_gated_delta_chunked(flip(q), flip(k), flip(v), flip(g[1]), flip(beta[1])))
    o = (o_fwd + o_bwd).transpose(0, 2, 1, 3)
    o = o * lax.rsqrt(jnp.mean(o * o, axis=-1, keepdims=True) + EPS) * g_out.astype(jnp.float32)
    o = o * jax.nn.silu(gate.astype(jnp.float32).reshape(b, s, DN_HEADS, DN_HEAD_V))
    return o.reshape(b, s, DN_WIDTH)

def _memory_cross_attention(h, mem_n, w_q, w_kv, w_o):
    b, s = h.shape[0], h.shape[1]
    m = mem_n.shape[1]
    q = (h @ w_q).reshape(b, s, CROSS_HEADS, CROSS_HEAD_DIM).astype(jnp.float32)
    kv = mem_n @ w_kv
    k = kv[..., :D_MODEL].reshape(b, m, CROSS_HEADS, CROSS_HEAD_DIM).astype(jnp.float32)
    v = kv[..., D_MODEL:].reshape(b, m, CROSS_HEADS, CROSS_HEAD_DIM).astype(jnp.float32)
    p = jax.nn.softmax(jnp.einsum('bqhd,bkhd->bhqk', q, k) * (CROSS_HEAD_DIM ** -0.5), axis=-1)
    o = jnp.einsum('bhqk,bkhd->bqhd', p, v).reshape(b, s, D_MODEL).astype(h.dtype)
    return o @ w_o

def _swiglu(h, w_gate_up, w_down):
    gu = h @ w_gate_up
    return (jax.nn.silu(gu[..., :D_FF_2]) * gu[..., D_FF_2:]) @ w_down

def second_inputs(seed: int = 0) -> dict:
    key = jax.random.key(seed)
    ks = jax.random.split(key, 24)
    f32 = jnp.float32

    def dense(k, fan_in, fan_out):
        return jax.random.normal(k, (DEPTH_2, fan_in, fan_out), f32) * fan_in ** -0.5

    def gain(k, n):
        return 1.0 + 0.02 * jax.random.normal(k, (DEPTH_2, n), f32)

    x = jax.random.normal(ks[0], (BATCH, SEQ, D_MODEL), f32)
    mem = jax.random.normal(ks[1], (BATCH, MEM_LEN, D_MODEL), f32)
    offsets = jax.random.randint(ks[2], (BATCH, 1), 0, 4096, dtype=jnp.int32)
    positions = jnp.arange(SEQ, dtype=jnp.int32)[None, :] + offsets
    dt = jnp.exp(jax.random.uniform(ks[3], (DEPTH_2, N_DIRS, DN_HEADS), f32)
                 * (np.log(0.1) - np.log(0.001)) + np.log(0.001))
    return {
        'x': x,
        'mem': mem,
        'positions': positions,
        'g_mix_pre': gain(ks[4], D_MODEL),
        'w_in': dense(ks[5], D_MODEL, IN_COLS),
        'conv_w': jax.random.normal(ks[6], (DEPTH_2, DN_CONV, DN_QKV), f32) * DN_CONV ** -0.5,
        'a_log': jnp.log(jax.random.uniform(ks[7], (DEPTH_2, N_DIRS, DN_HEADS), f32, 1.0, 16.0)),
        'dt_bias': dt + jnp.log(-jnp.expm1(-dt)),
        'g_dn_out': gain(ks[8], DN_HEAD_V),
        'attn_sink': 0.5 * jax.random.normal(ks[9], (DEPTH_2, ATTN_HEADS), f32),
        'w_out': dense(ks[10], MIX_WIDTH, D_MODEL),
        'g_mix_post': gain(ks[11], D_MODEL),
        'g_cross_pre': gain(ks[12], D_MODEL),
        'g_mem': gain(ks[13], D_MODEL),
        'w_cq': dense(ks[14], D_MODEL, D_MODEL),
        'w_ckv': dense(ks[15], D_MODEL, 2 * D_MODEL),
        'w_co': dense(ks[16], D_MODEL, D_MODEL),
        'g_cross_post': gain(ks[17], D_MODEL),
        'g_ffn_pre': gain(ks[18], D_MODEL),
        'w_gate_up': dense(ks[19], D_MODEL, 2 * D_FF_2),
        'w_down': dense(ks[20], D_FF_2, D_MODEL),
        'g_ffn_post': gain(ks[21], D_MODEL),
    }

def second_block(x, mem, positions, g_mix_pre, w_in, conv_w, a_log, dt_bias, g_dn_out, attn_sink,
              w_out, g_mix_post, g_cross_pre, g_mem, w_cq, w_ckv, w_co, g_cross_post,
              g_ffn_pre, w_gate_up, w_down, g_ffn_post):
    b, s = x.shape[0], x.shape[1]
    for l in range(DEPTH_2):
        h = _rms_norm(x, g_mix_pre[l])
        proj = h @ w_in[l]
        aq, ak, av, dqkv, dgate, dalpha, dbeta = jnp.split(proj, IN_SPLITS, axis=-1)
        aq = _rope(aq.reshape(b, s, ATTN_HEADS, ATTN_HEAD_DIM), positions)
        ak = _rope(ak.reshape(b, s, ATTN_KV_HEADS, ATTN_HEAD_DIM), positions)
        av = av.reshape(b, s, ATTN_KV_HEADS, ATTN_HEAD_DIM).astype(jnp.float32)
        attn_o = _window_attention(aq, ak, av, attn_sink[l]).astype(x.dtype)
        dn_o = _gated_deltanet(dqkv, dgate, dalpha, dbeta, conv_w[l], a_log[l], dt_bias[l],
                               g_dn_out[l]).astype(x.dtype)
        mix = jnp.concatenate([attn_o, dn_o], axis=-1) @ w_out[l]
        x = x + _rms_norm(mix, g_mix_post[l])
        c = _memory_cross_attention(_rms_norm(x, g_cross_pre[l]), _rms_norm(mem, g_mem[l]),
                                    w_cq[l], w_ckv[l], w_co[l])
        x = x + _rms_norm(c, g_cross_post[l])
        f = _swiglu(_rms_norm(x, g_ffn_pre[l]), w_gate_up[l], w_down[l])
        x = x + _rms_norm(f, g_ffn_post[l])
    return x


def setup_inputs(seed=0):
    out = dict(first_inputs(seed))
    for name, value in second_inputs(seed + 1).items():
        if name != "x":
            out[name + "_2"] = value
    return out


def reference(
    x, g_ffn1, w_ffn1_gate, w_ffn1_up, w_ffn1_down, g_mix, w_in, w_gate, b_gate, w_br_a, w_br_b,
    w_br_c, w_out, lam_q1, lam_k1, lam_q2, lam_k2, subln_g, rel_bias, g_ffn2, w_ffn2_gate,
    w_ffn2_up, w_ffn2_down, g_final, mem_2, positions_2, g_mix_pre_2, w_in_2, conv_w_2, a_log_2,
    dt_bias_2, g_dn_out_2, attn_sink_2, w_out_2, g_mix_post_2, g_cross_pre_2, g_mem_2, w_cq_2,
    w_ckv_2, w_co_2, g_cross_post_2, g_ffn_pre_2, w_gate_up_2, w_down_2, g_ffn_post_2,
):
    x = first_block(
        x, g_ffn1, w_ffn1_gate, w_ffn1_up, w_ffn1_down, g_mix, w_in, w_gate, b_gate, w_br_a,
        w_br_b, w_br_c, w_out, lam_q1, lam_k1, lam_q2, lam_k2, subln_g, rel_bias, g_ffn2,
        w_ffn2_gate, w_ffn2_up, w_ffn2_down, g_final,
    )
    return second_block(
        x, mem_2, positions_2, g_mix_pre_2, w_in_2, conv_w_2, a_log_2, dt_bias_2, g_dn_out_2,
        attn_sink_2, w_out_2, g_mix_post_2, g_cross_pre_2, g_mem_2, w_cq_2, w_ckv_2, w_co_2,
        g_cross_post_2, g_ffn_pre_2, w_gate_up_2, w_down_2, g_ffn_post_2,
    )


_drawn_inputs = setup_inputs


def setup_inputs(seed=0):
    import zlib

    import numpy as np

    out = dict(_drawn_inputs(seed))
    spreads = {}
    factors = {'b_gate': 7.071,
     'g_dn_out_2': 4.432,
     'attn_sink_2': 8.0,
     'g_mix_post_2': 3.453,
     'g_cross_pre_2': 4.494,
     'g_mem_2': 2.917,
     'g_cross_post_2': 13.168,
     'g_ffn_pre_2': 11.047,
     'g_ffn_post_2': 22.847}
    for name, (base, spread) in spreads.items():
        noise = np.random.default_rng([zlib.crc32(name.encode()), seed]).standard_normal(out[name].shape)
        drawn = base * np.exp(spread * noise) if base else spread * noise
        out[name] = __import__('jax').numpy.asarray(drawn.astype(out[name].dtype))
    for name, factor in factors.items():
        out[name] = (out[name] * factor).astype(out[name].dtype)
    return out
```

```python
from contextlib import ExitStack, contextmanager

import numpy as np

import concourse.bass as bass
from concourse import mybir

F32 = mybir.dt.float32
F32R = mybir.dt.float32r
I32 = mybir.dt.int32
ALU = mybir.AluOpType
ACT = mybir.ActivationFunctionType
AX = mybir.AxisListType
ds = bass.ds

P = 128
S = 512
D = 1024
KT = D // P
LAYERS = 2
FF_PARTS = (8, 8, 6)
EPS = 1e-6


def tile(t, k, n=S):
    if isinstance(k, int):
        return t[:, k, 0:n]
    return t[:, ds(k, 1), 0:n].rearrange("p o n -> p (o n)")


class Count:

    def __init__(self, first, carrier=None):
        self.first = first
        self.carrier = carrier
        self.n = {}
        self.loops = []

    def now(self, key):
        value = self.n.get(key, self.first.get(key, 0))
        for reg, per in self.loops:
            if per.get(key, 0):
                value = reg * per[key] + value
        return value

    def up(self, key, by=1):
        self.n[key] = self.n.get(key, self.first.get(key, 0)) + by
        return by

    def next(self, key, by=1):
        self.up(key, by)
        return self.now(key)

    def take(self, key):
        value = self.now(key)
        self.up(key)
        return value

    @contextmanager
    def loop(self, eng, n, per):
        start = dict(self.n)
        if self.loops and self.carrier:
            eng.sem_inc(self.carrier, 1)
        with eng.Fori(0, n) as i:
            self.loops.append((i, per))
            yield i
            self.loops.pop()
        got = {k: v - start.get(k, self.first.get(k, 0)) for k, v in self.n.items()}
        got = {k: v for k, v in got.items() if v}
        assert got == {k: v for k, v in per.items() if v}, ("a loop's counts are", got, per)
        for k, v in got.items():
            self.n[k] += (n - 1) * v


LAYER_COLS = {"g_mix": 0, "g_ffn2": 8, "g_next": 16, "b_gate": 24, "subln": 48, "neg_lam": 49, "one_less": 50, "lam_init": 51}
LC = 52
TAIL = {n: 2 * LC + 8 * i for i, n in enumerate(
    ["g_first", "g_mix_pre", "g_mix_post", "g_cross_pre", "g_mem", "g_cross_post", "g_ffn_pre", "g_ffn_post"])}
EXTRA = 2 * LC + 8 * len(TAIL)
SINK, CONV, G_OUT, A_LOG, DT_BIAS, INV_FREQ, FORWARD, NSMALL = (EXTRA + n for n in (0, 8, 68, 69, 70, 71, 72, 74))
DN_TILES = 12
ROUND = 1.5 * 2 ** 23
NEAR_PI = 3.1415925
UT_BEFORE = 7 * LAYERS + 4
TWO_PI = (6.28125, 1.93500518798828125e-3, 3.0199159819567e-7)


HALF = S // 2 + 1
DFT_COLS = 2 * P + 2 * 4 * HALF
BIAS_N = [896] * 4 + [256] * 2 + [128] * 4
BIAS_AT = [sum(BIAS_N[:i]) for i in range(10)]
BIAS_COLS = sum(BIAS_N)
VEC = {0: (0, 1024), 1: (1024, 384), 2: (1408, 256), 3: (1664, 256)}
VEC_COLS = 1920
HEAD_OF = [6, 7, 8, 9, 0, 1, 2, 3, 4, 5]
KIND_OF = [0, 0, 0, 0, 1, 1, 2, 2, 3, 3]


PER = {
    "pe": {
        "u": 24, "lo0": 107, "evac0": 107, "acc": 24, "stat": 3, "job0": 107, "lo1": 107, "evac1": 107, "job1": 107, "m": 65,
        "tab": 32, "z_act": 8, "z_full": 16, "z_dve": 8, "y_done": 8, "pq": 8, "vt_done": 7, "vt_full": 7, "sc_free": 22,
        "sc_full": 22, "exp": 22, "tr_copied": 22, "tr_full": 22, "pv_copied": 19, "pv_full": 19, "ut_copied": 7,
        "ut_full": 7, "total": 6, "rows_copied": 6, "rows_full": 6, "mixw": 1, "wb_free": 3, "wb_full": 3, "prob": 16,
        "oT_done": 4,
    },
    "act": {
        "square": 24, "u_hi": 24, "raw0": 1712, "slot0": 107, "raw1": 1712, "slot1": 107, "stat": 3, "std": 4, "evac0": 107,
        "silu": 68, "job0": 107, "h": 61, "m_hi": 65, "job1": 107, "evac1": 107, "m": 65, "tab": 32, "z_full": 16, "z_act": 8,
        "pq": 8, "q_copied": 8, "max": 23, "exp": 22, "tr_full": 22, "tr_copied": 22, "pv_full": 19, "pv_copied": 19,
        "ut_full": 7, "ut_copied": 7, "rows_full": 6, "rows_copied": 6, "mixw": 1,
    },
    "dve": {
        "dve": 94, "square": 24, "acc": 24, "u_hi": 24, "u": 24, "std": 4, "job0": 107, "evac0": 107, "job1": 107,
        "evac1": 107, "silu": 68, "h": 61, "m_hi": 65, "m": 65, "z_full": 16, "z_dve": 8, "q_copied": 8, "pq": 8, "y_done": 8,
        "tab": 32, "vt_full": 7, "vt_done": 7, "sc_full": 22, "sc_free": 22, "max": 23, "exp": 22, "total": 6, "tr_full": 22,
        "rows": 6, "mixe": 1, "mixw": 1, "wb_full": 3, "wb_free": 3, "prob": 16, "oT_done": 4, "pv_full": 19,
    },
}


def bucket(rel):
    n = np.abs(rel)
    far = np.floor(8 + np.log(np.maximum(n, 1) / 8) / np.log(1024 / 8) * 8).astype(int)
    return np.where(rel > 0, 16, 0) + np.where(n < 8, n, np.minimum(far, 15))


def constants():
    c = {}
    k, n = np.arange(P), np.arange(S)
    a = 2 * np.pi * (k[:, None] * k[None, :] % P) / P
    t = 2 * np.pi * (n[:, None] * np.arange(HALF)[None, :] % S) / S
    tok = lambda m: m.reshape(4, P, HALF).transpose(1, 0, 2).reshape(P, -1)
    c["dft"] = np.concatenate([np.cos(a) / 256, np.sin(a) / 256, tok(np.cos(t)), tok(np.sin(t))], 1)
    hot = np.zeros((33, VEC_COLS))
    for kind, (at, size) in VEC.items():
        i = np.arange(size)
        rel, ok = ((i - 511, i < 1023), (i - 191, abs(i - 191) <= 64), (4 * (i - 127), abs(i - 127) <= 64),
                   (4 * (i - 127), (i - 127) % 4 == 0))[kind]
        hot[bucket(rel), at + i] = ok
        hot[32, at + i] = np.where(ok, 0, -1e30)
    c["hot"] = hot
    c["eye"] = np.concatenate([np.eye(P), np.eye(P)[::-1]], 1)
    sel = np.zeros((2, P))
    sel[0, :64] = sel[1, 64:] = 1
    c["sel"] = sel
    w = np.arange(3 * P)
    c["window"] = np.where(abs(w[None, :] - P - k[:, None]) <= P, 0, -1e30)
    i, j = k[:, None], k[None, :]
    incl = np.where(j >= i, 0, -1e30)
    level = [(i // (2 * b) == j // (2 * b)) & (i % (2 * b) >= b) & (j % (2 * b) < b) for b in (1, 2, 4, 8, 16, 32, 64)]
    c["chunk"] = np.concatenate(level + [m.T for m in level] + [incl, incl.T], 1)
    swap = np.zeros((P, P))
    for m in range(P):
        swap[m + 32 if m % 64 < 32 else m - 32, m] = -1 if m % 64 < 32 else 1
    c["swap"] = swap
    rows = np.zeros((8, 8 * P))
    for r in range(8):
        rows[r, r * P:r * P + P] = 1
    c["rows8"] = rows
    return {n: v.astype(np.float32) for n, v in c.items()}


def column_major(v):
    return v.reshape(-1, P).T


def weight_jobs(w):
    k, m = w.shape
    out = np.zeros((m // P, P, KT * P), np.float32)
    out[:, :, :k] = w.reshape(k // P, P, m // P, P).transpose(2, 1, 0, 3).reshape(m // P, P, k)
    return out


def ffn_jobs(gate, up, down):
    out, f0 = [], 0
    for n in FF_PARTS:
        cols = slice(f0 * P, (f0 + n) * P)
        pair = np.stack([weight_jobs(gate[:, cols]), weight_jobs(up[:, cols])], 1)
        out += [pair.reshape(-1, P, D), weight_jobs(down[cols])]
        f0 += n
    return out


def build(nc, jobs, x_in, small_in, mem_in, pos_in, rel_in, lam_in, dft_in, hot_in, eye_in, sel_in,
          window_in, chunk_in, swap_in, rows8_in, out):
    NJ = jobs.shape[0]
    with ExitStack() as ctx:
        def sb(name, shape, dt=F32):
            return ctx.enter_context(nc.sbuf_tensor(name, shape, dt))

        def sem(name):
            return ctx.enter_context(nc.semaphore(name))

        raw = sb("raw", [P, 2, KT * P])
        w_hi = sb("w_hi", [P, 2, KT * P], F32R)
        w_lo = sb("w_lo", [P, 2, KT * P], F32R)
        x = sb("x", [P, KT, S])
        u_hi = sb("u_hi", [P, KT, S], F32R)
        u_lo = sb("u_lo", [P, KT, S], F32R)
        m_hi = sb("m_hi", [P, KT, S], F32R)
        m_lo = sb("m_lo", [P, KT, S], F32R)
        T = sb("T", [P, 8, S])
        gr, sg, ur, hf, xsq, acc, std = (T[:, i] for i in range(7))
        rs = sb("rs", [P, S])
        ones = sb("ones", [P, P])
        pt = sb("pt", [P, 30, S])
        tab = sb("tab", [P, BIAS_COLS])
        eye = sb("eye", [P, 2 * P])
        stats = sb("stats", [P, 416])
        rs_mem = sb("rs_mem", [P, 256])
        sel = sb("sel", [2, P])
        vec_dram = nc.dram_tensor("vec_dram", (10, VEC_COLS), F32, kind="Internal").ap()
        bias_dram = nc.dram_tensor("bias_dram", (P, BIAS_COLS), F32, kind="Internal").ap()
        small = sb("small", [P, NSMALL])
        par = sb("par", [P, LC])
        eps = sb("eps", [P, 3])
        ps = [ctx.enter_context(nc.psum_tensor(f"ps{i}", [P, S], F32)) for i in range(8)]

        raw_full = [sem(f"raw_full{i}") for i in range(2)]
        hi_done = [sem(f"hi_done{i}") for i in range(2)]
        lo_done = [sem(f"lo_done{i}") for i in range(2)]
        job_done = [sem(f"job_done{i}") for i in range(2)]
        evac = [sem(f"evac{i}") for i in range(2)]
        names = """loaded setup_in par_ready vec_ready vec_stored hankel_in bias_made bias_stored tab_full
            silu_done h_done m_hi_done m_ready square_done acc_step u_hi_done u_ready stat_done std_done
            dve_step act_step out_done z_full z_act z_dve pq_full q_copied y_done vt_full vt_done sc_full sc_free
            max_done exp_done prob_done tr_full tr_copied pv_full pv_copied ut_full ut_copied
            rows_full rows_copied mixw_exp mixw_done wb_full wb_free oT_full oT_done total_done
            x_done tab2_in rope_full rope_done conv_done conv_silu rows_step kq_ready bc_full chunk_mm0 chunk_mm1
            angles_ready tables_ready tab3_in row_terms row_exps chunk_terms0 chunk_terms1
            chunk_dve0 chunk_dve1 chunk_act0 chunk_act1 dn_full dn_copied vm_full vm_done inner_loops"""
        (loaded, setup_in, par_ready, vec_ready, vec_stored, hankel_in, bias_made, bias_stored, tab_full,
         silu_done, h_done, m_hi_done, m_ready, square_done, acc_step, u_hi_done, u_ready, stat_done, std_done,
         dve_step, act_step, out_done, z_full, z_act, z_dve, pq_full, q_copied, y_done, vt_full, vt_done, sc_full, sc_free,
         max_done, exp_done, prob_done, tr_full, tr_copied, pv_full, pv_copied, ut_full, ut_copied,
         rows_full, rows_copied, mixw_exp, mixw_done, wb_full, wb_free, oT_full, oT_done, total_done,
         x_done, tab2_in, rope_full, rope_done, conv_done, conv_silu, rows_step, kq_ready, bc_full, chunk_mm0, chunk_mm1,
         angles_ready, tables_ready, tab3_in, row_terms, row_exps, chunk_terms0, chunk_terms1,
         chunk_dve0, chunk_dve1, chunk_act0, chunk_act1, dn_full, dn_copied, vm_full, vm_done, inner_loops) = [sem(n) for n in names.split()]
        FIRST = {k + str(i): 1 for k in ("job", "slot", "evac", "lo") for i in range(2)}
        FIRST |= {k: 1 for k in ("z_act", "z_dve", "q_copied", "y_done", "vt_done", "sc_free", "tr_copied", "pv_copied",
                                 "ut_copied", "rows_copied", "wb_free", "oT_done", "rope_done", "dn_copied", "vm_done")}
        JOB = {f"{k}{s}": 1 for k in ("job", "evac") for s in range(2)}
        PJOB = {**JOB, "lo0": 1, "lo1": 1}
        AJOB = {**JOB, "raw0": 16, "raw1": 16, "slot0": 1, "slot1": 1}
        flat = pt[:, :, :].rearrange("p a n -> p (a n)")
        ident = eye[:, 0:P]
        QB, KB, VB, QC, KC, VC = 8, 11, 14, 17, 21, 25
        OC = 8
        YB, YC = 8, 16
        dft_c, dft_s = tab[:, 0:P], tab[:, P:2 * P]
        dft_cs = tab[:, 0:2 * P]
        cos_t = tab[:, 2 * P:2 * P + 4 * HALF].rearrange("p (t n) -> p t n", t=4)
        sin_t = tab[:, 2 * P + 4 * HALF:DFT_COLS].rearrange("p (t n) -> p t n", t=4)
        nmax = stats[:, 0:24].rearrange("p (g t h) -> p g t h", g=3, t=4)
        total = stats[:, 24:48].rearrange("p (g t h) -> p g t h", g=3, t=4)
        rows_m = flat[0:2, KB * S:(KB + 3) * S].rearrange("p (g n) -> p g n", g=3)
        rows_z = flat[0:2, VB * S:(VB + 3) * S].rearrange("p (g n) -> p g n", g=3)
        hot = flat[0:33, 0:VEC_COLS]
        relb = pt[0:33, 4, 0:10]
        lamv = pt[0:64, 5, 0:8]
        lamp = pt[0:64, 6, 0:4]
        vec_sb = flat[0:10, 18 * S:18 * S + VEC_COLS]
        hankel = flat[:, 8 * S:8 * S + BIAS_COLS]

        def tokens(r, row):
            return row.rearrange("p (i c) -> p c i", c=4)[:, r]

        def natural(g, row):
            return row if g == 0 else row.rearrange("p (i c) -> p c i", c=4)

        def grouped(g, row):
            return row if g == 0 else row.rearrange("p (c i) -> p c i", c=4)

        AQ, AK, AV, DQ, DK, DV, DG, AB, AO = 0, 4, 5, 6, 10, 14, 18, 22, 24
        tabt = tab[:, :].rearrange("p (a n) -> p a n", n=S)
        memt = tabt[:, 0:4].rearrange("p a n -> p (a n)").rearrange("p (k n) -> p k n", k=KT)
        cos, sin = tabt[:, 4], tabt[:, 5]
        pos_i = tabt[:, 6].bitcast(I32)
        window = tabt[:, 7, 0:3 * P]
        swap = tabt[:, 8, 0:P]
        ktok = tabt[:, 0:4]
        chunk = tabt[:, 4:8].rearrange("p a n -> p (a n)")
        rows8 = pt[0:8, 28:30].rearrange("p a n -> p (a n)")
        neg_sink = stats[:, 400:408]
        gcol = stats[:, 96:128].rearrange("p (c r) -> p c r", c=4)
        bcol = stats[:, 128:192].rearrange("p (c r) -> p c r", c=4)
        beg = stats[:, 192:224].rearrange("p (c r) -> p c r", c=4)
        kgf = [stats[:, 224 + 8 * d:228 + 8 * d] for d in range(2)]
        glast = [stats[:, 228 + 8 * d:232 + 8 * d] for d in range(2)]
        LANE = [[T[:, i] for i in range(7)], [pt[:, i] for i in range(6)] + [pt[:, 23]]]
        chunk_terms = (chunk_terms0, chunk_terms1)
        chunk_mm, chunk_dve, chunk_act = (chunk_mm0, chunk_mm1), (chunk_dve0, chunk_dve1), (chunk_act0, chunk_act1)

        g_rows = pt[0:8, AB]
        STAGES = 18
        X_DONE = 3 * KT

        def vm(f, t):
            i, j = f // 2, (f % 2) * 2 + t
            return pt[:, 24 + i, j * P:j * P + P]

        def window_keys(r):
            return (min(r + 2, 4) - max(r - 1, 0)) * P

        def four(t):
            return t.rearrange("p (h n) -> p h n", h=4)

        def level_mask(d, m):
            return chunk[:, (7 * d + m) * P:(7 * d + m) * P + P]

        def incl_mask(d):
            return chunk[:, (14 + d) * P:(15 + d) * P]

        block = ctx.enter_context(nc.Block())

        @block.sync
        def _(sp):
            sp.dma_start(x[:, :, :], x_in).then_inc(loaded, 16)
            sp.dma_start(small[:, :], small_in).then_inc(loaded, 16)
            with sp.Fori(0, NJ // 2) as i:
                for s in range(2):
                    sp.wait_ge(lo_done[s], i + 1)
                    sp.dma_start(raw[:, s], jobs[ds(i * 2 + s, 1)].rearrange("o p n -> p (o n)")).then_inc(raw_full[s], 16)
            if NJ % 2:
                sp.wait_ge(lo_done[0], NJ // 2 + 1)
                sp.dma_start(raw[:, 0], jobs[NJ - 1]).then_inc(raw_full[0], 16)
            for k in range(KT):
                sp.wait_ge(x_done, X_DONE + k + 1)
                sp.dma_start(out[:, k], x[:, k]).then_inc(out_done, 16)
            sp.wait_ge(out_done, 16 * KT)

        @block.gpsimd
        def _(pool):
            for s in range(2):
                pool.sem_inc(lo_done[s], 1)
            with pool.Fori(0, NJ // 2) as i:
                for s in range(2):
                    pool.wait_ge(hi_done[s], i + 1)
                    pool.tensor_tensor(w_lo[:, s], raw[:, s], w_hi[:, s].bitcast(F32), ALU.subtract).then_inc(lo_done[s], 1)
            if NJ % 2:
                pool.wait_ge(hi_done[0], NJ // 2 + 1)
                pool.tensor_tensor(w_lo[:, 0], raw[:, 0], w_hi[:, 0].bitcast(F32), ALU.subtract).then_inc(lo_done[0], 1)

        @block.tensor
        def _(pe):
            c = Count(FIRST)
            for s in range(2):
                pe.sem_inc(job_done[s], 1)

            def job(s, hi, lo, ks=range(KT), ready=None, n=S, stat=False):
                pe.wait_ge(lo_done[s], c.next(f"lo{s}"))
                pe.wait_ge(evac[s], c.take(f"evac{s}"))
                product(s, s, hi, lo, ks, ready, n, stat).then_inc(job_done[s], c.up(f"job{s}"))

            def product(s, bank, hi, lo, ks, ready=None, n=S, stat=False):
                for k in ks:
                    if ready:
                        pe.wait_ge(ready[0], ready[1] + (k + 1))
                    w = slice(k * P, k * P + P)
                    pe.matmul(ps[bank][:, 0:n], w_hi[:, s, w], hi[:, k, 0:n], start=k == ks[0], stop=False)
                    pe.matmul(ps[bank][:, 0:n], w_lo[:, s, w], hi[:, k, 0:n], start=False, stop=False)
                    last = pe.matmul(ps[bank][:, 0:n], w_hi[:, s, w], lo[:, k, 0:n], start=False, stop=k == ks[-1])
                    if stat and k == 3:
                        statistic(n)
                return last

            def statistic(n=S):
                pe.wait_ge(acc_step, c.next("acc", 8))
                pe.matmul(ps[7][:, 0:n], ones[:, :], acc[:, 0:n], start=True, stop=True).then_inc(stat_done, c.up("stat"))

            def ffn():
                ready = (u_ready, c.now("u"))
                c.up("u", 8)
                for part, n in enumerate(FF_PARTS):
                    if part == 0:
                        job(0, u_hi, u_lo, ready=ready, stat=True)
                        job(1, u_hi, u_lo)
                    with c.loop(pe, n - (part == 0), PJOB):
                        job(0, u_hi, u_lo)
                        job(1, u_hi, u_lo)
                    with c.loop(pe, 4, PJOB):
                        job(0, m_hi, m_lo, range(n), ready=(m_ready, c.now("m")))
                        job(1, m_hi, m_lo, range(n))
                    c.up("m", n)

            def fourier():
                def along_channels(g):
                    for half in range(2):
                        free = z_act if half == 0 else z_dve
                        pe.wait_ge(free, c.take("z_act" if half == 0 else "z_dve"))
                        for t in (2 * half, 2 * half + 1):
                            mm = pe.matmul(ps[2 + half][:, (t % 2) * 256:(t % 2) * 256 + 256], pt[:, g, t * P:t * P + P],
                                           dft_cs, start=True, stop=True)
                        mm.then_inc(z_full, c.up("z_full"))

                pe.wait_ge(tab_full, c.next("tab", 16))
                c.up("tab", 16)
                along_channels(0)
                for g in range(8):
                    if g < 7:
                        along_channels(g + 1)
                    z = T[:, 2 * (g % 2):2 * (g % 2) + 2].rearrange("p a n -> p (a n)").rearrange("p (t n) -> p t n", t=4)
                    pe.wait_ge(z_act, c.now("z_act") - (1 if g < 7 else 0))
                    pe.wait_ge(z_dve, c.now("z_dve") - (1 if g < 7 else 0))
                    pe.wait_ge(y_done, c.take("y_done"))
                    for t in range(4):
                        pe.matmul(ps[4][:, 0:HALF], z[:, t, 0:P], cos_t[:, t], start=t == 0, stop=t == 3)
                    for t in range(4):
                        mm = pe.matmul(ps[5][:, 0:HALF], z[:, t, P:2 * P], sin_t[:, t], start=t == 0, stop=t == 3)
                    mm.then_inc(pq_full, c.up("pq"))

            def v_tiles(g):
                pe.wait_ge(vt_done, c.take("vt_done"))
                for r in range(4):
                    src = flat[:, (VB * S - 64 + r * P):(VB * S + 64 + r * P)] if g == 0 else tokens(r, pt[:, VB + g])
                    mm = pe.transpose(ps[5][:, r * P:r * P + P], src, ident)
                if g == 0:
                    mm = pe.transpose(ps[6][:, 0:P], flat[:, VB * S + 448:VB * S + 576], ident)
                mm.then_inc(vt_full, c.up("vt_full"))

            def dilated(g):
                v_tiles(g)
                v = pt[:, VB + g].rearrange("p (t n) -> p t n", t=4)
                for h in range(2):
                    hp = slice(64 * h, 64 * h + 64)
                    pe.wait_ge(sc_free, c.take("sc_free"))
                    for r in range(4):
                        q, k = pt[hp, QB + g], pt[hp, KB + g]
                        if g == 0:
                            a, b = max(r * P - 64, 0), min(r * P + 192, S)
                            o = (r % 2) * 256 + a - (r * P - 64)
                            mm = pe.matmul(ps[2 + r // 2][:, o:o + b - a], q[:, r * P:r * P + P], k[:, a:b], start=True, stop=True)
                        else:
                            mm = pe.matmul(ps[2][:, r * P:r * P + P], tokens(r, q), tokens(r, k), start=True, stop=True)
                    mm.then_inc(sc_full, c.up("sc_full"))
                    pe.wait_ge(exp_done, c.next("exp"))
                    pe.wait_ge(tr_copied, c.take("tr_copied"))
                    e = T[:, 0:2].rearrange("p a n -> p (a n)")
                    if g == 0:
                        for r in range(4):
                            for half in range(2):
                                a = r * 256 + half * P
                                mm = pe.transpose(ps[(4, 6)[half]][:, r * P:r * P + P], e[:, a:a + P], ident)
                    else:
                        for r in range(4):
                            mm = pe.transpose(ps[4][:, r * P:r * P + P], e[:, r * P:r * P + P], ident)
                    mm.then_inc(tr_full, c.up("tr_full"))
                    pe.wait_ge(tr_copied, c.now("tr_copied"))
                    if h == 0:
                        pe.wait_ge(vt_done, c.now("vt_done"))
                        pe.wait_ge(pv_copied, c.take("pv_copied"))
                    for r in range(4):
                        o = ps[5][:, r * P + 64 * h:r * P + 64 * h + 64]
                        vh = slice(64 * h, 64 * h + 64)
                        if g == 0:
                            after = v[:, r + 1, vh] if r < 3 else pt[:, 29, vh]
                            pe.matmul(o, T[:, 2, r * P:r * P + P], v[:, r, vh], start=True, stop=False)
                            mm = pe.matmul(o, T[:, 3, r * P:r * P + P], after, start=False, stop=True)
                        else:
                            mm = pe.matmul(o, T[:, 2, r * P:r * P + P], v[:, r, vh], start=True, stop=True)
                mm.then_inc(pv_full, c.up("pv_full"))
                pe.wait_ge(pv_copied, c.now("pv_copied"))
                pe.wait_ge(ut_copied, c.take("ut_copied"))
                for r in range(4):
                    mm = pe.transpose(ps[7][:, r * P:r * P + P], T[:, 4, r * P:r * P + P], ident)
                mm.then_inc(ut_full, c.up("ut_full"))

            def dilated_rows():
                pe.wait_ge(total_done, c.next("total", 6))
                for stat_of in (nmax, total):
                    for g in range(3):
                        pe.wait_ge(rows_copied, c.take("rows_copied"))
                        for r in range(4):
                            mm = pe.transpose(ps[2][0:2, r * P:r * P + P], stat_of[:, g, r], ident)
                        mm.then_inc(rows_full, c.up("rows_full"))
                pe.wait_ge(mixw_done, c.next("mixw"))
                for g in range(3):
                    pe.wait_ge(wb_free, c.take("wb_free"))
                    pe.matmul(ps[3][:, :], sel[:, :], rows_m[:, g], start=True, stop=True).then_inc(wb_full, c.up("wb_full"))

            def dense():
                c.up("exp", 16)
                for h in range(4):
                    pe.wait_ge(vt_done, c.take("vt_done"))
                    for r in range(4):
                        mm = pe.transpose(ps[6][:, r * P:r * P + P], pt[:, VC + h, r * P:r * P + P], ident)
                    mm.then_inc(vt_full, c.up("vt_full"))
                pe.wait_ge(vt_done, c.now("vt_done"))

                def scores(u):
                    h, r = divmod(u, 4)
                    pe.wait_ge(sc_free, c.take("sc_free"))
                    for m in range(2):
                        hp = slice(64 * m, 64 * m + 64)
                        mm = pe.matmul(ps[2 + m][:, :], pt[hp, QC + h, r * P:r * P + P], pt[hp, KC + h], start=True, stop=True)
                    mm.then_inc(sc_full, c.up("sc_full"))

                scores(0)
                for u in range(16):
                    if u < 15:
                        scores(u + 1)
                    h = u // 4
                    pe.wait_ge(prob_done, c.next("prob"))
                    pe.wait_ge(tr_copied, c.take("tr_copied"))
                    for k in range(4):
                        mm = pe.transpose(ps[4][:, k * P:k * P + P], T[:, 2 * (u % 2) + 1, k * P:k * P + P], ident)
                    mm.then_inc(tr_full, c.up("tr_full"))
                    pe.wait_ge(tr_copied, c.now("tr_copied"))
                    pe.wait_ge(pv_copied, c.take("pv_copied"))
                    v = pt[:, VC + h].rearrange("p (t n) -> p t n", t=4)
                    for k in range(4):
                        mm = pe.matmul(ps[5][:, 0:P], T[:, 4 + u % 2, k * P:k * P + P], v[:, k], start=k == 0, stop=k == 3)
                    mm.then_inc(pv_full, c.up("pv_full"))
                for h in range(4):
                    if h == 0:
                        pe.wait_ge(oT_done, c.now("oT_done") + 4)
                        c.up("oT_done", 4)
                    pe.wait_ge(ut_copied, c.take("ut_copied"))
                    for r in range(4):
                        mm = pe.transpose(ps[7][:, r * P:r * P + P], pt[:, OC + h, r * P:r * P + P], ident)
                    mm.then_inc(ut_full, c.up("ut_full"))

            def mixers():
                ready = (u_ready, c.now("u"))
                c.up("u", 8)
                job(0, u_hi, u_lo, ready=ready, stat=True)
                job(1, u_hi, u_lo)
                with c.loop(pe, 13, PJOB):
                    job(0, u_hi, u_lo)
                    job(1, u_hi, u_lo)
                job(0, u_hi, u_lo)
                job(1, u_hi, u_lo, range(1))
                pe.wait_ge(evac[0], c.now("evac0"))
                pe.wait_ge(evac[1], c.now("evac1"))
                fourier()
                with c.loop(pe, 8, PJOB):
                    job(0, u_hi, u_lo)
                    job(1, m_hi, m_lo, ready=(m_ready, c.now("m")))
                c.up("m", 8)
                for g in range(3):
                    dilated(g)
                dilated_rows()
                dense()
                with c.loop(pe, 4, PJOB):
                    for s in range(2):
                        pe.wait_ge(lo_done[s], c.next(f"lo{s}"))
                        pe.wait_ge(evac[s], c.take(f"evac{s}"))
                        if s == 0:
                            pe.wait_ge(m_ready, c.now("m") + 5)
                        product(s, 2 + s, m_hi, m_lo, range(1))
                        product(s, s, m_hi, m_lo, range(1, 5)).then_inc(job_done[s], c.up(f"job{s}"))
                c.up("m", 5)
                with c.loop(pe, 8, PJOB):
                    job(0, u_hi, u_lo)
                    job(1, u_hi, u_lo)
                with c.loop(pe, 4, PJOB):
                    job(0, m_hi, m_lo, ready=(m_ready, c.now("m")))
                    job(1, m_hi, m_lo)
                c.up("m", 8)

            def second():
                c.up("u", 8)
                statistic()
                ready = (u_ready, c.now("u"))
                c.up("u", 8)
                job(0, u_hi, u_lo, ready=ready, stat=True)
                job(1, u_hi, u_lo)
                with c.loop(pe, 10, PJOB):
                    job(0, u_hi, u_lo)
                    job(1, u_hi, u_lo)
                job(0, u_hi, u_lo)
                job(1, u_hi, u_lo, range(1))
                for s in range(2):
                    pe.wait_ge(evac[s], c.now(f"evac{s}"))
                statistic(256)
                window_attention()
                delta_net()
                m0 = c.now("m")
                c.up("m", 8)
                job(0, m_hi, m_lo, ready=(m_ready, m0))
                job(1, m_hi, m_lo)
                with c.loop(pe, 3, PJOB):
                    job(0, m_hi, m_lo)
                    job(1, m_hi, m_lo)
                pe.wait_ge(u_ready, c.next("u", 8))
                job(0, u_hi, u_lo, n=256)
                job(1, u_hi, u_lo, n=256)
                statistic()
                with c.loop(pe, 7, PJOB):
                    job(0, u_hi, u_lo, n=256)
                    job(1, u_hi, u_lo, n=256)
                m0 = c.now("m")
                c.up("m", 8)
                job(0, m_hi, m_lo, ready=(m_ready, m0), stat=True)
                job(1, m_hi, m_lo)
                with c.loop(pe, 3, PJOB):
                    job(0, m_hi, m_lo)
                    job(1, m_hi, m_lo)
                for s in range(2):
                    pe.wait_ge(evac[s], c.now(f"evac{s}"))
                cross()
                u0 = c.now("u")
                c.up("u", 8)
                job(0, u_hi, u_lo, ready=(u_ready, u0))
                job(1, u_hi, u_lo)
                with c.loop(pe, 3, PJOB):
                    job(0, u_hi, u_lo)
                    job(1, u_hi, u_lo)
                statistic()
                ffn()
                statistic()

            def window_attention():
                pe.wait_ge(tab2_in, 80)
                for i in range(5):
                    pe.wait_ge(rope_done, c.take("rope_done"))
                    pe.matmul(ps[2][:, :], swap, pt[:, i], start=True, stop=True).then_inc(rope_full, c.up("rope_full"))
                pe.wait_ge(vt_done, c.take("vt_done"))
                for r in range(4):
                    mm = pe.transpose(ps[6][:, r * P:r * P + P], pt[:, AV, r * P:r * P + P], ident)
                mm.then_inc(vt_full, c.up("vt_full"))
                pe.wait_ge(vt_done, c.now("vt_done"))
                pe.wait_ge(rope_done, c.now("rope_done"))
                v = four(pt[:, AV])

                def scores(u):
                    j, r = divmod(u, 4)
                    pe.wait_ge(sc_free, c.take("sc_free"))
                    lo, hi = max(r - 1, 0) * P, min(r + 2, 4) * P
                    for m in range(2):
                        hp = slice(64 * m, 64 * m + 64)
                        mm = pe.matmul(ps[2 + m][:, 0:hi - lo], pt[hp, AQ + j, r * P:r * P + P], pt[hp, AK, lo:hi], start=True, stop=True)
                    mm.then_inc(sc_full, c.up("sc_full"))

                scores(0)
                for u in range(16):
                    if u < 15:
                        scores(u + 1)
                    r = u % 4
                    keys = range(max(r - 1, 0), min(r + 2, 4))
                    pe.wait_ge(exp_done, c.next("exp"))
                    pe.wait_ge(tr_copied, c.take("tr_copied"))
                    for m in range(2):
                        for n in range(len(keys)):
                            mm = pe.transpose(ps[4 + 2 * m][:, n * P:n * P + P], T[:, 2 * (u % 2) + m, n * P:n * P + P], ident)
                    mm.then_inc(tr_full, c.up("tr_full"))
                    pe.wait_ge(tr_copied, c.now("tr_copied"))
                    pe.wait_ge(pv_copied, c.take("pv_copied"))
                    for m in range(2):
                        for n, k in enumerate(keys):
                            mm = pe.matmul(ps[5][:, 64 * m:64 * m + 64], T[:, 4 + m, n * P:n * P + P], v[:, k, 64 * m:64 * m + 64],
                                           start=n == 0, stop=n == len(keys) - 1)
                    mm.then_inc(pv_full, c.up("pv_full"))
                for f in range(4):
                    pe.wait_ge(ut_copied, c.take("ut_copied"))
                    if f == 0:
                        pe.wait_ge(pv_copied, c.now("pv_copied"))
                    for r in range(4):
                        mm = pe.transpose(ps[7][:, r * P:r * P + P], pt[:, AO + r, f * P:f * P + P], ident)
                    mm.then_inc(ut_full, c.up("ut_full"))

            def delta_net():
                for i in range(8):
                    pe.wait_ge(conv_silu, c.next("conv"))
                    pe.wait_ge(dn_copied, c.take("dn_copied"))
                    for r in range(4):
                        mm = pe.transpose(ps[2][:, r * P:r * P + P], pt[:, DQ + i, r * P:r * P + P], ident)
                    mm.then_inc(dn_full, c.up("dn_full"))
                for i in range(4):
                    pe.wait_ge(conv_silu, c.next("conv"))
                    pe.wait_ge(dn_copied, c.take("dn_copied"))
                    for r in range(4):
                        mm = pe.transpose(ps[2][:, r * P:r * P + P], pt[:, DV + i, r * P:r * P + P], ident)
                    mm.then_inc(dn_full, c.up("dn_full"))
                for i in range(8):
                    pe.wait_ge(kq_ready, c.next("kq"))
                    pe.wait_ge(dn_copied, c.take("dn_copied"))
                    src = T[:, i] if i < 4 else ktok[:, i - 4]
                    for r in range(4):
                        mm = pe.transpose(ps[2][:, r * P:r * P + P], src[:, r * P:r * P + P], ident)
                    mm.then_inc(dn_full, c.up("dn_full"))
                pe.wait_ge(rows_step, c.next("rows_step", 1))
                for r in range(4):
                    pe.transpose(ps[3][:, r * 8:r * 8 + 8], g_rows[:, r * P:r * P + P], ident[0:8, 0:8])
                for r in range(4):
                    mm = pe.transpose(ps[4][:, r * 16:r * 16 + 16], pt[0:16, AK, r * P:r * P + P], ident[0:16, 0:16])
                mm.then_inc(bc_full, 1)
                pe.wait_ge(dn_copied, c.now("dn_copied"))
                pe.wait_ge(rows_step, c.next("rows_step", 1))
                for step in range(4):
                    for stage in range(STAGES):
                        for d in range(2):
                            lane_pe(d, step, stage)
                for h in range(4):
                    if h == 0:
                        pe.wait_ge(oT_done, c.now("oT_done") + 4)
                        c.up("oT_done", 4)
                    pe.wait_ge(ut_copied, c.take("ut_copied"))
                    for r in range(4):
                        mm = pe.transpose(ps[7][:, r * P:r * P + P], pt[:, AO + r, h * P:h * P + P], ident)
                    mm.then_inc(ut_full, c.up("ut_full"))

            def lane_pe(d, step, stage):
                ch = step if d == 0 else 3 - step
                cs = slice(ch * P, ch * P + P)
                nt, sd, xx, xt, a1, qg, st = (four(t) for t in LANE[d])
                b0, b1, b2 = (four(ps[2 + 3 * d + i][:, :]) for i in range(3))

                def done(mm):
                    mm.then_inc(chunk_mm[d], c.up(f"mm{d}"))

                def ready():
                    pe.wait_ge(chunk_dve[d], c.next(f"cd{d}"))

                if stage == 0:
                    if step:
                        ready()
                    for h in range(4):
                        mm = pe.matmul(b0[:, h], rows8[:, (4 * d + h) * P:(4 * d + h) * P + P], g_rows[:, cs], start=True, stop=True)
                    done(mm)
                    for h in range(4):
                        pe.matmul(b1[:, h], pt[:, DK + h, cs], pt[:, DK + h, cs], start=True, stop=True)
                    for h in range(4):
                        mm = pe.matmul(b2[:, h], pt[:, DK + h, cs], pt[:, DQ + h, cs], start=True, stop=True)
                    done(mm)
                elif stage < 15:
                    m, half = divmod(stage - 1, 2)
                    ready()
                    if half == 0:
                        for h in range(4):
                            mm = pe.matmul(b0[:, h], nt[:, h], ident if m == 0 else xx[:, h], start=True, stop=True)
                    else:
                        if 0 < m < 6:
                            for h in range(4):
                                mm = pe.matmul(b1[:, h], xt[:, h], a1[:, h], start=True, stop=True)
                        for h in range(4):
                            mm = pe.matmul(b2[:, h], a1[:, h], ident if m == 0 else xt[:, h], start=True, stop=True)
                    done(mm)
                elif stage == 15:
                    ready()
                    for h in range(4):
                        mm = pe.matmul(b0[:, h], xt[:, h], nt[:, h], start=True, stop=True)
                    for h in range(4):
                        mm = pe.matmul(b1[:, h], a1[:, h], xt[:, h], start=True, stop=True)
                    done(mm)
                elif stage == 16:
                    pe.wait_ge(chunk_act[d], c.next(f"ca{d}", 2))
                    if step:
                        for h in range(4):
                            mm = pe.matmul(b2[:, h], xt[:, h], st[:, h], start=True, stop=True)
                        done(mm)
                else:
                    ready()
                    for h in range(4):
                        if step:
                            pe.matmul(b0[:, h], qg[:, h], st[:, h], start=True, stop=False)
                        pe.matmul(b0[:, h], sd[:, h], xx[:, h], start=not step, stop=True)
                    for h in range(4):
                        mm = pe.matmul(b1[:, h], nt[:, h], xx[:, h], start=True, stop=True)
                    done(mm)

            def cross():
                for i in range(4):
                    pe.wait_ge(vm_done, c.take("vm_done"))
                    for j in range(4):
                        f, t = 2 * i + j // 2, j % 2
                        mm = pe.transpose(ps[7][:, j * P:j * P + P], pt[:, 16 + f, t * P:t * P + P], ident)
                    mm.then_inc(vm_full, c.up("vm_full"))
                pe.wait_ge(vm_done, c.now("vm_done"))
                for h in range(4):
                    for q2 in range(2):
                        pe.wait_ge(sc_free, c.take("sc_free"))
                        for q in range(2):
                            qs = slice((2 * q2 + q) * P, (2 * q2 + q) * P + P)
                            for k in range(2):
                                mm = pe.matmul(ps[2][:, q * 256:q * 256 + 256], pt[:, 2 * h + k, qs], pt[:, 8 + 2 * h + k, 0:256],
                                               start=k == 0, stop=k == 1)
                        mm.then_inc(sc_full, c.up("sc_full"))
                        pe.wait_ge(prob_done, c.next("prob"))
                        pe.wait_ge(tr_copied, c.take("tr_copied"))
                        for q in range(2):
                            for t in range(2):
                                mm = pe.transpose(ps[4][:, t * 256 + q * P:t * 256 + q * P + P], T[:, 0, q * 256 + t * P:q * 256 + t * P + P], ident)
                        mm.then_inc(tr_full, c.up("tr_full"))
                    pe.wait_ge(tr_copied, c.now("tr_copied"))
                    pe.wait_ge(pv_copied, c.take("pv_copied"))
                    for f in range(2):
                        for t in range(2):
                            mm = pe.matmul(ps[5 + f][:, :], vm(2 * h + f, t), T[:, 2 + t], start=t == 0, stop=t == 1)
                    mm.then_inc(pv_full, c.up("pv_full"))

            pe.wait_ge(setup_in, 80)
            pe.wait_ge(par_ready, 3)
            for i in range(4):
                n = min(512, VEC_COLS - i * 512)
                mm = pe.matmul(ps[2 + i][0:10, 0:n], relb, hot[:, i * 512:i * 512 + n], start=True, stop=True)
            mm = pe.matmul(ps[6][:, 0:4], ones[0:64, :], lamp, start=True, stop=True)
            mm.then_inc(vec_ready, 1)
            pe.wait_ge(hankel_in, 160)
            for i in range(9):
                if i >= 6:
                    pe.wait_ge(bias_made, i - 5)
                if i == 0:
                    pe.wait_ge(act_step, 2)
                pe.matmul(ps[2 + i % 6][:, :], eye[:, P:2 * P], hankel[:, i * S:i * S + S], start=True, stop=True).then_inc(vec_ready, 1)
            pe.wait_ge(bias_made, 9)
            with c.loop(pe, LAYERS, PER["pe"]):
                ffn()
                mixers()
                ffn()
            second()

        @block.scalar
        def _(act):
            c = Count(FIRST)
            for free in (z_act, q_copied, tr_copied, pv_copied, ut_copied, rows_copied, dn_copied):
                act.sem_inc(free, 1)

            def pump(s):
                act.wait_ge(raw_full[s], c.next(f"raw{s}", 16))
                act.wait_ge(job_done[s], c.take(f"slot{s}"))
                act.activation(w_hi[:, s], raw[:, s], ACT.Copy).then_inc(hi_done[s], 1)

            def skip(s):
                c.up(f"job{s}")
                c.up(f"evac{s}")

            def prepare(k, gain, ready, n=S):
                act.wait_ge(*ready)
                act.activation(xsq[:, 0:n], tile(x, k, n), ACT.Square).then_inc(square_done, c.up("square"))
                act.activation(tile(u_hi, k, n), tile(x, k, n), ACT.Copy, scale=gain).then_inc(u_hi_done, c.up("u_hi"))

            def deviation(n=S):
                act.wait_ge(stat_done, c.next("stat"))
                act.activation(std[:, 0:n], ps[7][:, 0:n], ACT.Sqrt, bias=eps[:, 0:1], scale=1.0 / D).then_inc(std_done, c.up("std"))

            def gate(src, dst, bank, func, bias=0.0):
                act.wait_ge(evac[bank], c.next(f"evac{bank}"))
                act.activation(dst, src, func, bias=bias).then_inc(silu_done, c.up("silu"))
                c.up(f"job{bank}")

            def upper(k):
                act.wait_ge(h_done, c.next("h"))
                act.activation(tile(m_hi, k), hf, ACT.Copy).then_inc(m_hi_done, c.up("m_hi"))

            def residual_tile(s, k, gain):
                c.up(f"job{s}")
                prepare(k, par[:, ds(k + gain, 1)] if not isinstance(k, int) else par[:, k + gain:k + gain + 1],
                        (evac[s], c.next(f"evac{s}")))

            def last_tile(gain):
                residual_tile(1, 7, gain)

            def ffn(before, finish):
                for part, n in enumerate(FF_PARTS):
                    pump(1)
                    if part == 0:
                        before()
                        deviation()
                    pump(0)
                    gate(gr, sg, 0, ACT.Silu)
                    with c.loop(act, n - 1, {**AJOB, "silu": 1, "h": 1, "m_hi": 1}) as i:
                        pump(1)
                        upper(i)
                        skip(1)
                        pump(0)
                        gate(gr, sg, 0, ACT.Silu)
                    c.up("m", n)
                    pump(1)
                    upper(n - 1)
                    skip(1)
                    pump(0)
                    if part < 2:
                        skip(0)
                        skip(1)
                        with c.loop(act, 3, AJOB):
                            pump(1)
                            pump(0)
                            skip(0)
                            skip(1)
                    else:
                        finish()

            def residual_tiles(gain):
                residual_tile(0, 0, gain)
                with c.loop(act, 3, {**AJOB, "square": 2, "u_hi": 2}) as i:
                    pump(1)
                    residual_tile(1, i * 2 + 1, gain)
                    pump(0)
                    residual_tile(0, i * 2 + 2, gain)

            def fourier():
                act.wait_ge(tab_full, c.now("tab"))
                for g in range(8):
                    act.wait_ge(z_full, c.next("z_full"))
                    if g >= 2:
                        act.wait_ge(pq_full, c.now("pq"))
                    act.activation(T[:, 2 * (g % 2)], ps[2][:, :], ACT.Copy).then_inc(z_act, c.up("z_act"))
                    c.up("z_full")
                    if g:
                        fourier_out(g - 1)
                fourier_out(7)

            def fourier_out(g):
                act.wait_ge(pq_full, c.next("pq"))
                act.activation(T[:, 4, 0:HALF], ps[5][:, 0:HALF], ACT.Copy).then_inc(q_copied, c.up("q_copied"))
                act.wait_ge(h_done, c.next("h"))
                act.activation(tile(m_hi, g), T[:, 7], ACT.Copy).then_inc(m_hi_done, c.up("m_hi"))

            def dilated(g):
                n = 1024 if g == 0 else 512
                for h in range(2):
                    act.wait_ge(max_done, c.next("max"))
                    e = T[:, 0:2].rearrange("p a n -> p (a n)")[:, 0:n]
                    act.activation(e, e, ACT.Exp).then_inc(exp_done, c.up("exp"))
                    act.wait_ge(tr_full, c.next("tr_full"))
                    if g == 0:
                        act.activation(T[:, 3], ps[6][:, :], ACT.Copy)
                    act.activation(T[:, 2], ps[4][:, :], ACT.Copy).then_inc(tr_copied, c.up("tr_copied"))
                act.wait_ge(pv_full, c.next("pv_full"))
                act.activation(T[:, 4], ps[5][:, :], ACT.Copy).then_inc(pv_copied, c.up("pv_copied"))
                act.wait_ge(ut_full, c.next("ut_full"))
                act.activation(natural(g, pt[:, QB + g]), grouped(g, ps[7][:, :]), ACT.Copy).then_inc(ut_copied, c.up("ut_copied"))

            def dilated_rows():
                for rows in (rows_m, rows_z):
                    for g in range(3):
                        act.wait_ge(rows_full, c.next("rows_full"))
                        act.activation(natural(g, rows[:, g]), grouped(g, ps[2][0:2, :]), ACT.Copy).then_inc(rows_copied, c.up("rows_copied"))
                act.wait_ge(max_done, c.next("max"))
                act.activation(rows_m, rows_m, ACT.Exp).then_inc(mixw_exp, c.up("mixw"))
                upper(0)

            def dense():
                def exps(u):
                    act.wait_ge(max_done, c.next("max"))
                    b = u % 2
                    for m in range(2):
                        e = T[:, 2 * b + m]
                        ins = act.activation(e, e, ACT.Exp, bias=stats[:, 48 + 2 * b + m:49 + 2 * b + m],
                                             accum_out=stats[:, 52 + 2 * b + m:53 + 2 * b + m])
                    ins.then_inc(exp_done, c.up("exp"))

                exps(0)
                for u in range(16):
                    if u < 15:
                        exps(u + 1)
                    act.wait_ge(tr_full, c.next("tr_full"))
                    act.activation(T[:, 4 + u % 2], ps[4][:, :], ACT.Copy).then_inc(tr_copied, c.up("tr_copied"))
                    act.wait_ge(pv_full, c.next("pv_full"))
                    act.activation(pt[:, OC + u // 4, (u % 4) * P:(u % 4) * P + P], ps[5][:, 0:P], ACT.Copy)
                    act.activation(T[:, 6, 0:P], ps[5][:, 0:P], ACT.Square, accum_out=stats[:, 64 + u:65 + u]).then_inc(pv_copied, c.up("pv_copied"))
                    act.wait_ge(pv_copied, c.now("pv_copied"))
                act.activation(stats[:, 64:80], stats[:, 64:80], ACT.Sqrt, bias=eps[:, 1:2], scale=1.0 / P).then_inc(std_done, c.up("std"))
                for h in range(4):
                    act.wait_ge(ut_full, c.next("ut_full"))
                    act.activation(hf, ps[7][:, :], ACT.Copy, scale=par[:, LAYER_COLS["subln"]:LAYER_COLS["subln"] + 1]).then_inc(ut_copied, c.up("ut_copied"))
                    act.wait_ge(ut_copied, c.now("ut_copied"))
                    act.activation(tile(m_hi, 1 + h), hf, ACT.Copy).then_inc(m_hi_done, c.up("m_hi"))
                    act.wait_ge(m_ready, c.next("m"))

            def bgate(branch, m):
                return par[:, ds(m + (LAYER_COLS["b_gate"] + 8 * branch), 1)] if not isinstance(m, int) else \
                    par[:, LAYER_COLS["b_gate"] + 8 * branch + m:LAYER_COLS["b_gate"] + 8 * branch + m + 1]

            def mixers(before, gain):
                act.dma_start(tab[:, 0:DFT_COLS], dft_in).then_inc(tab_full, c.up("tab", 16))
                pump(1)
                before()
                deviation()
                pump(0)
                skip(0)
                skip(1)
                with c.loop(act, 14, AJOB):
                    pump(1)
                    pump(0)
                    skip(0)
                    skip(1)
                fourier()
                act.dma_start(tab[:, :], bias_dram).then_inc(tab_full, c.up("tab", 16))
                with c.loop(act, 8, {**AJOB, "silu": 1}) as m:
                    pump(1)
                    pump(0)
                    gate(gr, sg, 0, ACT.Sigmoid, bgate(0, m))
                    skip(1)
                act.wait_ge(evac[1], c.now("evac1"))
                c.up("m", 8)
                for g in range(3):
                    dilated(g)
                dilated_rows()
                c.up("m", 1)
                dense()
                with c.loop(act, 4, AJOB):
                    pump(1)
                    pump(0)
                    skip(0)
                    skip(1)
                pump(1)
                pump(0)
                gate(gr, sg, 0, ACT.Sigmoid, bgate(1, 0))
                with c.loop(act, 7, {**AJOB, "silu": 2, "h": 1, "m_hi": 1}) as m:
                    pump(1)
                    gate(ur, xsq, 1, ACT.Sigmoid, bgate(2, m))
                    upper(m)
                    pump(0)
                    gate(gr, sg, 0, ACT.Sigmoid, bgate(1, m + 1))
                pump(1)
                gate(ur, xsq, 1, ACT.Sigmoid, bgate(2, 7))
                upper(7)
                pump(0)
                residual_tiles(gain)
                c.up("m", 8)

            def step(ins):
                ins.then_inc(act_step, c.up("act"))
                act.wait_ge(act_step, c.now("act"))

            def column(at, k):
                return small[:, at + k:at + k + 1] if isinstance(k, int) else small[:, ds(k + at, 1)]

            def pairs(n):
                with c.loop(act, n, AJOB):
                    pump(1)
                    pump(0)
                    skip(0)
                    skip(1)

            def squares(s, k):
                c.up(f"job{s}")
                act.wait_ge(evac[s], c.next(f"evac{s}"))
                act.activation(xsq, tile(pt, k), ACT.Square).then_inc(square_done, c.up("square"))

            def pairs_with_squares(at):
                with c.loop(act, 4, {**AJOB, "square": 2}) as i:
                    pump(1)
                    squares(0, i * 2 + at)
                    pump(0)
                    squares(1, i * 2 + (at + 1))

            def last_squares():
                squares(0, 0)
                with c.loop(act, 2, {**AJOB, "square": 2}) as i:
                    pump(1)
                    squares(1, i * 2 + 1)
                    pump(0)
                    squares(0, i * 2 + 2)
                pump(1)
                squares(1, 5)
                squares(0, 6)
                squares(1, 7)

            def second():
                c.up("act", 2)
                act.dma_start(window, window_in).then_inc(tab2_in, 16)
                act.dma_start(swap, swap_in).then_inc(tab2_in, 16)
                act.dma_start(pos_i, bass.AP(pos_in.tensor, 0, [[0, P], [1, S]])).then_inc(tab2_in, 16)
                act.dma_start(tabt[:, 0:4].rearrange("p a n -> p (a n)"), mem_in.rearrange("p k n -> p (k n)")).then_inc(tab2_in, 16)
                act.dma_start(rows8, rows8_in).then_inc(tab2_in, 16)
                deviation()
                for k in range(KT):
                    prepare(k, column(TAIL["g_mix_pre"], k), (x_done, c.next("x")))
                pump(1)
                deviation()
                pump(0)
                skip(0)
                skip(1)
                pairs(11)
                act.wait_ge(tab2_in, 80)
                act.activation(T[:, 0:4], tabt[:, 0:4], ACT.Square).then_inc(square_done, c.up("square"))
                for s in range(2):
                    act.wait_ge(job_done[s], c.now(f"job{s}"))
                for k in range(KT):
                    act.activation(u_hi[:, k, 0:256], memt[:, k], ACT.Copy, scale=column(TAIL["g_mem"], k)).then_inc(u_hi_done, c.up("u_hi"))
                deviation(256)
                window_attention()
                delta_net()
                pairs_with_squares(0)
                pump(1)
                deviation()
                pump(0)
                skip(0)
                skip(1)
                with c.loop(act, 7, {**AJOB, "square": 1, "u_hi": 1, "x": 1}) as i:
                    pump(1)
                    prepare_m(i)
                    pump(0)
                    skip(0)
                    skip(1)
                prepare_m(7)
                pump(1)
                deviation()
                pump(0)
                skip(0)
                skip(1)
                pairs(3)
                cross()
                pairs_with_squares(8)
                deviation()
                for k in range(KT):
                    prepare(k, column(TAIL["g_ffn_pre"], k), (x_done, c.next("x")))
                ffn(lambda: None, last_squares)
                deviation()

            def prepare_m(k):
                act.wait_ge(x_done, c.next("x"))
                act.activation(xsq, tile(x, k), ACT.Square).then_inc(square_done, c.up("square"))
                act.activation(tile(m_hi, k), tile(x, k), ACT.Copy, scale=column(TAIL["g_cross_pre"], k)).then_inc(u_hi_done, c.up("u_hi"))

            def window_attention():
                act.wait_ge(angles_ready, 1)
                act.activation(cos, T[:, 1], ACT.Sin)
                act.activation(sin, T[:, 0], ACT.Sin).then_inc(tables_ready, 1)

                def exps(u):
                    act.wait_ge(max_done, c.next("max"))
                    b, n = u % 2, window_keys(u % 4)
                    for m in range(2):
                        e = T[:, 2 * b + m, 0:n]
                        act.activation(e, e, ACT.Exp, bias=stats[:, 48 + 2 * b + m:49 + 2 * b + m],
                                       accum_out=stats[:, 52 + 2 * b + m:53 + 2 * b + m])
                    sink = stats[:, 56 + 2 * b:58 + 2 * b]
                    act.activation(sink, sink, ACT.Exp).then_inc(exp_done, c.up("exp"))

                exps(0)
                for u in range(16):
                    if u < 15:
                        exps(u + 1)
                    n = window_keys(u % 4)
                    act.wait_ge(tr_full, c.next("tr_full"))
                    act.activation(T[:, 4, 0:n], ps[4][:, 0:n], ACT.Copy)
                    act.activation(T[:, 5, 0:n], ps[6][:, 0:n], ACT.Copy).then_inc(tr_copied, c.up("tr_copied"))
                c.up("pv_full", 16)
                for f in range(4):
                    act.wait_ge(ut_full, c.next("ut_full"))
                    if f == 0:
                        act.dma_start(chunk, chunk_in).then_inc(tab3_in, 16)
                    act.activation(hf, ps[7][:, :], ACT.Copy).then_inc(ut_copied, c.up("ut_copied"))
                    act.wait_ge(ut_copied, c.now("ut_copied"))
                    act.activation(tile(m_hi, f), hf, ACT.Copy).then_inc(m_hi_done, c.up("m_hi"))
                    act.wait_ge(m_ready, c.next("m"))

            def delta_net():
                def to_tokens(i, dst):
                    act.wait_ge(dn_full, c.next("dn_full"))
                    act.activation(dst, ps[2][:, :], ACT.Copy).then_inc(dn_copied, c.up("dn_copied"))

                for i in range(DN_TILES):
                    act.wait_ge(conv_done, c.next("conv_done"))
                    act.activation(pt[:, DQ + i], T[:, 6 + i % 2], ACT.Silu).then_inc(conv_silu, c.up("conv"))
                    to_tokens(i, T[:, i] if i < 4 else ktok[:, i - 4] if i < 8 else pt[:, DV + i - 8])
                act.wait_ge(row_terms, c.next("terms"))
                e = T[0:8, 5]
                step(act.activation(e, e, ACT.Exp))
                act.activation(e, e, ACT.Ln, bias=ones[0:8, 0:1])
                act.activation(stats[0:8, 88:89], small[0:8, A_LOG:A_LOG + 1], ACT.Exp)
                act.activation(pt[0:16, AK], pt[0:16, AB], ACT.Sigmoid).then_inc(row_exps, c.up("exps"))
                act.wait_ge(row_terms, c.next("terms"))
                act.activation(stats[:, 0:32], stats[:, 0:32], ACT.Sqrt, bias=eps[:, 0:1]).then_inc(row_exps, c.up("exps"))
                for i in range(8):
                    to_tokens(i, pt[:, DQ + i])
                act.activation(pt[:, DG:DG + 4], pt[:, DG:DG + 4], ACT.Silu).then_inc(row_exps, c.up("exps"))
                act.wait_ge(row_terms, c.next("terms"))
                act.activation(beg, gcol, ACT.Exp).then_inc(row_exps, c.up("exps"))
                for s in range(4):
                    for d in range(2):
                        b0 = ps[2 + 3 * d]
                        act.wait_ge(chunk_terms[d], c.next(f"terms{d}"))
                        act.activation(LANE[d][5], b0[:, :], ACT.Exp)
                        act.activation(stats[:, 224 + 8 * d:232 + 8 * d], stats[:, 224 + 8 * d:232 + 8 * d], ACT.Exp)
                        act.activation(LANE[d][4], LANE[d][4], ACT.Exp).then_inc(chunk_act[d], c.up(f"ca{d}"))
                    for d in range(2):
                        act.wait_ge(chunk_mm[d], c.next(f"mm{d}", 17))
                        act.activation(LANE[d][2], ps[2 + 3 * d][:, :], ACT.Copy)
                        act.activation(LANE[d][3], ps[3 + 3 * d][:, :], ACT.Copy).then_inc(chunk_act[d], c.up(f"ca{d}"))
                        c.up(f"mm{d}", 2 if s else 1)
                act.wait_ge(row_terms, c.next("terms"))
                act.activation(stats[:, 0:16], stats[:, 0:16], ACT.Sqrt, bias=eps[:, 0:1], scale=1.0 / P).then_inc(row_exps, c.up("exps"))
                for h in range(4):
                    upper(4 + h)
                c.up("m", 4)

            def cross():
                for h in range(4):
                    for q2 in range(2):
                        act.wait_ge(max_done, c.next("max"))
                        for q in range(2):
                            ins = act.activation(T[:, 0, q * 256:q * 256 + 256], ps[2][:, q * 256:q * 256 + 256], ACT.Exp, scale=0.0625,
                                                 bias=stats[:, 48 + q:49 + q], accum_out=stats[:, 52 + q:53 + q])
                        ins.then_inc(exp_done, c.up("exp"))
                        act.wait_ge(tr_full, c.next("tr_full"))
                        act.activation(T[:, 2:4, q2 * 256:q2 * 256 + 256], ps[4][:, :].rearrange("p (t n) -> p t n", t=2), ACT.Copy).then_inc(tr_copied, c.up("tr_copied"))
                    act.wait_ge(pv_full, c.next("pv_full"))
                    for f in range(2):
                        act.activation(tile(u_hi, 2 * h + f), ps[5 + f][:, :], ACT.Copy).then_inc(u_hi_done, c.up("u_hi"))

            act.dma_start(hot, hot_in).then_inc(setup_in, 16)
            act.dma_start(pt[0:32, 4, 0:10], rel_in).then_inc(setup_in, 16)
            act.dma_start(lamv, lam_in).then_inc(setup_in, 16)
            act.dma_start(eye[:, :], eye_in).then_inc(setup_in, 16)
            act.dma_start(sel[:, :], sel_in).then_inc(setup_in, 16)
            act.wait_ge(loaded, 32)
            for k in range(KT):
                if k:
                    act.wait_ge(acc_step, k)
                prepare(k, small[:, TAIL["g_first"] + k:TAIL["g_first"] + k + 1], (par_ready, 3))
            pump(0)
            act.wait_ge(vec_ready, 1)
            act.activation(stats[:, 0:4], ps[6][:, 0:4], ACT.Exp).then_inc(act_step, 1)
            for i in range(4):
                n = min(512, VEC_COLS - i * 512)
                ins = act.activation(vec_sb[:, i * 512:i * 512 + n], ps[2 + i][0:10, 0:n], ACT.Copy)
            ins.then_inc(act_step, 1)
            act.wait_ge(act_step, 2)
            act.dma_start(vec_dram, vec_sb).then_inc(vec_stored, 16)
            act.wait_ge(vec_stored, 16)
            for i in range(10):
                start = HEAD_OF[i] * VEC_COLS + VEC[KIND_OF[i]][0]
                act.dma_start(hankel[:, BIAS_AT[i]:BIAS_AT[i] + BIAS_N[i]],
                              bass.AP(vec_dram.tensor, start, [[1, P], [1, BIAS_N[i]]])).then_inc(hankel_in, 16)
            act.wait_ge(bias_made, 9)
            act.dma_start(bias_dram, tab[:, :]).then_inc(bias_stored, 16)
            act.wait_ge(bias_stored, 16)
            before = lambda: None
            with c.loop(act, LAYERS, PER["act"]) as l:
                ffn(before, lambda: residual_tiles(LAYER_COLS["g_mix"]))
                mixers(lambda: last_tile(LAYER_COLS["g_mix"]), LAYER_COLS["g_ffn2"])
                ffn(lambda: last_tile(LAYER_COLS["g_ffn2"]), lambda: residual_tiles(LAYER_COLS["g_next"]))
                last_tile(LAYER_COLS["g_next"])
            second()

        @block.vector
        def _(dve):
            c = Count(FIRST, inner_loops)
            dve.memset(ones[:, :], 1.0)
            dve.memset(acc, 0.0).then_inc(dve_step, c.up("dve"))
            for s in range(2):
                dve.sem_inc(evac[s], 1)
            for free in (z_dve, y_done, vt_done, sc_free, wb_free, oT_done, rope_done, vm_done):
                dve.sem_inc(free, 1)
            dve.memset(eps[:, 0:1], EPS)
            dve.memset(eps[:, 1:2], 1e-5).then_inc(par_ready, 1)
            dve.memset(relb[32:33], 1.0).then_inc(par_ready, 1)
            dve.wait_ge(dve_step, c.now("dve"))

            def step(ins):
                ins.then_inc(dve_step, c.up("dve"))
                dve.wait_ge(dve_step, c.now("dve"))

            def prepare(k, gain, n=S):
                dve.wait_ge(square_done, c.next("square"))
                dve.wait_ge(acc_step, c.now("acc")) if c.n.get("acc", 0) or c.loops else None
                dve.tensor_tensor(acc[:, 0:n], acc[:, 0:n], xsq[:, 0:n], ALU.add).then_inc(acc_step, c.up("acc"))
                dve.wait_ge(u_hi_done, c.next("u_hi"))
                dve.scalar_tensor_tensor(out=tile(u_lo, k), in0=tile(x, k), scalar=gain, in1=tile(u_hi, k).bitcast(F32),
                                         op0=ALU.mult, op1=ALU.subtract).then_inc(u_ready, c.up("u"))

            def reciprocal_rms(n=S):
                dve.wait_ge(std_done, c.next("std"))
                step(dve.reciprocal(rs[:, 0:n], std[:, 0:n]))

            def scaled(s, dst):
                dve.wait_ge(job_done[s], c.next(f"job{s}"))
                dve.tensor_tensor(dst, ps[s][:, :], rs[:, :], ALU.mult).then_inc(evac[s], c.up(f"evac{s}"))

            def lower(k):
                dve.wait_ge(m_hi_done, c.next("m_hi"))
                dve.tensor_tensor(tile(m_lo, k), hf, tile(m_hi, k).bitcast(F32), ALU.subtract).then_inc(m_ready, c.up("m"))

            def ff_tile(k):
                scaled(0, gr)
                scaled(1, ur)
                dve.wait_ge(evac[1], c.now("evac1"))
                dve.wait_ge(silu_done, c.next("silu"))
                dve.tensor_tensor(hf, sg, ur, ALU.mult).then_inc(h_done, c.up("h"))
                lower(k)

            def residual(s, k, scale):
                dve.wait_ge(job_done[s], c.next(f"job{s}"))
                dve.scalar_tensor_tensor(out=tile(x, k), in0=ps[s][:, :], scalar=scale, in1=tile(x, k),
                                         op0=ALU.mult, op1=ALU.add).then_inc(evac[s], c.up(f"evac{s}"))
                dve.wait_ge(evac[s], c.now(f"evac{s}"))

            def residual_tiles(scale, gain):
                step(dve.memset(acc, 0.0))
                with c.loop(dve, 4, {**JOB, "square": 2, "u_hi": 2, "u": 2, "acc": 2}) as i:
                    for s in range(2):
                        residual(s, i * 2 + s, scale)
                        prepare(i * 2 + s, par[:, ds(i * 2 + (s + gain), 1)])

            def ffn(gain):
                reciprocal_rms()
                for part, n in enumerate(FF_PARTS):
                    with c.loop(dve, n, {**JOB, "silu": 1, "h": 1, "m_hi": 1, "m": 1}) as i:
                        ff_tile(i)
                    if part < 2:
                        with c.loop(dve, 4, JOB) as i:
                            for s in range(2):
                                residual(s, i * 2 + s, 0.5)
                    else:
                        residual_tiles(0.5, gain)

            def fourier():
                for g in range(8):
                    c.up("z_full")
                    dve.wait_ge(z_full, c.next("z_full"))
                    if g >= 2:
                        dve.wait_ge(pq_full, c.now("pq"))
                    dve.tensor_copy(T[:, 2 * (g % 2) + 1], ps[3][:, :]).then_inc(z_dve, c.up("z_dve"))
                    if g:
                        fourier_out(g - 1)
                fourier_out(7)

            def fourier_out(g):
                dve.wait_ge(q_copied, c.next("q_copied"))
                c.up("pq")
                if g:
                    dve.wait_ge(m_ready, c.now("m"))
                dve.tensor_tensor(T[:, 7, 0:HALF], ps[4][:, 0:HALF], T[:, 4, 0:HALF], ALU.subtract)
                dve.tensor_tensor(T[:, 7, S - 1:HALF - 1:-1], ps[4][:, 1:HALF - 1], T[:, 4, 1:HALF - 1], ALU.add).then_inc(y_done, c.up("y_done"))
                dve.wait_ge(y_done, c.now("y_done"))
                dve.sem_inc(h_done, c.up("h"))
                dve.wait_ge(m_hi_done, c.next("m_hi"))
                dve.tensor_tensor(tile(m_lo, g), T[:, 7], tile(m_hi, g).bitcast(F32), ALU.subtract).then_inc(m_ready, c.up("m"))

            def dilated(g):
                dve.wait_ge(vt_full, c.next("vt_full"))
                if g == 0:
                    dve.tensor_copy(pt[:, 29, 0:P], ps[6][:, 0:P])
                dve.tensor_copy(pt[:, VB + g], ps[5][:, :]).then_inc(vt_done, c.up("vt_done"))
                n = 256 if g == 0 else P
                l = T[:, 0:2].rearrange("p a n -> p (a n)")[:, 0:4 * n]
                l4 = l.rearrange("p (t n) -> p t n", t=4)
                for h in range(2):
                    a = BIAS_AT[4 + 2 * g + h]
                    bias = tab[:, a:a + n]
                    dve.wait_ge(sc_full, c.next("sc_full"))
                    if h:
                        dve.wait_ge(tr_full, c.now("tr_full"))
                    if g == 0:
                        dve.memset(l[:, 0:64], -1e30)
                        dve.memset(l[:, 960:1024], -1e30)
                        for r in range(4):
                            lo, hi = (64 if r == 0 else 0), (192 if r == 3 else 256)
                            ins = dve.scalar_tensor_tensor(out=l4[:, r, lo:hi], in0=ps[2 + r // 2][:, (r % 2) * 256 + lo:(r % 2) * 256 + hi],
                                                           scalar=0.125, in1=bias[:, lo:hi], op0=ALU.mult, op1=ALU.add)
                    else:
                        ins = dve.scalar_tensor_tensor(out=l4, in0=ps[2][:, :].rearrange("p (t n) -> p t n", t=4), scalar=0.125,
                                                       in1=bias[:, None, :].broadcast_to([P, 4, P]), op0=ALU.mult, op1=ALU.add)
                    ins.then_inc(sc_free, c.up("sc_free"))
                    dve.wait_ge(sc_free, c.now("sc_free"))
                    step(dve.tensor_reduce(nmax[:, g, :, h], l4, AX.X, ALU.max, negate=True))
                    dve.tensor_tensor(l4, l4, nmax[:, g, :, h:h + 1].broadcast_to([P, 4, n]), ALU.add).then_inc(max_done, c.up("max"))
                    dve.wait_ge(exp_done, c.next("exp"))
                    dve.tensor_reduce(total[:, g, :, h], l4, AX.X, ALU.add).then_inc(total_done, c.up("total"))
                    dve.wait_ge(total_done, c.now("total"))
                    c.up("tr_full")

            def dilated_rows():
                c.up("rows", 6)
                dve.wait_ge(rows_copied, c.now("rows") + 1)
                least = T[0:2, 0]
                step(dve.tensor_tensor(least, rows_m[:, 0], rows_m[:, 1], ALU.min))
                step(dve.tensor_tensor(least, least, rows_m[:, 2], ALU.min))
                dve.tensor_tensor(rows_m, T[0:2, 0:1, :].broadcast_to([2, 3, S]), rows_m, ALU.subtract).then_inc(max_done, c.up("max"))
                dve.wait_ge(mixw_exp, c.next("mixe"))
                step(dve.tensor_tensor(rows_z, rows_z, rows_m, ALU.mult))
                step(dve.tensor_tensor(T[0:2, 1], rows_z[:, 0], rows_z[:, 1], ALU.add))
                step(dve.tensor_tensor(T[0:2, 1], T[0:2, 1], rows_z[:, 2], ALU.add))
                step(dve.reciprocal(T[0:2, 2], T[0:2, 1]))
                dve.tensor_tensor(rows_m, rows_m, T[0:2, 2:3, :].broadcast_to([2, 3, S]), ALU.mult).then_inc(mixw_done, c.up("mixw"))
                for g in range(3):
                    dve.wait_ge(wb_full, c.next("wb_full"))
                    dst = hf if g == 0 else T[:, 5]
                    dve.tensor_tensor(dst, pt[:, QB + g], ps[3][:, :], ALU.mult).then_inc(wb_free, c.up("wb_free"))
                    dve.wait_ge(wb_free, c.now("wb_free"))
                    if g == 1:
                        step(dve.tensor_tensor(hf, hf, T[:, 5], ALU.add))
                    if g == 2:
                        dve.tensor_tensor(hf, hf, T[:, 5], ALU.add).then_inc(h_done, c.up("h"))
                lower(0)

            def dense():
                for h in range(4):
                    dve.wait_ge(vt_full, c.next("vt_full"))
                    dve.tensor_copy(pt[:, VC + h], ps[6][:, :]).then_inc(vt_done, c.up("vt_done"))

                def logits(u):
                    h, r = divmod(u, 4)
                    b = u % 2
                    dve.wait_ge(sc_full, c.next("sc_full"))
                    if u >= 2:
                        dve.wait_ge(tr_full, c.now("tr_full"))
                    a = BIAS_AT[h] + 384 - r * P
                    for m in range(2):
                        ins = dve.scalar_tensor_tensor(out=T[:, 2 * b + m], in0=ps[2 + m][:, :], scalar=0.125,
                                                       in1=tab[:, a:a + S], op0=ALU.mult, op1=ALU.add)
                    ins.then_inc(sc_free, c.up("sc_free"))
                    dve.wait_ge(sc_free, c.now("sc_free"))
                    dve.tensor_reduce(stats[:, 48 + 2 * b:50 + 2 * b], T[:, 2 * b:2 * b + 2], AX.X, ALU.max, negate=True).then_inc(max_done, c.up("max"))

                def probabilities(u):
                    b = u % 2
                    dve.wait_ge(exp_done, c.next("exp"))
                    if u:
                        dve.wait_ge(prob_done, c.now("prob"))
                    step(dve.reciprocal(stats[:, 56:58], stats[:, 52 + 2 * b:54 + 2 * b]))
                    step(dve.tensor_tensor(stats[:, 58:59], stats[:, 57:58], par[:, 49:50], ALU.mult))
                    step(dve.tensor_scalar(T[:, 2 * b + 1], T[:, 2 * b + 1], stats[:, 58:59], None, ALU.mult))
                    dve.scalar_tensor_tensor(out=T[:, 2 * b + 1], in0=T[:, 2 * b], scalar=stats[:, 56:57], in1=T[:, 2 * b + 1],
                                             op0=ALU.mult, op1=ALU.add).then_inc(prob_done, c.up("prob"))

                logits(0)
                for u in range(16):
                    if u < 15:
                        logits(u + 1)
                    probabilities(u)
                    c.up("tr_full")
                dve.wait_ge(std_done, c.next("std"))
                step(dve.reciprocal(stats[:, 80:96], stats[:, 64:80]))
                step(dve.tensor_scalar(stats[:, 80:96], stats[:, 80:96], par[:, 50:51], None, ALU.mult))
                for h in range(4):
                    o = pt[:, OC + h].rearrange("p (t n) -> p t n", t=4)
                    dve.tensor_tensor(o, o, stats[:, 80 + 4 * h:84 + 4 * h, None].broadcast_to([P, 4, P]), ALU.mult).then_inc(oT_done, c.up("oT_done"))
                for h in range(4):
                    lower(1 + h)

            def mixers():
                reciprocal_rms()
                with c.loop(dve, 15, JOB) as i:
                    for s in range(2):
                        scaled(s, tile(pt, i * 2 + s))
                for s in range(2):
                    dve.wait_ge(evac[s], c.now(f"evac{s}"))
                fourier()
                with c.loop(dve, 8, {**JOB, "silu": 1}) as m:
                    scaled(0, gr)
                    dve.wait_ge(silu_done, c.next("silu"))
                    dve.wait_ge(job_done[1], c.next("job1"))
                    dve.tensor_tensor(tile(pt, m), sg, ps[1][:, :], ALU.mult).then_inc(evac[1], c.up("evac1"))
                dve.wait_ge(evac[1], c.now("evac1"))
                dve.wait_ge(tab_full, c.next("tab", 32))
                for g in range(3):
                    dilated(g)
                dilated_rows()
                dense()
                c.up("pv_full", 3 + 16)
                with c.loop(dve, 4, JOB) as i:
                    for s in range(2):
                        dve.wait_ge(job_done[s], c.next(f"job{s}"))
                        dve.tensor_copy(tile(pt, i * 2 + (s + YB)), ps[2 + s][:, :])
                        dve.tensor_copy(tile(pt, i * 2 + (s + YC)), ps[s][:, :]).then_inc(evac[s], c.up(f"evac{s}"))
                for s in range(2):
                    dve.wait_ge(evac[s], c.now(f"evac{s}"))
                with c.loop(dve, 8, {**JOB, "silu": 2, "dve": 3, "h": 1, "m_hi": 1, "m": 1}) as m:
                    scaled(0, gr)
                    scaled(1, ur)
                    dve.wait_ge(silu_done, c.next("silu"))
                    step(dve.tensor_tensor(hf, sg, tile(pt, m + YB), ALU.mult))
                    step(dve.tensor_tensor(hf, hf, tile(pt, m), ALU.add))
                    dve.wait_ge(silu_done, c.next("silu"))
                    step(dve.tensor_tensor(std, xsq, tile(pt, m + YC), ALU.mult))
                    dve.tensor_tensor(hf, hf, std, ALU.add).then_inc(h_done, c.up("h"))
                    lower(m)
                residual_tiles(1.0, LAYER_COLS["g_ffn2"])

            def column(at, k):
                return small[:, at + k:at + k + 1] if isinstance(k, int) else small[:, ds(k + at, 1)]

            def add_squares():
                dve.wait_ge(square_done, c.next("square"))
                dve.wait_ge(acc_step, c.now("acc"))
                dve.tensor_tensor(acc, acc, xsq, ALU.add).then_inc(acc_step, c.up("acc"))

            def normed_tile(k, at, gain):
                step(dve.tensor_tensor(gr, tile(pt, k + at), rs[:, :], ALU.mult))
                dve.scalar_tensor_tensor(out=tile(x, k), in0=gr, scalar=column(TAIL[gain], k), in1=tile(x, k),
                                         op0=ALU.mult, op1=ALU.add).then_inc(x_done, c.up("x"))
                dve.wait_ge(x_done, c.now("x"))

            def keep_with_squares(at):
                step(dve.memset(acc, 0.0))
                with c.loop(dve, 4, {**JOB, "square": 2, "acc": 2}) as i:
                    for s in range(2):
                        dve.wait_ge(job_done[s], c.next(f"job{s}"))
                        dve.tensor_copy(tile(pt, i * 2 + (s + at)), ps[s][:, :]).then_inc(evac[s], c.up(f"evac{s}"))
                        add_squares()

            def second():
                reciprocal_rms()
                step(dve.memset(acc, 0.0))
                for k in range(KT):
                    dve.scalar_tensor_tensor(out=tile(x, k), in0=tile(x, k), scalar=column(LC + LAYER_COLS["g_next"], k), in1=rs[:, :],
                                             op0=ALU.mult, op1=ALU.mult).then_inc(x_done, c.up("x"))
                    dve.wait_ge(x_done, c.now("x"))
                    prepare(k, column(TAIL["g_mix_pre"], k))
                reciprocal_rms()
                with c.loop(dve, 12, JOB) as i:
                    for s in range(2):
                        scaled(s, tile(pt, i * 2 + s))
                dve.wait_ge(square_done, c.next("square"))
                dve.tensor_reduce(acc[:, 0:256], T[:, 0:4].rearrange("p a n -> p (a n)").rearrange("p (k n) -> p n k", k=KT),
                                  AX.X, ALU.add).then_inc(acc_step, c.up("acc", 8))
                for k in range(KT):
                    dve.wait_ge(u_hi_done, c.next("u_hi"))
                    dve.scalar_tensor_tensor(out=u_lo[:, k, 0:256], in0=memt[:, k], scalar=column(TAIL["g_mem"], k),
                                             in1=u_hi[:, k, 0:256].bitcast(F32), op0=ALU.mult, op1=ALU.subtract).then_inc(u_ready, c.up("u"))
                dve.wait_ge(std_done, c.next("std"))
                step(dve.reciprocal(rs_mem[:, :], std[:, 0:256]))
                window_attention()
                delta_net()
                keep_with_squares(0)

                def memory_pair(i):
                    for s in range(2):
                        dve.wait_ge(job_done[s], c.next(f"job{s}"))
                        k = i * 2 + (s + 8)
                        dst = pt[:, k, 0:256] if isinstance(k, int) else pt[:, ds(k, 1), 0:256].rearrange("p o n -> p (o n)")
                        dve.tensor_tensor(dst, ps[s][:, 0:256], rs_mem[:, :], ALU.mult).then_inc(evac[s], c.up(f"evac{s}"))

                def cross_input(k):
                    normed_tile(k, 0, "g_mix_post")
                    add_squares()
                    dve.wait_ge(u_hi_done, c.next("u_hi"))
                    dve.scalar_tensor_tensor(out=tile(m_lo, k), in0=tile(x, k), scalar=column(TAIL["g_cross_pre"], k),
                                             in1=tile(m_hi, k).bitcast(F32), op0=ALU.mult, op1=ALU.subtract).then_inc(m_ready, c.up("m"))

                memory_pair(0)
                reciprocal_rms()
                step(dve.memset(acc, 0.0))
                with c.loop(dve, 7, {**JOB, "square": 1, "acc": 1, "u_hi": 1, "m": 1, "x": 1, "dve": 1}) as i:
                    memory_pair(i + 1)
                    cross_input(i)
                cross_input(7)
                reciprocal_rms()
                with c.loop(dve, 4, JOB) as i:
                    for s in range(2):
                        scaled(s, tile(pt, i * 2 + s))
                cross()
                keep_with_squares(8)
                reciprocal_rms()
                step(dve.memset(acc, 0.0))
                for k in range(KT):
                    normed_tile(k, 8, "g_cross_post")
                    prepare(k, column(TAIL["g_ffn_pre"], k))
                reciprocal_rms()
                for part, n in enumerate(FF_PARTS):
                    with c.loop(dve, n, {**JOB, "silu": 1, "h": 1, "m_hi": 1, "m": 1}) as i:
                        ff_tile(i)
                    if part == 0:
                        with c.loop(dve, 4, JOB) as i:
                            for s in range(2):
                                dve.wait_ge(job_done[s], c.next(f"job{s}"))
                                dve.tensor_copy(tile(pt, i * 2 + s), ps[s][:, :]).then_inc(evac[s], c.up(f"evac{s}"))
                    if part == 2:
                        step(dve.memset(acc, 0.0))
                    if part:
                        with c.loop(dve, 4, JOB if part == 1 else {**JOB, "square": 2, "acc": 2}) as i:
                            for s in range(2):
                                dve.wait_ge(job_done[s], c.next(f"job{s}"))
                                dst = tile(pt, i * 2 + s)
                                dve.tensor_tensor(dst, dst, ps[s][:, :], ALU.add).then_inc(evac[s], c.up(f"evac{s}"))
                                if part == 2:
                                    add_squares()
                reciprocal_rms()
                for k in range(KT):
                    normed_tile(k, 0, "g_ffn_post")

            def window_attention():
                step(dve.tensor_scalar(neg_sink, small[:, SINK:SINK + 8], -1.0, None, ALU.mult))
                ang, k, a, b = T[:, 0], T[:, 1], T[:, 2], T[:, 3]
                step(dve.tensor_copy(ang, pos_i))
                step(dve.tensor_scalar(ang, ang, small[:, INV_FREQ:INV_FREQ + 1], None, ALU.mult))
                step(dve.tensor_scalar(k, ang, float(1 / (2 * np.pi)), ROUND, ALU.mult, ALU.add))
                step(dve.tensor_scalar(k, k, ROUND, None, ALU.subtract))
                for turn in TWO_PI:
                    step(dve.scalar_tensor_tensor(out=ang, in0=k, scalar=-turn, in1=ang, op0=ALU.mult, op1=ALU.add))
                step(dve.tensor_scalar(a, ang, float(np.pi / 2), None, ALU.add))
                step(dve.tensor_scalar(b, a, float(np.pi), float(-2 * np.pi), ALU.is_gt, ALU.mult))
                step(dve.tensor_tensor(k, a, b, ALU.add))
                step(dve.tensor_scalar(ang, ang, NEAR_PI, -NEAR_PI, ALU.min, ALU.max))
                dve.tensor_scalar(k, k, NEAR_PI, -NEAR_PI, ALU.min, ALU.max).then_inc(angles_ready, 1)
                dve.wait_ge(tables_ready, 1)
                for i in range(5):
                    dve.wait_ge(rope_full, c.next("rope_full"))
                    step(dve.tensor_tensor(a, ps[2][:, :], sin, ALU.mult))
                    step(dve.tensor_tensor(pt[:, i], pt[:, i], cos, ALU.mult))
                    dve.tensor_tensor(pt[:, i], pt[:, i], a, ALU.add).then_inc(rope_done, c.up("rope_done"))
                    dve.wait_ge(rope_done, c.now("rope_done"))
                dve.wait_ge(vt_full, c.next("vt_full"))
                dve.tensor_copy(pt[:, AV], ps[6][:, :]).then_inc(vt_done, c.up("vt_done"))

                def logits(u):
                    j, r = divmod(u, 4)
                    b, n = u % 2, window_keys(r)
                    dve.wait_ge(sc_full, c.next("sc_full"))
                    if u >= 2:
                        dve.wait_ge(tr_full, c.now("tr_full"))
                    w = window[:, 0 if r else P:(0 if r else P) + n]
                    for m in range(2):
                        ins = dve.scalar_tensor_tensor(out=T[:, 2 * b + m, 0:n], in0=ps[2 + m][:, 0:n], scalar=0.125, in1=w,
                                                       op0=ALU.mult, op1=ALU.add)
                    ins.then_inc(sc_free, c.up("sc_free"))
                    dve.wait_ge(sc_free, c.now("sc_free"))
                    top = stats[:, 48 + 2 * b:50 + 2 * b]
                    step(dve.tensor_reduce(top, T[:, 2 * b:2 * b + 2, 0:n], AX.X, ALU.max, negate=True))
                    step(dve.tensor_tensor(top, top, neg_sink[:, j:j + 5:4], ALU.min))
                    dve.tensor_tensor(stats[:, 56 + 2 * b:58 + 2 * b], top, neg_sink[:, j:j + 5:4], ALU.subtract).then_inc(max_done, c.up("max"))

                def outputs(u):
                    j, r = divmod(u, 4)
                    b = u % 2
                    dve.wait_ge(exp_done, c.next("exp"))
                    share = stats[:, 60 + 2 * b:62 + 2 * b]
                    step(dve.tensor_tensor(share, stats[:, 52 + 2 * b:54 + 2 * b], stats[:, 56 + 2 * b:58 + 2 * b], ALU.add))
                    step(dve.reciprocal(share, share))
                    dve.wait_ge(pv_full, c.next("pv_full"))
                    o = pt[:, AO + r].rearrange("p (m n) -> p m n", m=2)[:, :, 64 * j:64 * j + 64]
                    dve.tensor_tensor(o, ps[5][:, 0:P].rearrange("p (m n) -> p m n", m=2),
                                      share[:, :, None].broadcast_to([P, 2, 64]), ALU.mult).then_inc(pv_copied, c.up("pv_copied"))

                logits(0)
                for u in range(16):
                    if u < 15:
                        logits(u + 1)
                    outputs(u)
                    c.up("tr_full")
                for f in range(4):
                    lower(f)

            def delta_net():
                for i in range(DN_TILES):
                    src, dst = pt[:, DQ + i], T[:, 6 + i % 2]
                    if i >= 2:
                        dve.wait_ge(conv_silu, i - 1)
                    tap = lambda t: small[:, CONV + 5 * i + t:CONV + 5 * i + t + 1]
                    step(dve.tensor_scalar(dst, src, tap(2), None, ALU.mult))
                    for t in (0, 1, 3, 4):
                        to, frm = (slice(2 - t, S), slice(0, S - 2 + t)) if t < 2 else (slice(0, S + 2 - t), slice(t - 2, S))
                        ins = dve.scalar_tensor_tensor(out=dst[:, to], in0=src[:, frm], scalar=tap(t), in1=dst[:, to], op0=ALU.mult, op1=ALU.add)
                        if t < 4:
                            step(ins)
                    ins.then_inc(conv_done, c.up("conv_done"))
                z, e = T[0:8, 4], T[0:8, 5]
                step(dve.tensor_scalar(z, g_rows, small[0:8, DT_BIAS:DT_BIAS + 1], None, ALU.add))
                step(dve.scalar_tensor_tensor(out=e, in0=z, scalar=-1.0, in1=z, op0=ALU.mult, op1=ALU.min))
                dve.tensor_scalar(z, z, 0.0, None, ALU.max).then_inc(row_terms, c.up("terms"))
                for i in range(8):
                    dve.wait_ge(dn_copied, c.next("dn_copied"))
                    t = T[:, i] if i < 4 else ktok[:, i - 4]
                    sq = T[:, 6 + i % 2]
                    if i < 2:
                        dve.wait_ge(conv_silu, 11 + i)
                    step(dve.tensor_tensor(sq, t, t, ALU.mult))
                    step(dve.tensor_reduce(stats[:, 4 * i:4 * i + 4], four(sq), AX.X, ALU.add))
                dve.sem_inc(row_terms, c.up("terms"))
                c.up("dn_copied", 12)
                dve.wait_ge(row_exps, c.next("exps"))
                step(dve.tensor_tensor(z, z, e, ALU.add))
                step(dve.tensor_scalar(z, z, stats[0:8, 88:89], -1.0, ALU.mult, ALU.mult))
                ahead, back = T[0:8, 6], T[0:8, 7]
                for ch in range(4):
                    cs = slice(ch * P, ch * P + P)
                    dve.tensor_tensor_scan(ahead[:, cs], ones[0:8, :], z[:, cs], 0.0, ALU.mult, ALU.add)
                    rev = slice(ch * P + P - 1, ch * P - 1 if ch else None, -1)
                    ins = dve.tensor_tensor_scan(back[:, rev], ones[0:8, :], z[:, rev], 0.0, ALU.mult, ALU.add)
                step(ins)
                step(dve.tensor_scalar(ahead, ahead, small[0:8, FORWARD:FORWARD + 1], None, ALU.mult))
                dve.scalar_tensor_tensor(out=g_rows, in0=back, scalar=small[0:8, FORWARD + 1:FORWARD + 2], in1=ahead,
                                         op0=ALU.mult, op1=ALU.add).then_inc(rows_step, c.up("rows_step"))
                dve.wait_ge(row_exps, c.next("exps"))
                step(dve.reciprocal(stats[:, 32:64], stats[:, 0:32]))
                step(dve.tensor_scalar(stats[:, 32:48], stats[:, 32:48], float(P ** -0.5), None, ALU.mult))
                for i in range(8):
                    t = four(T[:, i] if i < 4 else ktok[:, i - 4])
                    dve.tensor_tensor(t, t, stats[:, 32 + 4 * i:36 + 4 * i, None].broadcast_to([P, 4, P]), ALU.mult).then_inc(kq_ready, c.up("kq"))
                dve.wait_ge(bc_full, 1)
                dve.tensor_copy(gcol.rearrange("p c r -> p (c r)"), ps[3][:, 0:32]).then_inc(row_terms, c.up("terms"))
                step(dve.tensor_copy(bcol.rearrange("p c r -> p (c r)"), ps[4][:, 0:64]))
                dve.wait_ge(row_exps, c.next("exps", 2))
                dve.tensor_tensor(beg, beg, bcol[:, :, 8:16], ALU.mult).then_inc(rows_step, c.up("rows_step"))
                dve.wait_ge(rows_step, c.now("rows_step"))
                dve.wait_ge(tab3_in, 16)
                for step_ in range(4):
                    for stage in range(STAGES):
                        for d in range(2):
                            lane_dve(d, step_, stage)
                for d in range(2):
                    dve.wait_ge(chunk_dve[d], c.now(f"cd{d}"))
                for r in range(4):
                    step(dve.tensor_tensor(T[:, 7], pt[:, AO + r], pt[:, AO + r], ALU.mult))
                    step(dve.tensor_reduce(stats[:, 4 * r:4 * r + 4], four(T[:, 7]), AX.X, ALU.add))
                dve.sem_inc(row_terms, c.up("terms"))
                dve.wait_ge(row_exps, c.next("exps"))
                step(dve.reciprocal(stats[:, 16:32], stats[:, 0:16]))
                for r in range(4):
                    o = four(pt[:, AO + r])
                    dve.tensor_tensor(o, o, stats[:, 16 + 4 * r:20 + 4 * r, None].broadcast_to([P, 4, P]), ALU.mult).then_inc(oT_done, c.up("oT_done"))
                for h in range(4):
                    dve.wait_ge(ut_full, UT_BEFORE + h + 1)
                    dve.scalar_tensor_tensor(out=hf, in0=ps[7][:, :], scalar=small[:, G_OUT:G_OUT + 1], in1=pt[:, DG + h],
                                             op0=ALU.mult, op1=ALU.mult).then_inc(h_done, c.up("h"))
                    dve.wait_ge(h_done, c.now("h"))
                    dve.sem_inc(ut_copied, 1)
                    lower(4 + h)
                    dve.wait_ge(m_ready, c.now("m"))

            def lane_dve(d, s, stage):
                ch = s if d == 0 else 3 - s
                cs = slice(ch * P, ch * P + P)
                nt, sd, xx, xt, a1, qg, st = (four(t) for t in LANE[d])
                b0, b1, b2 = (four(ps[2 + 3 * d + i][:, :]) for i in range(3))
                eye4 = ident[:, None, :].broadcast_to([P, 4, P])
                per_head = lambda v: v[:, :, None].broadcast_to([P, 4, P])

                def products():
                    dve.wait_ge(chunk_mm[d], c.next(f"mm{d}"))

                def ready(ins):
                    ins.then_inc(chunk_dve[d], c.up(f"cd{d}"))

                if stage == 0:
                    last = P - 1 if d == 0 else 0
                    products()
                    g = gcol[:, ch, 4 * d:4 * d + 4]
                    dve.tensor_tensor(kgf[d], b0[:, :, last], g, ALU.subtract)
                    dve.tensor_copy(glast[d], b0[:, :, last])
                    for h in range(4):
                        ins = dve.scalar_tensor_tensor(out=a1[:, h], in0=b0[:, h], scalar=g[:, h:h + 1], in1=incl_mask(d),
                                                       op0=ALU.subtract, op1=ALU.add)
                    ins.then_inc(chunk_terms[d], c.up(f"terms{d}"))
                    products()
                    dve.wait_ge(chunk_act[d], c.next(f"ca{d}"))
                    dve.tensor_tensor(sd, b2, a1, ALU.mult)
                    dve.tensor_tensor(qg, qg, pt[:, DQ:DQ + 4, cs], ALU.mult)
                    ready(dve.tensor_tensor(nt, b1, a1, ALU.mult))
                elif stage < 15:
                    m, half = divmod(stage - 1, 2)
                    products()
                    if half == 0:
                        for h in range(4):
                            ins = dve.scalar_tensor_tensor(out=a1[:, h], in0=b0[:, h], scalar=bcol[:, ch, 8 + 4 * d + h:9 + 4 * d + h],
                                                           in1=level_mask(d, m), op0=ALU.mult, op1=ALU.mult)
                        ready(ins)
                    elif m == 0:
                        dve.tensor_tensor(xx, eye4, a1, ALU.subtract)
                        ready(dve.tensor_tensor(xt, eye4, b2, ALU.subtract))
                    elif m < 6:
                        dve.tensor_tensor(xx, xx, b1, ALU.subtract)
                        ready(dve.tensor_tensor(xt, xt, b2, ALU.subtract))
                    else:
                        dve.tensor_tensor(nt, pt[:, DV:DV + 4, cs], per_head(bcol[:, ch, 8 + 4 * d:12 + 4 * d]), ALU.mult)
                        dve.tensor_tensor(a1, ktok[:, :, cs], per_head(beg[:, ch, 4 * d:4 * d + 4]), ALU.mult)
                        ready(dve.tensor_tensor(xt, xt, b2, ALU.subtract))
                elif stage == 15:
                    products()
                    c.up(f"ca{d}")
                elif stage == 16:
                    if s:
                        products()
                        dve.tensor_tensor(xx, xx, b2, ALU.subtract)
                    ready(dve.tensor_tensor(nt, ktok[:, :, cs], per_head(kgf[d]), ALU.mult))
                else:
                    products()
                    for h in range(4):
                        if s:
                            dve.scalar_tensor_tensor(out=st[:, h], in0=st[:, h], scalar=glast[d][:, h:h + 1], in1=b1[:, h],
                                                     op0=ALU.mult, op1=ALU.add)
                    if not s:
                        dve.tensor_copy(st, b1)
                    o = four(pt[:, AO + ch])
                    ready(dve.tensor_copy(o, b0) if s < 2 else dve.tensor_tensor(o, o, b0, ALU.add))

            def cross():
                for i in range(4):
                    dve.wait_ge(vm_full, c.next("vm_full"))
                    dve.tensor_copy(pt[:, 24 + i], ps[7][:, :]).then_inc(vm_done, c.up("vm_done"))
                for h in range(4):
                    for q2 in range(2):
                        dve.wait_ge(sc_full, c.next("sc_full"))
                        top, share = stats[:, 48:50], stats[:, 56:58]
                        step(dve.tensor_reduce(top, ps[2][:, :].rearrange("p (q n) -> p q n", q=2), AX.X, ALU.max, negate=True))
                        dve.tensor_scalar(top, top, 0.0625, None, ALU.mult).then_inc(max_done, c.up("max"))
                        dve.wait_ge(exp_done, c.next("exp"))
                        dve.sem_inc(sc_free, c.up("sc_free"))
                        step(dve.reciprocal(share, stats[:, 52:54]))
                        p = T[:, 0].rearrange("p (q n) -> p q n", q=2)
                        dve.tensor_tensor(p, p, share[:, :, None].broadcast_to([P, 2, 256]), ALU.mult).then_inc(prob_done, c.up("prob"))
                    for f in range(2):
                        dve.wait_ge(u_hi_done, c.next("u_hi"))
                        dve.tensor_tensor(tile(u_lo, 2 * h + f), ps[5 + f][:, :], tile(u_hi, 2 * h + f).bitcast(F32),
                                          ALU.subtract).then_inc(u_ready, c.up("u"))
                    dve.wait_ge(u_ready, c.now("u"))
                    dve.sem_inc(pv_copied, c.up("pv_copied"))

            dve.wait_ge(setup_in, 80)
            lam4 = lamv.rearrange("p (l m j) -> p l m j", l=2, m=2)
            dve.tensor_tensor(lamp.rearrange("p (l j) -> p l j", l=2), lam4[:, :, 0], lam4[:, :, 1], ALU.mult).then_inc(par_ready, 1)
            dve.wait_ge(loaded, 32)
            for k in range(KT):
                prepare(k, small[:, TAIL["g_first"] + k:TAIL["g_first"] + k + 1])
            dve.wait_ge(act_step, 1)
            for l in range(2):
                a = l * LC + LAYER_COLS["neg_lam"]
                step(dve.tensor_tensor(small[:, a:a + 1], stats[:, 2 * l + 1:2 * l + 2], stats[:, 2 * l:2 * l + 1], ALU.subtract))
                step(dve.tensor_tensor(small[:, a:a + 1], small[:, a:a + 1], small[:, a + 2:a + 3], ALU.subtract))
            for i in range(9):
                dve.wait_ge(vec_ready, i + 2)
                dve.tensor_copy(tab[:, i * S:i * S + S], ps[2 + i % 6][:, :]).then_inc(bias_made, 1)
            with c.loop(dve, LAYERS, PER["dve"]) as l:
                dve.wait_ge(u_ready, c.now("u"))
                step(dve.tensor_copy(par[:, :], small[:, ds(l * LC, LC)]))
                ffn(LAYER_COLS["g_mix"])
                mixers()
                ffn(LAYER_COLS["g_next"])
            second()




def arrays_of(i):
    jobs = []
    for l in range(LAYERS):
        jobs += ffn_jobs(i["w_ffn1_gate"][l], i["w_ffn1_up"][l], i["w_ffn1_down"][l])
        gate = i["w_gate"][l]
        a = [weight_jobs(gate[:, D * j:D * j + D]) for j in range(3)]
        jobs += [weight_jobs(i["w_in"][l]), np.zeros((1, P, D), np.float32)]
        jobs.append(np.stack([a[0], weight_jobs(i["w_br_a"][l])], 1).reshape(-1, P, D))
        jobs.append(weight_jobs(np.concatenate([i["w_br_b"][l], i["w_br_c"][l]])))
        jobs.append(np.stack([a[1], a[2]], 1).reshape(-1, P, D))
        jobs.append(weight_jobs(i["w_out"][l]))
        jobs += ffn_jobs(i["w_ffn2_gate"][l], i["w_ffn2_up"][l], i["w_ffn2_down"][l])
    w = i["w_in_2"][0]
    heads = w[:, :512].reshape(D, 2, 4, 64).transpose(0, 2, 1, 3).reshape(D, 512)
    few = np.concatenate([w[:, 2816:], np.zeros((D, 112), np.float32)], 1)
    jobs += [weight_jobs(heads), weight_jobs(w[:, 512:2816]), weight_jobs(few), np.zeros((1, P, D), np.float32)]
    jobs += [weight_jobs(i["w_out_2"][0]), weight_jobs(i["w_ckv_2"][0]), weight_jobs(i["w_cq_2"][0]), weight_jobs(i["w_co_2"][0])]
    jobs += ffn_jobs(i["w_gate_up_2"][0][:, :2816], i["w_gate_up_2"][0][:, 2816:], i["w_down_2"][0])
    small = np.zeros((P, NSMALL), np.float32)
    for l in range(2):
        cols = {"g_mix": i["g_mix"][l], "g_ffn2": i["g_ffn2"][l], "b_gate": i["b_gate"][l], "subln": i["subln_g"][l],
                "g_next": i["g_ffn1"][l + 1] if l + 1 < 2 else i["g_final"]}
        for n, v in cols.items():
            a = l * LC + LAYER_COLS[n]
            small[:, a:a + v.size // P] = column_major(v)
    for l in range(2):
        small[:, l * LC + LAYER_COLS["lam_init"]] = 0.8 - 0.6 * np.exp(-0.3 * l)
        small[:, l * LC + LAYER_COLS["one_less"]] = 0.2 + 0.6 * np.exp(-0.3 * l)
    tail = {"g_first": i["g_ffn1"][0]}
    for n in TAIL:
        if n != "g_first":
            tail[n] = i[n + "_2"][0]
    for n, v in tail.items():
        small[:, TAIL[n]:TAIL[n] + 8] = column_major(v)
    small[:, SINK:SINK + 8] = i["attn_sink_2"][0][None, :]
    small[:, CONV:CONV + 60] = i["conv_w_2"][0].reshape(5, DN_TILES, P).transpose(2, 1, 0).reshape(P, 60)
    small[:, G_OUT] = i["g_dn_out_2"][0]
    small[:8, A_LOG] = i["a_log_2"][0].reshape(8)
    small[:8, DT_BIAS] = i["dt_bias_2"][0].reshape(8)
    small[:, INV_FREQ] = np.tile(np.float32(10000.0) ** (-np.arange(32, dtype=np.float32) / np.float32(32)), 4)
    small[:4, FORWARD] = small[4:8, FORWARD + 1] = 1
    return {
        "jobs": np.concatenate(jobs),
        "x_in": np.ascontiguousarray(i["x"][0].T.reshape(KT, P, S).transpose(1, 0, 2)),
        "small_in": small,
        "mem_in": np.ascontiguousarray(i["mem_2"][0].T.reshape(KT, P, 256).transpose(1, 0, 2)),
        "pos_in": i["positions_2"],
        "rel_in": i["rel_bias"],
        "lam_in": np.stack([i[n][l] for l in range(2) for n in ("lam_q1", "lam_q2", "lam_k1", "lam_k2")], 1),
        **{n + "_in": v for n, v in constants().items()},
    }


def kernel(**inputs):
    import concourse.bacc as bacc
    from concourse.bass_utils import run_bass_kernel_spmd

    nc = bacc.Bacc("TRN2", target_bir_lowering=False, num_devices=1)
    arrays = arrays_of(inputs)
    aps = [nc.dram_tensor(n, a.shape, mybir.dt.from_np(a.dtype), kind="ExternalInput").ap() for n, a in arrays.items()]
    out = nc.dram_tensor("out", (P, KT, S), F32, kind="ExternalOutput").ap()
    build(nc, *aps, out)
    r = run_bass_kernel_spmd(nc, [arrays], core_ids=[0])
    y = r.results[0]["out"]
    return np.ascontiguousarray(y.transpose(1, 0, 2).reshape(D, S).T)[None]
```

```python
from contextlib import ExitStack, contextmanager

import numpy as np

import concourse.bass as bass
from concourse import mybir

F32 = mybir.dt.float32
F32R = mybir.dt.float32r
I32 = mybir.dt.int32
ALU = mybir.AluOpType
ACT = mybir.ActivationFunctionType
AX = mybir.AxisListType
ds = bass.ds

P = 128
S = 512
D = 1024
KT = D // P
LAYERS = 2
FF_PARTS = (8, 8, 6)
EPS = 1e-6


def tile(t, k, n=S):
    if isinstance(k, int):
        return t[:, k, 0:n]
    return t[:, ds(k, 1), 0:n].rearrange("p o n -> p (o n)")


class Count:

    def __init__(self, first, carrier=None):
        self.first = first
        self.carrier = carrier
        self.n = {}
        self.loops = []

    def now(self, key):
        value = self.n.get(key, self.first.get(key, 0))
        for reg, per in self.loops:
            if per.get(key, 0):
                value = reg * per[key] + value
        return value

    def up(self, key, by=1):
        self.n[key] = self.n.get(key, self.first.get(key, 0)) + by
        return by

    def next(self, key, by=1):
        self.up(key, by)
        return self.now(key)

    def take(self, key):
        value = self.now(key)
        self.up(key)
        return value

    @contextmanager
    def loop(self, eng, n, per):
        start = dict(self.n)
        if self.loops and self.carrier:
            eng.sem_inc(self.carrier, 1)
        with eng.Fori(0, n) as i:
            self.loops.append((i, per))
            yield i
            self.loops.pop()
        got = {k: v - start.get(k, self.first.get(k, 0)) for k, v in self.n.items()}
        got = {k: v for k, v in got.items() if v}
        assert got == {k: v for k, v in per.items() if v}, ("a loop's counts are", got, per)
        for k, v in got.items():
            self.n[k] += (n - 1) * v


LAYER_COLS = {"g_mix": 0, "g_ffn2": 8, "g_next": 16, "b_gate": 24, "subln": 48, "neg_lam": 49, "one_less": 50, "lam_init": 51}
LC = 52
TAIL = {n: 2 * LC + 8 * i for i, n in enumerate(
    ["g_first", "g_mix_pre", "g_mix_post", "g_cross_pre", "g_mem", "g_cross_post", "g_ffn_pre", "g_ffn_post"])}
EXTRA = 2 * LC + 8 * len(TAIL)
SINK, CONV, G_OUT, A_LOG, DT_BIAS, INV_FREQ, FORWARD, NSMALL = (EXTRA + n for n in (0, 8, 68, 69, 70, 71, 72, 74))
DN_TILES = 12
ROUND = 1.5 * 2 ** 23
NEAR_PI = 3.1415925
UT_BEFORE = 7 * LAYERS + 4
TWO_PI = (6.28125, 1.93500518798828125e-3, 3.0199159819567e-7)


HALF = S // 2 + 1
DFT_COLS = 2 * P + 2 * 4 * HALF
BIAS_N = [896] * 4 + [256] * 2 + [128] * 4
BIAS_AT = [sum(BIAS_N[:i]) for i in range(10)]
BIAS_COLS = sum(BIAS_N)
VEC = {0: (0, 1024), 1: (1024, 384), 2: (1408, 256), 3: (1664, 256)}
VEC_COLS = 1920
HEAD_OF = [6, 7, 8, 9, 0, 1, 2, 3, 4, 5]
KIND_OF = [0, 0, 0, 0, 1, 1, 2, 2, 3, 3]


PER = {
    "pe": {
        "u": 24, "lo0": 107, "evac0": 107, "acc": 24, "stat": 3, "job0": 107, "lo1": 107, "evac1": 107, "job1": 107, "m": 65,
        "vt_done": 7, "vt_full": 7, "sc_free": 22, "sc_full": 22, "exp": 22, "tr_copied": 22, "tr_full": 22, "pv_copied": 19,
        "pv_full": 19, "ut_copied": 7, "ut_full": 7, "total": 6, "rows_copied": 6, "rows_full": 6, "tab": 176, "z_act": 8,
        "z_full": 16, "z_dve": 8, "y_done": 8, "pq": 8, "mixw": 1, "wb_free": 3, "wb_full": 3, "prob": 16, "oT_done": 4,
    },
    "act": {
        "square": 24, "u_hi": 24, "raw0": 1712, "slot0": 107, "raw1": 1712, "slot1": 107, "stat": 3, "std": 4, "evac0": 107,
        "silu": 68, "job0": 107, "h": 61, "m_hi": 65, "job1": 107, "evac1": 107, "m": 65, "tab": 176, "max": 23, "exp": 22,
        "tr_full": 22, "tr_copied": 22, "pv_full": 19, "pv_copied": 19, "ut_full": 7, "ut_copied": 7, "rows_full": 6,
        "rows_copied": 6, "z_full": 16, "z_act": 8, "pq": 8, "q_copied": 8, "mixw": 1,
    },
    "dve": {
        "dve": 95, "square": 24, "acc": 24, "u_hi": 24, "u": 24, "std": 4, "job0": 107, "evac0": 107, "job1": 107,
        "evac1": 107, "silu": 68, "h": 61, "m_hi": 65, "m": 65, "tab": 176, "vt_full": 7, "vt_done": 7, "sc_full": 22,
        "sc_free": 22, "max": 23, "exp": 22, "total": 6, "tr_full": 22, "z_full": 16, "z_dve": 8, "q_copied": 8, "pq": 8,
        "y_done": 8, "rows": 6, "mixe": 1, "mixw": 1, "wb_full": 3, "wb_free": 3, "prob": 16, "oT_done": 4, "pv_full": 19,
    },
}


def bucket(rel):
    n = np.abs(rel)
    far = np.floor(8 + np.log(np.maximum(n, 1) / 8) / np.log(1024 / 8) * 8).astype(int)
    return np.where(rel > 0, 16, 0) + np.where(n < 8, n, np.minimum(far, 15))


def constants():
    c = {}
    k, n = np.arange(P), np.arange(S)
    a = 2 * np.pi * (k[:, None] * k[None, :] % P) / P
    t = 2 * np.pi * (n[:, None] * np.arange(HALF)[None, :] % S) / S
    tok = lambda m: m.reshape(4, P, HALF).transpose(1, 0, 2).reshape(P, -1)
    c["dft"] = np.concatenate([np.cos(a) / 256, np.sin(a) / 256, tok(np.cos(t)), tok(np.sin(t))], 1)
    hot = np.zeros((33, VEC_COLS))
    for kind, (at, size) in VEC.items():
        i = np.arange(size)
        rel, ok = ((i - 511, i < 1023), (i - 191, abs(i - 191) <= 64), (4 * (i - 127), abs(i - 127) <= 64),
                   (4 * (i - 127), (i - 127) % 4 == 0))[kind]
        hot[bucket(rel), at + i] = ok
        hot[32, at + i] = np.where(ok, 0, -1e30)
    for at, size in VEC.values():
        hot[:, at:at + size] = hot[:, at:at + size][:, ::-1].copy()
    c["hot"] = hot
    c["eye"] = np.eye(P)
    sel = np.zeros((2, P))
    sel[0, :64] = sel[1, 64:] = 1
    c["sel"] = sel
    w = np.arange(3 * P)
    c["window"] = np.where(abs(w[None, :] - P - k[:, None]) <= P, 0, -1e30)
    i, j = k[:, None], k[None, :]
    incl = np.where(j >= i, 0, -1e30)
    level = [(i // (2 * b) == j // (2 * b)) & (i % (2 * b) >= b) & (j % (2 * b) < b) for b in (1, 2, 4, 8, 16, 32, 64)]
    c["chunk"] = np.concatenate(level + [m.T for m in level] + [incl, incl.T], 1)
    swap = np.zeros((P, P))
    for m in range(P):
        swap[m + 32 if m % 64 < 32 else m - 32, m] = -1 if m % 64 < 32 else 1
    c["swap"] = swap
    rows = np.zeros((8, 8 * P))
    for r in range(8):
        rows[r, r * P:r * P + P] = 1
    c["rows8"] = rows
    return {n: v.astype(np.float32) for n, v in c.items()}


def column_major(v):
    return v.reshape(-1, P).T


def weight_jobs(w):
    k, m = w.shape
    out = np.zeros((m // P, P, KT * P), np.float32)
    out[:, :, :k] = w.reshape(k // P, P, m // P, P).transpose(2, 1, 0, 3).reshape(m // P, P, k)
    return out


def ffn_jobs(gate, up, down):
    out, f0 = [], 0
    for n in FF_PARTS:
        cols = slice(f0 * P, (f0 + n) * P)
        pair = np.stack([weight_jobs(gate[:, cols]), weight_jobs(up[:, cols])], 1)
        out += [pair.reshape(-1, P, D), weight_jobs(down[cols])]
        f0 += n
    return out


def build(nc, jobs, x_in, small_in, mem_in, pos_in, rel_in, lam_in, dft_in, hot_in, eye_in, sel_in,
          window_in, chunk_in, swap_in, rows8_in, out):
    NJ = jobs.shape[0]
    with ExitStack() as ctx:
        def sb(name, shape, dt=F32):
            return ctx.enter_context(nc.sbuf_tensor(name, shape, dt))

        def sem(name):
            return ctx.enter_context(nc.semaphore(name))

        raw = sb("raw", [P, 2, KT * P])
        w_hi = sb("w_hi", [P, 2, KT * P], F32R)
        w_lo = sb("w_lo", [P, 2, KT * P], F32R)
        x = sb("x", [P, KT, S])
        u_hi = sb("u_hi", [P, KT, S], F32R)
        u_lo = sb("u_lo", [P, KT, S], F32R)
        m_hi = sb("m_hi", [P, KT, S], F32R)
        m_lo = sb("m_lo", [P, KT, S], F32R)
        T = sb("T", [P, 8, S])
        gr, sg, ur, hf, xsq, acc, std = (T[:, i] for i in range(7))
        rs = sb("rs", [P, S])
        ones = sb("ones", [P, P])
        pt = sb("pt", [P, 30, S])
        tab = sb("tab", [P, BIAS_COLS])
        eye = sb("eye", [P, P])
        stats = sb("stats", [P, 416])
        rs_mem = sb("rs_mem", [P, 256])
        sel = sb("sel", [2, P])
        vec_dram = nc.dram_tensor("vec_dram", (10, VEC_COLS), F32, kind="Internal").ap()
        small = sb("small", [P, NSMALL])
        par = sb("par", [P, LC])
        eps = sb("eps", [P, 3])
        ps = [ctx.enter_context(nc.psum_tensor(f"ps{i}", [P, S], F32)) for i in range(8)]

        x_in_part = [sem(f"x_in_part{i}") for i in range(4)]
        raw_full = [sem(f"raw_full{i}") for i in range(2)]
        hi_done = [sem(f"hi_done{i}") for i in range(2)]
        lo_done = [sem(f"lo_done{i}") for i in range(2)]
        job_done = [sem(f"job_done{i}") for i in range(2)]
        evac = [sem(f"evac{i}") for i in range(2)]
        names = """loaded setup_in mixer_in mem_loaded tile_squared par_ready vec_ready vec_stored tab_full
            silu_done h_done m_hi_done m_ready square_done acc_step u_hi_done u_ready stat_done std_done
            dve_step act_step out_done z_full z_act z_dve pq_full q_copied y_done vt_full vt_done sc_full sc_free
            max_done exp_done prob_done tr_full tr_copied pv_full pv_copied ut_full ut_copied
            rows_full rows_copied mixw_exp mixw_done wb_full wb_free oT_done total_done
            x_done tab2_in rope_full rope_done conv_done conv_silu rows_step kq_ready bc_full chunk_mm0 chunk_mm1
            angles_ready tables_ready tab3_in row_terms row_exps chunk_terms0 chunk_terms1
            chunk_dve0 chunk_dve1 chunk_act0 chunk_act1 dn_full dn_copied vm_full vm_done inner_loops"""
        (loaded, setup_in, mixer_in, mem_loaded, tile_squared, par_ready, vec_ready, vec_stored, tab_full,
         silu_done, h_done, m_hi_done, m_ready, square_done, acc_step, u_hi_done, u_ready, stat_done, std_done,
         dve_step, act_step, out_done, z_full, z_act, z_dve, pq_full, q_copied, y_done, vt_full, vt_done, sc_full, sc_free,
         max_done, exp_done, prob_done, tr_full, tr_copied, pv_full, pv_copied, ut_full, ut_copied,
         rows_full, rows_copied, mixw_exp, mixw_done, wb_full, wb_free, oT_done, total_done,
         x_done, tab2_in, rope_full, rope_done, conv_done, conv_silu, rows_step, kq_ready, bc_full, chunk_mm0, chunk_mm1,
         angles_ready, tables_ready, tab3_in, row_terms, row_exps, chunk_terms0, chunk_terms1,
         chunk_dve0, chunk_dve1, chunk_act0, chunk_act1, dn_full, dn_copied, vm_full, vm_done, inner_loops) = [sem(n) for n in names.split()]
        FIRST = {k + str(i): 1 for k in ("job", "slot", "evac", "lo") for i in range(2)}
        FIRST |= {k: 1 for k in ("z_act", "z_dve", "q_copied", "y_done", "vt_done", "sc_free", "tr_copied", "pv_copied",
                                 "ut_copied", "wb_free", "oT_done", "rope_done", "vm_done")}
        FIRST |= {"dn_copied": 2, "rows_copied": 2}
        JOB = {f"{k}{s}": 1 for k in ("job", "evac") for s in range(2)}
        PJOB = {**JOB, "lo0": 1, "lo1": 1}
        AJOB = {**JOB, "raw0": 16, "raw1": 16, "slot0": 1, "slot1": 1}
        flat = pt[:, :, :].rearrange("p a n -> p (a n)")
        ident = eye[:, 0:P]
        QB, KB, VB, QC, KC, VC = 8, 11, 14, 17, 21, 25
        OC = 8
        MIX = 12
        YB, YC = 8, 16
        dft_c, dft_s = tab[:, 0:P], tab[:, P:2 * P]
        dft_cs = tab[:, 0:2 * P]
        cos_t = tab[:, 2 * P:2 * P + 4 * HALF].rearrange("p (t n) -> p t n", t=4)
        sin_t = tab[:, 2 * P + 4 * HALF:DFT_COLS].rearrange("p (t n) -> p t n", t=4)
        nmax = stats[:, 0:24].rearrange("p (g t h) -> p g t h", g=3, t=4)
        total = stats[:, 24:48].rearrange("p (g t h) -> p g t h", g=3, t=4)
        rows_m = flat[0:2, KB * S:(KB + 3) * S].rearrange("p (g n) -> p g n", g=3)
        rows_z = flat[0:2, VB * S:(VB + 3) * S].rearrange("p (g n) -> p g n", g=3)
        hot = flat[0:33, 0:VEC_COLS]
        relb = pt[0:33, 4, 0:10]
        lamv = pt[0:64, 5, 0:8]
        lamp = pt[0:64, 6, 0:4]
        vec_sb = flat[0:10, 18 * S:18 * S + VEC_COLS]

        def bias_of(i, first, n):
            start = BIAS_AT[i] + BIAS_N[i] - 1 - first
            return tab[:, start:start - n if start >= n else None:-1]

        def tokens(r, row):
            return row.rearrange("p (i c) -> p c i", c=4)[:, r]

        def natural(g, row):
            return row if g == 0 else row.rearrange("p (i c) -> p c i", c=4)

        def grouped(g, row):
            return row if g == 0 else row.rearrange("p (c i) -> p c i", c=4)

        AQ, AK, AV, DQ, DK, DV, DG, AB, AO = 0, 4, 5, 6, 10, 14, 18, 22, 24
        tabt = tab[:, :].rearrange("p (a n) -> p a n", n=S)
        memt = tabt[:, 0:4].rearrange("p a n -> p (a n)").rearrange("p (k n) -> p k n", k=KT)
        cos, sin = tabt[:, 4], tabt[:, 5]
        pos_i = tabt[:, 6].bitcast(I32)
        window = tabt[:, 7, 0:3 * P]
        swap = tabt[:, 8, 0:P]
        ktok = tabt[:, 0:4]
        chunk = tabt[:, 4:8].rearrange("p a n -> p (a n)")
        rows8 = pt[0:8, 28:30].rearrange("p a n -> p (a n)")
        neg_sink = stats[:, 400:408]
        gcol = stats[:, 96:128].rearrange("p (c r) -> p c r", c=4)
        bcol = stats[:, 128:160].rearrange("p (c r) -> p c r", c=4)
        beg = stats[:, 192:224].rearrange("p (c r) -> p c r", c=4)
        kgf = [stats[:, 224 + 8 * d:228 + 8 * d] for d in range(2)]
        glast = [stats[:, 228 + 8 * d:232 + 8 * d] for d in range(2)]
        LANE = [[T[:, i] for i in range(7)], [pt[:, i] for i in range(6)] + [pt[:, 23]]]
        chunk_terms = (chunk_terms0, chunk_terms1)
        chunk_mm, chunk_dve, chunk_act = (chunk_mm0, chunk_mm1), (chunk_dve0, chunk_dve1), (chunk_act0, chunk_act1)

        mem_sum = T[:, 7, 0:256]
        beta_rows = T[0:8, 7]
        g_rows = pt[0:8, AB]
        STAGES = 18
        X_DONE = 3 * KT

        def vm(f, t):
            i, j = f // 2, (f % 2) * 2 + t
            return pt[:, 24 + i, j * P:j * P + P]

        def lane_stages():
            for i in range(4 * STAGES):
                for d in range(2):
                    yield d, i // STAGES, i % STAGES

        def window_keys(r):
            return (min(r + 2, 4) - max(r - 1, 0)) * P

        def four(t):
            return t.rearrange("p (h n) -> p h n", h=4)

        def level_mask(d, m):
            return chunk[:, (7 * d + m) * P:(7 * d + m) * P + P]

        def incl_mask(d):
            return chunk[:, (14 + d) * P:(15 + d) * P]

        block = ctx.enter_context(nc.Block())

        @block.sync
        def _(sp):
            sp.dma_start(small[:, :], small_in).then_inc(loaded, 16)
            for i in range(4):
                sp.dma_start(x[:, 2 * i:2 * i + 2], x_in[:, 2 * i:2 * i + 2]).then_inc(x_in_part[i], 16)
            with sp.Fori(0, NJ // 2) as i:
                for s in range(2):
                    sp.wait_ge(lo_done[s], i + 1)
                    sp.dma_start(raw[:, s], jobs[ds(i * 2 + s, 1)].rearrange("o p n -> p (o n)")).then_inc(raw_full[s], 16)
            if NJ % 2:
                sp.wait_ge(lo_done[0], NJ // 2 + 1)
                sp.dma_start(raw[:, 0], jobs[NJ - 1]).then_inc(raw_full[0], 16)
            for k in range(KT):
                sp.wait_ge(x_done, X_DONE + k + 1)
                sp.dma_start(out[:, k], x[:, k]).then_inc(out_done, 16)
            sp.wait_ge(out_done, 16 * KT)

        @block.gpsimd
        def _(pool):
            for s in range(2):
                pool.sem_inc(lo_done[s], 1)
            with pool.Fori(0, NJ // 2) as i:
                for s in range(2):
                    pool.wait_ge(hi_done[s], i + 1)
                    pool.tensor_tensor(w_lo[:, s], raw[:, s], w_hi[:, s].bitcast(F32), ALU.subtract).then_inc(lo_done[s], 1)
            if NJ % 2:
                pool.wait_ge(hi_done[0], NJ // 2 + 1)
                pool.tensor_tensor(w_lo[:, 0], raw[:, 0], w_hi[:, 0].bitcast(F32), ALU.subtract).then_inc(lo_done[0], 1)

        @block.tensor
        def _(pe):
            c = Count(FIRST)
            for s in range(2):
                pe.sem_inc(job_done[s], 1)

            def job(s, hi, lo, ks=range(KT), ready=None, n=S, stat=False):
                pe.wait_ge(lo_done[s], c.next(f"lo{s}"))
                pe.wait_ge(evac[s], c.take(f"evac{s}"))
                product(s, s, hi, lo, ks, ready, n, stat).then_inc(job_done[s], c.up(f"job{s}"))

            def product(s, bank, hi, lo, ks, ready=None, n=S, stat=False):
                for k in ks:
                    if ready:
                        pe.wait_ge(ready[0], ready[1] + (k + 1))
                    w = slice(k * P, k * P + P)
                    pe.matmul(ps[bank][:, 0:n], w_hi[:, s, w], hi[:, k, 0:n], start=k == ks[0], stop=False)
                    pe.matmul(ps[bank][:, 0:n], w_lo[:, s, w], hi[:, k, 0:n], start=False, stop=False)
                    last = pe.matmul(ps[bank][:, 0:n], w_hi[:, s, w], lo[:, k, 0:n], start=False, stop=k == ks[-1])
                    if stat == "tiles":
                        pe.wait_ge(tile_squared, c.next("tile_squared"))
                        mm = pe.matmul(ps[7][:, :], ones[:, :], T[:, k], start=k == 0, stop=k == KT - 1)
                        if k == KT - 1:
                            mm.then_inc(stat_done, c.up("stat"))
                    elif stat and k == 3:
                        statistic(n)
                return last

            def statistic(n=S, squares=acc):
                pe.wait_ge(acc_step, c.next("acc", 8))
                pe.matmul(ps[7][:, 0:n], ones[:, :], squares[:, 0:n], start=True, stop=True).then_inc(stat_done, c.up("stat"))

            def ffn(stat=True):
                ready = (u_ready, c.now("u"))
                c.up("u", 8)
                for part, n in enumerate(FF_PARTS):
                    if part == 0:
                        job(0, u_hi, u_lo, ready=ready, stat=stat)
                        job(1, u_hi, u_lo)
                    with c.loop(pe, n - (part == 0), PJOB):
                        job(0, u_hi, u_lo)
                        job(1, u_hi, u_lo)
                    with c.loop(pe, 4, PJOB):
                        job(0, m_hi, m_lo, range(n), ready=(m_ready, c.now("m")))
                        job(1, m_hi, m_lo, range(n))
                    c.up("m", n)

            def fourier():
                def along_channels(g):
                    for half in range(2):
                        free = z_act if half == 0 else z_dve
                        pe.wait_ge(free, c.take("z_act" if half == 0 else "z_dve"))
                        for t in (2 * half, 2 * half + 1):
                            mm = pe.matmul(ps[2 + half][:, (t % 2) * 256:(t % 2) * 256 + 256], pt[:, g, t * P:t * P + P],
                                           dft_cs, start=True, stop=True)
                        mm.then_inc(z_full, c.up("z_full"))

                pe.wait_ge(tab_full, c.next("tab", 128))
                c.up("tab", 48)
                along_channels(0)
                for g in range(8):
                    if g < 7:
                        along_channels(g + 1)
                    if 1 <= g <= 4:
                        pe.wait_ge(vt_done, c.take("vt_done"))
                        for r in range(4):
                            mm = pe.transpose(ps[6][:, r * P:r * P + P], pt[:, VC + g - 1, r * P:r * P + P], ident)
                        mm.then_inc(vt_full, c.up("vt_full"))
                    z = T[:, 2 * (g % 2):2 * (g % 2) + 2].rearrange("p a n -> p (a n)").rearrange("p (t n) -> p t n", t=4)
                    pe.wait_ge(z_act, c.now("z_act") - (1 if g < 7 else 0))
                    pe.wait_ge(z_dve, c.now("z_dve") - (1 if g < 7 else 0))
                    pe.wait_ge(y_done, c.take("y_done"))
                    for t in range(4):
                        pe.matmul(ps[4][:, 0:HALF], z[:, t, 0:P], cos_t[:, t], start=t == 0, stop=t == 3)
                    for t in range(4):
                        mm = pe.matmul(ps[5][:, 0:HALF], z[:, t, P:2 * P], sin_t[:, t], start=t == 0, stop=t == 3)
                    mm.then_inc(pq_full, c.up("pq"))

            def v_tiles(g):
                pe.wait_ge(vt_done, c.take("vt_done"))
                for r in range(4):
                    src = flat[:, (VB * S - 64 + r * P):(VB * S + 64 + r * P)] if g == 0 else tokens(r, pt[:, VB + g])
                    mm = pe.transpose(ps[5][:, r * P:r * P + P], src, ident)
                if g == 0:
                    mm = pe.transpose(ps[6][:, 0:P], flat[:, VB * S + 448:VB * S + 576], ident)
                mm.then_inc(vt_full, c.up("vt_full"))

            def dilated(g):
                v_tiles(g)
                v = pt[:, VB + g].rearrange("p (t n) -> p t n", t=4)
                for h in range(2):
                    hp = slice(64 * h, 64 * h + 64)
                    pe.wait_ge(sc_free, c.take("sc_free"))
                    for r in range(4):
                        q, k = pt[hp, QB + g], pt[hp, KB + g]
                        if g == 0:
                            a, b = max(r * P - 64, 0), min(r * P + 192, S)
                            o = (r % 2) * 256 + a - (r * P - 64)
                            mm = pe.matmul(ps[2 + r // 2][:, o:o + b - a], q[:, r * P:r * P + P], k[:, a:b], start=True, stop=True)
                        else:
                            mm = pe.matmul(ps[2][:, r * P:r * P + P], tokens(r, q), tokens(r, k), start=True, stop=True)
                    mm.then_inc(sc_full, c.up("sc_full"))
                    job(0, u_hi, u_lo)
                    pe.wait_ge(exp_done, c.next("exp"))
                    pe.wait_ge(tr_copied, c.take("tr_copied"))
                    e = T[:, 0:2].rearrange("p a n -> p (a n)")
                    if g == 0:
                        for r in range(4):
                            for half in range(2):
                                a = r * 256 + half * P
                                mm = pe.transpose(ps[(4, 6)[half]][:, r * P:r * P + P], e[:, a:a + P], ident)
                    else:
                        for r in range(4):
                            mm = pe.transpose(ps[4][:, r * P:r * P + P], e[:, r * P:r * P + P], ident)
                    mm.then_inc(tr_full, c.up("tr_full"))
                    job(1, u_hi, u_lo, range(1) if (g, h) == (2, 1) else range(KT))
                    pe.wait_ge(tr_copied, c.now("tr_copied"))
                    if h == 0:
                        pe.wait_ge(vt_done, c.now("vt_done"))
                        pe.wait_ge(pv_copied, c.take("pv_copied"))
                    for r in range(4):
                        o = ps[5][:, r * P + 64 * h:r * P + 64 * h + 64]
                        vh = slice(64 * h, 64 * h + 64)
                        if g == 0:
                            after = v[:, r + 1, vh] if r < 3 else pt[:, 29, vh]
                            pe.matmul(o, T[:, 2, r * P:r * P + P], v[:, r, vh], start=True, stop=False)
                            mm = pe.matmul(o, T[:, 3, r * P:r * P + P], after, start=False, stop=True)
                        else:
                            mm = pe.matmul(o, T[:, 2, r * P:r * P + P], v[:, r, vh], start=True, stop=True)
                mm.then_inc(pv_full, c.up("pv_full"))
                pe.wait_ge(pv_copied, c.now("pv_copied"))
                pe.wait_ge(ut_copied, c.take("ut_copied"))
                for r in range(4):
                    mm = pe.transpose(ps[7][:, r * P:r * P + P], T[:, 4, r * P:r * P + P], ident)
                mm.then_inc(ut_full, c.up("ut_full"))

            def dilated_rows():
                pe.wait_ge(total_done, c.next("total", 6))
                for stat_of in (nmax, total):
                    for g in range(3):
                        pe.wait_ge(rows_copied, c.take("rows_copied") - 1)
                        for r in range(4):
                            mm = pe.transpose(ps[2 + (g + (stat_of is total)) % 2][0:2, r * P:r * P + P], stat_of[:, g, r], ident)
                        mm.then_inc(rows_full, c.up("rows_full"))

            def mix_groups(first_scores):
                pe.wait_ge(mixw_done, c.next("mixw"))
                for g in range(3):
                    pe.wait_ge(wb_free, c.take("wb_free"))
                    pe.matmul(ps[7][:, :], sel[:, :], rows_m[:, g], start=True, stop=True).then_inc(wb_full, c.up("wb_full"))
                    if g == 0:
                        first_scores()

            def dense():
                c.up("exp", 16)

                def scores(u):
                    h, r = 3 - u // 4, u % 4
                    pe.wait_ge(sc_free, c.take("sc_free"))
                    for m in range(2):
                        hp = slice(64 * m, 64 * m + 64)
                        mm = pe.matmul(ps[2 + m][:, :], pt[hp, QC + h, r * P:r * P + P], pt[hp, KC + h], start=True, stop=True)
                    mm.then_inc(sc_full, c.up("sc_full"))

                mix_groups(lambda: scores(0))
                pe.wait_ge(vt_done, c.now("vt_done"))
                scores(1)
                for u in range(16):
                    if u < 14:
                        scores(u + 2)
                    h = 3 - u // 4
                    pe.wait_ge(prob_done, c.next("prob"))
                    pe.wait_ge(tr_copied, c.take("tr_copied"))
                    for k in range(4):
                        mm = pe.transpose(ps[4][:, k * P:k * P + P], T[:, 2 * (u % 2) + 1, k * P:k * P + P], ident)
                    mm.then_inc(tr_full, c.up("tr_full"))
                    pe.wait_ge(tr_copied, c.now("tr_copied"))
                    pe.wait_ge(pv_copied, c.take("pv_copied"))
                    v = pt[:, VC + h].rearrange("p (t n) -> p t n", t=4)
                    for k in range(4):
                        mm = pe.matmul(ps[5][:, 0:P], T[:, 4 + u % 2, k * P:k * P + P], v[:, k], start=k == 0, stop=k == 3)
                    mm.then_inc(pv_full, c.up("pv_full"))
                    if u % 2 == 0:
                        job(0, u_hi, u_lo)
                    else:
                        job(1, m_hi, m_lo, ready=(m_ready, c.now("m")) if u == 1 else None)
                c.up("m", 8)
                job(0, u_hi, u_lo)
                job(1, u_hi, u_lo)
                for h in range(4):
                    if h == 0:
                        pe.wait_ge(oT_done, c.now("oT_done") + 4)
                        c.up("oT_done", 4)
                    pe.wait_ge(ut_copied, c.take("ut_copied"))
                    for r in range(4):
                        mm = pe.transpose(ps[7][:, r * P:r * P + P], pt[:, OC + h, r * P:r * P + P], ident)
                    mm.then_inc(ut_full, c.up("ut_full"))

            def mixers():
                ready = (u_ready, c.now("u"))
                c.up("u", 8)
                job(0, u_hi, u_lo, ready=ready, stat=True)
                job(1, u_hi, u_lo)
                with c.loop(pe, 8, PJOB):
                    job(0, u_hi, u_lo)
                    job(1, u_hi, u_lo)
                pe.wait_ge(evac[0], c.now("evac0"))
                pe.wait_ge(evac[1], c.now("evac1"))
                pe.wait_ge(act_step, 2)
                for g in range(3):
                    dilated(g)
                dilated_rows()
                pe.wait_ge(evac[0], c.now("evac0"))
                pe.wait_ge(evac[1], c.now("evac1"))
                pe.wait_ge(rows_copied, c.now("rows_copied"))
                fourier()
                pe.wait_ge(y_done, c.now("y_done"))
                dense()
                with c.loop(pe, 4, PJOB):
                    for s in range(2):
                        pe.wait_ge(lo_done[s], c.next(f"lo{s}"))
                        pe.wait_ge(evac[s], c.take(f"evac{s}"))
                        if s == 0:
                            pe.wait_ge(m_ready, c.now("m") + 5)
                        product(s, 2 + s, m_hi, m_lo, range(1))
                        product(s, s, m_hi, m_lo, range(1, 5)).then_inc(job_done[s], c.up(f"job{s}"))
                c.up("m", 5)
                with c.loop(pe, 7, PJOB):
                    job(0, u_hi, u_lo)
                    job(1, u_hi, u_lo)
                with c.loop(pe, 4, PJOB):
                    job(0, m_hi, m_lo, ready=(m_ready, c.now("m")))
                    job(1, m_hi, m_lo)
                c.up("m", 8)

            def second():
                c.up("u", 8)
                statistic()
                ready = (u_ready, c.now("u"))
                c.up("u", 8)
                job(0, u_hi, u_lo, ready=ready, stat="tiles")
                job(1, u_hi, u_lo)
                with c.loop(pe, 2, PJOB):
                    job(0, u_hi, u_lo)
                    job(1, u_hi, u_lo)
                for s in range(2):
                    pe.wait_ge(evac[s], c.now(f"evac{s}"))
                window_attention()
                for s in range(2):
                    pe.wait_ge(evac[s], c.now(f"evac{s}"))
                delta_net()
                m0 = c.now("m")
                c.up("m", 8)
                job(0, m_hi, m_lo, ready=(m_ready, m0))
                statistic(256, mem_sum)
                job(1, m_hi, m_lo)
                with c.loop(pe, 3, PJOB):
                    job(0, m_hi, m_lo)
                    job(1, m_hi, m_lo)
                pe.wait_ge(u_ready, c.next("u", 8))
                job(0, u_hi, u_lo, n=256)
                job(1, u_hi, u_lo, n=256)
                statistic()
                with c.loop(pe, 7, PJOB):
                    job(0, u_hi, u_lo, n=256)
                    job(1, u_hi, u_lo, n=256)
                m0 = c.now("m")
                c.up("m", 8)
                for s in range(2):
                    pe.wait_ge(evac[s], c.now(f"evac{s}"))
                memory_values()
                job(0, m_hi, m_lo, ready=(m_ready, m0), stat=True)
                job(1, m_hi, m_lo)
                cross()
                u0 = c.now("u")
                c.up("u", 8)
                job(0, u_hi, u_lo, ready=(u_ready, u0))
                job(1, u_hi, u_lo)
                with c.loop(pe, 3, PJOB):
                    job(0, u_hi, u_lo)
                    job(1, u_hi, u_lo)
                statistic()
                ffn("tiles")
                statistic()

            def window_attention():
                pe.wait_ge(tab2_in, 64)
                for i in range(5):
                    pe.wait_ge(rope_done, c.take("rope_done"))
                    pe.matmul(ps[2][:, :], swap, pt[:, i], start=True, stop=True).then_inc(rope_full, c.up("rope_full"))
                    if i in (0, 2):
                        job(i // 2, u_hi, u_lo)
                pe.wait_ge(vt_done, c.take("vt_done"))
                for r in range(4):
                    mm = pe.transpose(ps[6][:, r * P:r * P + P], pt[:, AV, r * P:r * P + P], ident)
                mm.then_inc(vt_full, c.up("vt_full"))
                pe.wait_ge(vt_done, c.now("vt_done"))
                pe.wait_ge(rope_done, c.now("rope_done"))
                v = four(pt[:, AV])

                def scores(u):
                    j, r = divmod(u, 4)
                    pe.wait_ge(sc_free, c.take("sc_free"))
                    lo, hi = max(r - 1, 0) * P, min(r + 2, 4) * P
                    for m in range(2):
                        hp = slice(64 * m, 64 * m + 64)
                        mm = pe.matmul(ps[2 + m][:, 0:hi - lo], pt[hp, AQ + j, r * P:r * P + P], pt[hp, AK, lo:hi], start=True, stop=True)
                    mm.then_inc(sc_full, c.up("sc_full"))

                scores(0)
                scores(1)
                for u in range(16):
                    if u < 14:
                        scores(u + 2)
                    r = u % 4
                    keys = range(max(r - 1, 0), min(r + 2, 4))
                    pe.wait_ge(exp_done, c.next("exp"))
                    pe.wait_ge(tr_copied, c.take("tr_copied"))
                    for m in range(2):
                        for n in range(len(keys)):
                            mm = pe.transpose(ps[4 + 2 * m][:, n * P:n * P + P], T[:, 2 * (u % 2) + m, n * P:n * P + P], ident)
                    mm.then_inc(tr_full, c.up("tr_full"))
                    pe.wait_ge(tr_copied, c.now("tr_copied"))
                    pe.wait_ge(pv_copied, c.take("pv_copied"))
                    for m in range(2):
                        for n, k in enumerate(keys):
                            mm = pe.matmul(ps[5][:, 64 * m:64 * m + 64], T[:, 4 + m, n * P:n * P + P], v[:, k, 64 * m:64 * m + 64],
                                           start=n == 0, stop=n == len(keys) - 1)
                    mm.then_inc(pv_full, c.up("pv_full"))
                    job(u % 2, u_hi, u_lo, range(1) if u == 15 else range(KT))
                free = c.now("ut_copied")
                c.up("ut_copied", 4)
                for f in range(4):
                    if f != 1:
                        pe.wait_ge(ut_copied, free + max(f - 1, 0))
                    if f == 0:
                        pe.wait_ge(pv_copied, c.now("pv_copied"))
                    for r in range(4):
                        mm = pe.transpose(ps[7 - f % 2][:, r * P:r * P + P], pt[:, AO + r, f * P:f * P + P], ident)
                    mm.then_inc(ut_full, c.up("ut_full"))

            def delta_net():
                for i in range(8):
                    pe.wait_ge(conv_silu, c.next("conv"))
                    pe.wait_ge(dn_copied, c.take("dn_copied") - 1)
                    for r in range(4):
                        mm = pe.transpose(ps[2 + i % 2][:, r * P:r * P + P], pt[:, DQ + i, r * P:r * P + P], ident)
                    mm.then_inc(dn_full, c.up("dn_full"))
                for i in range(4):
                    pe.wait_ge(conv_silu, c.next("conv"))
                    pe.wait_ge(dn_copied, c.take("dn_copied") - 1)
                    for r in range(4):
                        mm = pe.transpose(ps[2 + i % 2][:, r * P:r * P + P], pt[:, DV + i, r * P:r * P + P], ident)
                    mm.then_inc(dn_full, c.up("dn_full"))
                for i in range(8):
                    pe.wait_ge(kq_ready, c.next("kq"))
                    pe.wait_ge(dn_copied, c.take("dn_copied") - 1)
                    src = T[:, i] if i < 4 else ktok[:, i - 4]
                    for r in range(4):
                        mm = pe.transpose(ps[2 + i % 2][:, r * P:r * P + P], src[:, r * P:r * P + P], ident)
                    mm.then_inc(dn_full, c.up("dn_full"))
                pe.wait_ge(rows_step, c.next("rows_step", 1))
                for r in range(4):
                    pe.transpose(ps[5][:, r * 8:r * 8 + 8], g_rows[:, r * P:r * P + P], ident[0:8, 0:8])
                for r in range(4):
                    mm = pe.transpose(ps[4][:, r * 8:r * 8 + 8], beta_rows[:, r * P:r * P + P], ident[0:8, 0:8])
                mm.then_inc(bc_full, 1)
                pe.wait_ge(dn_copied, c.now("dn_copied"))
                pe.wait_ge(rows_step, c.next("rows_step", 1))
                for d, step, stage in lane_stages():
                    lane_pe(d, step, stage)
                for h in range(4):
                    if h == 0:
                        pe.wait_ge(oT_done, c.now("oT_done") + 4)
                        c.up("oT_done", 4)
                    pe.wait_ge(ut_copied, c.take("ut_copied"))
                    for r in range(4):
                        mm = pe.transpose(ps[7][:, r * P:r * P + P], pt[:, AO + r, h * P:h * P + P], ident)
                    mm.then_inc(ut_full, c.up("ut_full"))

            def lane_pe(d, step, stage):
                ch = step if d == 0 else 3 - step
                cs = slice(ch * P, ch * P + P)
                nt, sd, xx, xt, a1, qg, st = (four(t) for t in LANE[d])
                b0, b1, b2 = (four(ps[2 + 3 * d + i][:, :]) for i in range(3))

                def done(mm):
                    mm.then_inc(chunk_mm[d], c.up(f"mm{d}"))

                def ready():
                    pe.wait_ge(chunk_dve[d], c.next(f"cd{d}"))

                if stage == 0:
                    if step:
                        ready()
                    for h in range(4):
                        pe.matmul(b0[:, h], rows8[:, (4 * d + h) * P:(4 * d + h) * P + P], g_rows[:, cs], start=True, stop=True)
                        mm = pe.matmul(four(ps[d][:, :])[:, h], rows8[:, (4 * d + h) * P:(4 * d + h) * P + P], beta_rows[:, cs], start=True, stop=True)
                    done(mm)
                    for h in range(4):
                        pe.matmul(b1[:, h], pt[:, DK + h, cs], pt[:, DK + h, cs], start=True, stop=True)
                    for h in range(4):
                        mm = pe.matmul(b2[:, h], pt[:, DK + h, cs], pt[:, DQ + h, cs], start=True, stop=True)
                    done(mm)
                elif stage < 15:
                    m, half = divmod(stage - 1, 2)
                    ready()
                    if half == 0:
                        for h in range(4):
                            mm = pe.transpose(b0[:, h], nt[:, h], ident) if m == 0 else \
                                pe.matmul(b0[:, h], nt[:, h], xx[:, h], start=True, stop=True)
                    else:
                        if 0 < m < 6:
                            for h in range(4):
                                mm = pe.matmul(b1[:, h], xt[:, h], a1[:, h], start=True, stop=True)
                            done(mm)
                        for h in range(4):
                            mm = pe.transpose(b2[:, h], a1[:, h], ident) if m == 0 else \
                                pe.matmul(b2[:, h], a1[:, h], xt[:, h], start=True, stop=True)
                    done(mm)
                elif stage == 15:
                    ready()
                    for h in range(4):
                        mm = pe.matmul(b0[:, h], xt[:, h], nt[:, h], start=True, stop=True)
                    for h in range(4):
                        mm = pe.matmul(b1[:, h], a1[:, h], xt[:, h], start=True, stop=True)
                    done(mm)
                elif stage == 16:
                    pe.wait_ge(chunk_act[d], c.next(f"ca{d}", 2))
                    if step:
                        for h in range(4):
                            mm = pe.matmul(b2[:, h], xt[:, h], st[:, h], start=True, stop=True)
                        done(mm)
                else:
                    ready()
                    for h in range(4):
                        if step:
                            pe.matmul(b0[:, h], qg[:, h], st[:, h], start=True, stop=False)
                        pe.matmul(b0[:, h], sd[:, h], xx[:, h], start=not step, stop=True)
                    for h in range(4):
                        mm = pe.matmul(b1[:, h], nt[:, h], xx[:, h], start=True, stop=True)
                    done(mm)

            def memory_values():
                for i in range(4):
                    pe.wait_ge(vm_done, c.take("vm_done"))
                    for j in range(4):
                        f, t = 2 * i + j // 2, j % 2
                        mm = pe.transpose(ps[7][:, j * P:j * P + P], pt[:, 16 + f, t * P:t * P + P], ident)
                    mm.then_inc(vm_full, c.up("vm_full"))
                pe.wait_ge(vm_done, c.now("vm_done"))

            def cross():
                for h in range(4):
                    for s in range(2):
                        pe.wait_ge(evac[s], c.now(f"evac{s}"))
                    for q2 in range(2):
                        pe.wait_ge(sc_free, c.take("sc_free"))
                        for q in range(2):
                            qs = slice((2 * q2 + q) * P, (2 * q2 + q) * P + P)
                            for k in range(2):
                                mm = pe.matmul(ps[2][:, q * 256:q * 256 + 256], pt[:, 2 * h + k, qs], pt[:, 8 + 2 * h + k, 0:256],
                                               start=k == 0, stop=k == 1)
                        mm.then_inc(sc_full, c.up("sc_full"))
                        if h < 3:
                            job(q2, m_hi, m_lo)
                        pe.wait_ge(prob_done, c.next("prob"))
                        pe.wait_ge(tr_copied, c.take("tr_copied"))
                        for q in range(2):
                            for t in range(2):
                                mm = pe.transpose(ps[4][:, t * 256 + q * P:t * 256 + q * P + P], T[:, 0, q * 256 + t * P:q * 256 + t * P + P], ident)
                        mm.then_inc(tr_full, c.up("tr_full"))
                    pe.wait_ge(tr_copied, c.now("tr_copied"))
                    pe.wait_ge(pv_copied, c.take("pv_copied"))
                    for f in range(2):
                        for t in range(2):
                            mm = pe.matmul(ps[5 + f][:, :], vm(2 * h + f, t), T[:, 2 + t], start=t == 0, stop=t == 1)
                    mm.then_inc(pv_full, c.up("pv_full"))

            pe.wait_ge(setup_in, 48)
            pe.wait_ge(par_ready, 3)
            for i in range(4):
                n = min(512, VEC_COLS - i * 512)
                mm = pe.matmul(ps[2 + i][0:10, 0:n], relb, hot[:, i * 512:i * 512 + n], start=True, stop=True)
            mm = pe.matmul(ps[6][:, 0:4], ones[0:64, :], lamp, start=True, stop=True)
            mm.then_inc(vec_ready, 1)
            pe.wait_ge(mixer_in, 32)
            with c.loop(pe, LAYERS, PER["pe"]):
                ffn()
                mixers()
                ffn()
            second()

        @block.scalar
        def _(act):
            c = Count(FIRST)
            for free in (z_act, q_copied, tr_copied, pv_copied, ut_copied):
                act.sem_inc(free, 1)
            for free in (dn_copied, rows_copied):
                act.sem_inc(free, 2)

            def pump(s):
                act.wait_ge(raw_full[s], c.next(f"raw{s}", 16))
                act.wait_ge(job_done[s], c.take(f"slot{s}"))
                act.activation(w_hi[:, s], raw[:, s], ACT.Copy).then_inc(hi_done[s], 1)

            def skip(s):
                c.up(f"job{s}")
                c.up(f"evac{s}")

            def prepare(k, gain, ready, n=S):
                act.wait_ge(*ready)
                act.activation(xsq[:, 0:n], tile(x, k, n), ACT.Square).then_inc(square_done, c.up("square"))
                act.activation(tile(u_hi, k, n), tile(x, k, n), ACT.Copy, scale=gain).then_inc(u_hi_done, c.up("u_hi"))

            def deviation(n=S):
                act.wait_ge(stat_done, c.next("stat"))
                act.activation(std[:, 0:n], ps[7][:, 0:n], ACT.Sqrt, bias=eps[:, 0:1], scale=1.0 / D).then_inc(std_done, c.up("std"))

            def gate(src, dst, bank, func, bias=0.0):
                act.wait_ge(evac[bank], c.next(f"evac{bank}"))
                act.activation(dst, src, func, bias=bias).then_inc(silu_done, c.up("silu"))
                c.up(f"job{bank}")

            def upper(k, src=None):
                act.wait_ge(h_done, c.next("h"))
                act.activation(tile(m_hi, k), hf if src is None else src, ACT.Copy).then_inc(m_hi_done, c.up("m_hi"))

            def residual_tile(s, k, gain):
                c.up(f"job{s}")
                prepare(k, par[:, ds(k + gain, 1)] if not isinstance(k, int) else par[:, k + gain:k + gain + 1],
                        (evac[s], c.next(f"evac{s}")))

            def last_tile(gain):
                residual_tile(1, 7, gain)

            def ffn(before, finish):
                for part, n in enumerate(FF_PARTS):
                    pump(1)
                    if part == 0:
                        before()
                        deviation()
                    pump(0)
                    gate(gr, sg, 0, ACT.Silu)
                    with c.loop(act, n - 1, {**AJOB, "silu": 1, "h": 1, "m_hi": 1}) as i:
                        pump(1)
                        upper(i)
                        skip(1)
                        pump(0)
                        gate(gr, sg, 0, ACT.Silu)
                    c.up("m", n)
                    pump(1)
                    upper(n - 1)
                    skip(1)
                    pump(0)
                    if part < 2:
                        skip(0)
                        skip(1)
                        with c.loop(act, 3, AJOB):
                            pump(1)
                            pump(0)
                            skip(0)
                            skip(1)
                    else:
                        finish()

            def residual_tiles(gain):
                residual_tile(0, 0, gain)
                with c.loop(act, 3, {**AJOB, "square": 2, "u_hi": 2}) as i:
                    pump(1)
                    residual_tile(1, i * 2 + 1, gain)
                    pump(0)
                    residual_tile(0, i * 2 + 2, gain)

            def fourier():
                act.wait_ge(tab_full, c.now("tab"))
                for g in range(8):
                    act.wait_ge(z_full, c.next("z_full"))
                    if g >= 2:
                        act.wait_ge(pq_full, c.now("pq"))
                    act.activation(T[:, 2 * (g % 2)], ps[2][:, :], ACT.Copy).then_inc(z_act, c.up("z_act"))
                    c.up("z_full")
                    if g == 2:
                        mix_exp()
                    if g:
                        fourier_out(g - 1)
                fourier_out(7)

            def fourier_out(g):
                act.wait_ge(pq_full, c.next("pq"))
                act.activation(T[:, 4, 0:HALF], ps[5][:, 0:HALF], ACT.Copy).then_inc(q_copied, c.up("q_copied"))
                act.wait_ge(h_done, c.next("h"))
                act.activation(tile(m_hi, g), T[:, 7], ACT.Copy).then_inc(m_hi_done, c.up("m_hi"))

            def dilated(g):
                n = 1024 if g == 0 else 512
                for h in range(2):
                    pump(1)
                    act.wait_ge(max_done, c.next("max"))
                    e = T[:, 0:2].rearrange("p a n -> p (a n)")[:, 0:n]
                    act.activation(e, e, ACT.Exp).then_inc(exp_done, c.up("exp"))
                    pump(0)
                    skip(0)
                    skip(1)
                    act.wait_ge(tr_full, c.next("tr_full"))
                    if g == 0:
                        act.activation(T[:, 3], ps[6][:, :], ACT.Copy)
                    act.activation(T[:, 2], ps[4][:, :], ACT.Copy).then_inc(tr_copied, c.up("tr_copied"))
                act.wait_ge(pv_full, c.next("pv_full"))
                act.activation(T[:, 4], ps[5][:, :], ACT.Copy).then_inc(pv_copied, c.up("pv_copied"))
                act.wait_ge(ut_full, c.next("ut_full"))
                act.activation(natural(g, pt[:, QB + g]), grouped(g, ps[7][:, :]), ACT.Copy).then_inc(ut_copied, c.up("ut_copied"))

            def dilated_rows():
                for i, rows in enumerate((rows_m, rows_z)):
                    for g in range(3):
                        act.wait_ge(rows_full, c.next("rows_full"))
                        act.activation(natural(g, rows[:, g]), grouped(g, ps[2 + (g + i) % 2][0:2, :]), ACT.Copy).then_inc(rows_copied, c.up("rows_copied"))

            def mix_exp():
                act.wait_ge(max_done, c.next("max"))
                act.activation(rows_m, rows_m, ACT.Exp).then_inc(mixw_exp, c.up("mixw"))

            def dense():
                def exps(u):
                    act.wait_ge(max_done, c.next("max"))
                    b = u % 2
                    for m in range(2):
                        e = T[:, 2 * b + m]
                        ins = act.activation(e, e, ACT.Exp, bias=stats[:, 48 + 2 * b + m:49 + 2 * b + m],
                                             accum_out=stats[:, 52 + 2 * b + m:53 + 2 * b + m])
                    ins.then_inc(exp_done, c.up("exp"))

                exps(0)
                exps(1)
                for u in range(16):
                    act.wait_ge(tr_full, c.next("tr_full"))
                    act.activation(T[:, 4 + u % 2], ps[4][:, :], ACT.Copy).then_inc(tr_copied, c.up("tr_copied"))
                    if u % 2:
                        gate(T[:, 7], T[:, 7], 0, ACT.Sigmoid, bgate(0, u // 2))
                    act.wait_ge(pv_full, c.next("pv_full"))
                    act.activation(pt[:, OC + 3 - u // 4, (u % 4) * P:(u % 4) * P + P], ps[5][:, 0:P], ACT.Copy)
                    act.activation(T[:, 6, 0:P], ps[5][:, 0:P], ACT.Square, accum_out=stats[:, 64 + u:65 + u]).then_inc(pv_copied, c.up("pv_copied"))
                    act.wait_ge(pv_copied, c.now("pv_copied"))
                    if u < 14:
                        exps(u + 2)
                    pump(1 - u % 2)
                    if u % 2:
                        skip(1)
                pump(1)
                act.activation(stats[:, 64:80], stats[:, 64:80], ACT.Sqrt, bias=eps[:, 1:2], scale=1.0 / P).then_inc(std_done, c.up("std"))
                act.wait_ge(evac[1], c.now("evac1"))
                upper(0, pt[:, MIX])
                gate(gr, sg, 0, ACT.Sigmoid, bgate(1, 0))
                pump(0)
                gate(ur, xsq, 1, ACT.Sigmoid, bgate(2, 0))
                c.up("m", 1)
                for h in range(4):
                    act.wait_ge(ut_full, c.next("ut_full"))
                    act.activation(hf, ps[7][:, :], ACT.Copy, scale=par[:, LAYER_COLS["subln"]:LAYER_COLS["subln"] + 1]).then_inc(ut_copied, c.up("ut_copied"))
                    act.wait_ge(ut_copied, c.now("ut_copied"))
                    act.activation(tile(m_hi, 1 + h), hf, ACT.Copy).then_inc(m_hi_done, c.up("m_hi"))
                    act.wait_ge(m_ready, c.next("m"))

            def bgate(branch, m):
                return par[:, ds(m + (LAYER_COLS["b_gate"] + 8 * branch), 1)] if not isinstance(m, int) else \
                    par[:, LAYER_COLS["b_gate"] + 8 * branch + m:LAYER_COLS["b_gate"] + 8 * branch + m + 1]

            def load_biases(which):
                for i in which:
                    start = HEAD_OF[i] * VEC_COLS + VEC[KIND_OF[i]][0] + 1
                    act.dma_start(tab[:, BIAS_AT[i]:BIAS_AT[i] + BIAS_N[i]],
                                  bass.AP(vec_dram.tensor, start, [[1, P], [1, BIAS_N[i]]])).then_inc(tab_full, c.up("tab", 16))

            def mixers(before, gain):
                act.dma_start(tab[:, 0:DFT_COLS], dft_in).then_inc(tab_full, c.up("tab", 16))
                act.wait_ge(vec_stored, 16)
                load_biases(range(3, 10))
                pump(1)
                before()
                deviation()
                pump(0)
                skip(0)
                skip(1)
                pairs(8)
                for g in range(3):
                    dilated(g)
                dilated_rows()
                fourier()
                load_biases(range(3))
                c.up("m", 8)
                dense()
                with c.loop(act, 4, AJOB):
                    pump(1)
                    pump(0)
                    skip(0)
                    skip(1)
                pump(1)
                upper(0)
                pump(0)
                gate(gr, sg, 0, ACT.Sigmoid, bgate(1, 1))
                with c.loop(act, 6, {**AJOB, "silu": 2, "h": 1, "m_hi": 1}) as m:
                    pump(1)
                    gate(ur, xsq, 1, ACT.Sigmoid, bgate(2, m + 1))
                    upper(m + 1)
                    pump(0)
                    gate(gr, sg, 0, ACT.Sigmoid, bgate(1, m + 2))
                pump(1)
                gate(ur, xsq, 1, ACT.Sigmoid, bgate(2, 7))
                upper(7)
                pump(0)
                residual_tiles(gain)
                c.up("m", 8)

            def step(ins):
                ins.then_inc(act_step, c.up("act"))
                act.wait_ge(act_step, c.now("act"))

            def column(at, k):
                return small[:, at + k:at + k + 1] if isinstance(k, int) else small[:, ds(k + at, 1)]

            def pairs(n):
                with c.loop(act, n, AJOB):
                    pump(1)
                    pump(0)
                    skip(0)
                    skip(1)

            def squares(s, k):
                c.up(f"job{s}")
                act.wait_ge(evac[s], c.next(f"evac{s}"))
                act.activation(xsq, tile(pt, k), ACT.Square).then_inc(square_done, c.up("square"))

            def pairs_with_squares(at):
                with c.loop(act, 4, {**AJOB, "square": 2}) as i:
                    pump(1)
                    squares(0, i * 2 + at)
                    pump(0)
                    squares(1, i * 2 + (at + 1))

            def last_squares():
                squares(0, 0)
                with c.loop(act, 2, {**AJOB, "square": 2}) as i:
                    pump(1)
                    squares(1, i * 2 + 1)
                    pump(0)
                    squares(0, i * 2 + 2)
                pump(1)
                squares(1, 5)
                squares(0, 6)
                squares(1, 7)

            def second():
                c.up("act", 2)
                act.dma_start(window, window_in).then_inc(tab2_in, 16)
                act.dma_start(swap, swap_in).then_inc(tab2_in, 16)
                act.dma_start(pos_i, bass.AP(pos_in.tensor, 0, [[0, P], [1, S]])).then_inc(tab2_in, 16)
                act.dma_start(rows8, rows8_in).then_inc(tab2_in, 16)
                deviation()
                for k in range(KT):
                    prepare_tile(k, "g_mix_pre")
                pump(1)
                deviation()
                pump(0)
                skip(0)
                skip(1)
                pairs(2)
                window_attention()
                delta_net()
                act.wait_ge(mem_loaded, 16)
                act.wait_ge(m_ready, c.now("m"))
                act.activation(T[:, 0:4], tabt[:, 0:4], ACT.Square).then_inc(square_done, c.up("square"))
                for k in range(KT):
                    act.activation(u_hi[:, k, 0:256], memt[:, k], ACT.Copy, scale=column(TAIL["g_mem"], k)).then_inc(u_hi_done, c.up("u_hi"))
                pump(1)
                deviation(256)
                squares(0, 0)
                pump(0)
                squares(1, 1)
                with c.loop(act, 3, {**AJOB, "square": 2}) as i:
                    pump(1)
                    squares(0, i * 2 + 2)
                    pump(0)
                    squares(1, i * 2 + 3)
                pump(1)
                deviation()
                pump(0)
                skip(0)
                skip(1)
                with c.loop(act, 7, {**AJOB, "square": 1, "u_hi": 1, "x": 1}) as i:
                    pump(1)
                    pump(0)
                    prepare_m(i)
                    skip(0)
                    skip(1)
                prepare_m(7)
                pump(1)
                deviation()
                pump(0)
                skip(0)
                skip(1)
                cross()
                pairs_with_squares(8)
                deviation()
                for k in range(KT):
                    prepare_tile(k, "g_ffn_pre")
                ffn(lambda: None, last_squares)
                deviation()

            def prepare_tile(k, gain):
                act.wait_ge(x_done, c.next("x"))
                act.activation(T[:, k], x[:, k], ACT.Square).then_inc(tile_squared, 1)
                act.activation(u_hi[:, k], x[:, k], ACT.Copy, scale=column(TAIL[gain], k)).then_inc(u_hi_done, c.up("u_hi"))

            def prepare_m(k):
                act.wait_ge(x_done, c.next("x"))
                act.activation(xsq, tile(x, k), ACT.Square).then_inc(square_done, c.up("square"))
                act.activation(tile(m_hi, k), tile(x, k), ACT.Copy, scale=column(TAIL["g_cross_pre"], k)).then_inc(u_hi_done, c.up("u_hi"))

            def window_attention():
                act.wait_ge(angles_ready, 1)
                act.activation(cos, T[:, 1], ACT.Sin)
                act.activation(sin, T[:, 0], ACT.Sin).then_inc(tables_ready, 1)
                pump(1)
                pump(0)
                skip(0)
                skip(1)

                def exps(u):
                    act.wait_ge(max_done, c.next("max"))
                    b, n = u % 2, window_keys(u % 4)
                    for m in range(2):
                        e = T[:, 2 * b + m, 0:n]
                        act.activation(e, e, ACT.Exp, bias=stats[:, 48 + 2 * b + m:49 + 2 * b + m],
                                       accum_out=stats[:, 52 + 2 * b + m:53 + 2 * b + m])
                    sink = stats[:, 56 + 2 * b:58 + 2 * b]
                    act.activation(sink, sink, ACT.Exp).then_inc(exp_done, c.up("exp"))

                exps(0)
                exps(1)
                for u in range(16):
                    n = window_keys(u % 4)
                    act.wait_ge(tr_full, c.next("tr_full"))
                    act.activation(T[:, 4, 0:n], ps[4][:, 0:n], ACT.Copy)
                    act.activation(T[:, 5, 0:n], ps[6][:, 0:n], ACT.Copy).then_inc(tr_copied, c.up("tr_copied"))
                    pump(1 - u % 2)
                    if u % 2:
                        skip(0)
                        skip(1)
                    if 0 < u <= DN_TILES:
                        act.wait_ge(conv_done, c.next("conv_done"))
                        act.activation(pt[:, DQ + u - 1], T[:, 6 + (u - 1) % 2], ACT.Silu).then_inc(conv_silu, c.up("conv"))
                    if u < 14:
                        exps(u + 2)
                c.up("pv_full", 16)
                for f in range(4):
                    act.wait_ge(ut_full, c.next("ut_full"))
                    if f == 0:
                        act.dma_start(chunk, chunk_in).then_inc(tab3_in, 16)
                    act.activation(tile(m_hi, f), ps[7 - f % 2][:, :], ACT.Copy).then_inc(m_hi_done, c.up("m_hi"))
                c.up("m", 4)

            def delta_net():
                def to_tokens(i, dst):
                    act.wait_ge(dn_full, c.next("dn_full"))
                    act.activation(dst, ps[2 + i % 2][:, :], ACT.Copy).then_inc(dn_copied, c.up("dn_copied"))

                for i in range(DN_TILES):
                    to_tokens(i, T[:, i] if i < 4 else ktok[:, i - 4] if i < 8 else pt[:, DV + i - 8])
                act.wait_ge(row_terms, c.next("terms"))
                e = T[0:8, 5]
                step(act.activation(e, e, ACT.Exp))
                act.activation(e, e, ACT.Ln, bias=ones[0:8, 0:1])
                act.activation(stats[0:8, 88:89], small[0:8, A_LOG:A_LOG + 1], ACT.Exp)
                act.activation(beta_rows, pt[32:40, AB], ACT.Sigmoid).then_inc(row_exps, c.up("exps"))
                act.wait_ge(row_terms, c.next("terms"))
                act.activation(stats[:, 0:32], stats[:, 0:32], ACT.Sqrt, bias=eps[:, 0:1]).then_inc(row_exps, c.up("exps"))
                for i in range(8):
                    to_tokens(i, pt[:, DQ + i])
                act.wait_ge(row_terms, c.next("terms"))
                act.activation(beg, gcol, ACT.Exp).then_inc(row_exps, c.up("exps"))
                for d, s, stage in lane_stages():
                    if stage == 0:
                        b0 = ps[2 + 3 * d]
                        act.wait_ge(chunk_terms[d], c.next(f"terms{d}"))
                        act.activation(LANE[d][5], b0[:, :], ACT.Exp)
                        act.activation(stats[:, 224 + 8 * d:232 + 8 * d], stats[:, 224 + 8 * d:232 + 8 * d], ACT.Exp)
                        act.activation(LANE[d][4], LANE[d][4], ACT.Exp).then_inc(chunk_act[d], c.up(f"ca{d}"))
                    elif stage == 15:
                        act.wait_ge(chunk_mm[d], c.next(f"mm{d}", 22))
                        act.activation(LANE[d][2], ps[2 + 3 * d][:, :], ACT.Copy)
                        act.activation(LANE[d][3], ps[3 + 3 * d][:, :], ACT.Copy).then_inc(chunk_act[d], c.up(f"ca{d}"))
                        c.up(f"mm{d}", 2 if s else 1)
                        if d == 1 and s == 0:
                            act.activation(pt[:, DG:DG + 4], pt[:, DG:DG + 4], ACT.Silu)
                act.wait_ge(row_terms, c.next("terms"))
                act.dma_start(tabt[:, 0:4].rearrange("p a n -> p (a n)"), mem_in.rearrange("p k n -> p (k n)")).then_inc(mem_loaded, 16)
                act.activation(stats[:, 0:16], stats[:, 0:16], ACT.Sqrt, bias=eps[:, 0:1], scale=1.0 / P).then_inc(row_exps, c.up("exps"))
                for h in range(4):
                    upper(4 + h)
                c.up("m", 4)

            def cross():
                for h in range(4):
                    if h < 3:
                        pump(1)
                    for q2 in range(2):
                        act.wait_ge(max_done, c.next("max"))
                        for q in range(2):
                            ins = act.activation(T[:, 0, q * 256:q * 256 + 256], ps[2][:, q * 256:q * 256 + 256], ACT.Exp, scale=0.0625,
                                                 bias=stats[:, 48 + q:49 + q], accum_out=stats[:, 52 + q:53 + q])
                        ins.then_inc(exp_done, c.up("exp"))
                        if h < 3 and q2 == 0:
                            pump(0)
                            skip(0)
                            skip(1)
                        act.wait_ge(tr_full, c.next("tr_full"))
                        act.activation(T[:, 2:4, q2 * 256:q2 * 256 + 256], ps[4][:, :].rearrange("p (t n) -> p t n", t=2), ACT.Copy).then_inc(tr_copied, c.up("tr_copied"))
                    act.wait_ge(pv_full, c.next("pv_full"))
                    for f in range(2):
                        act.activation(tile(u_hi, 2 * h + f), ps[5 + f][:, :], ACT.Copy).then_inc(u_hi_done, c.up("u_hi"))

            act.dma_start(hot, hot_in).then_inc(setup_in, 16)
            act.dma_start(pt[0:32, 4, 0:10], rel_in).then_inc(setup_in, 16)
            act.dma_start(lamv, lam_in).then_inc(setup_in, 16)
            act.dma_start(eye[:, :], eye_in).then_inc(mixer_in, 16)
            act.dma_start(sel[:, :], sel_in).then_inc(mixer_in, 16)
            act.wait_ge(loaded, 16)
            for k in range(KT):
                if k:
                    act.wait_ge(acc_step, k)
                if k == 2:
                    pump(0)
                prepare(k, small[:, TAIL["g_first"] + k:TAIL["g_first"] + k + 1], (x_in_part[k // 2], 16))
            act.wait_ge(vec_ready, 1)
            act.activation(stats[:, 0:4], ps[6][:, 0:4], ACT.Exp).then_inc(act_step, 1)
            for i in range(4):
                n = min(512, VEC_COLS - i * 512)
                ins = act.activation(vec_sb[:, i * 512:i * 512 + n], ps[2 + i][0:10, 0:n], ACT.Copy)
            ins.then_inc(act_step, 1)
            act.wait_ge(act_step, 2)
            act.dma_start(vec_dram, vec_sb).then_inc(vec_stored, 16)
            before = lambda: None
            with c.loop(act, LAYERS, PER["act"]) as l:
                ffn(before, lambda: residual_tiles(LAYER_COLS["g_mix"]))
                mixers(lambda: last_tile(LAYER_COLS["g_mix"]), LAYER_COLS["g_ffn2"])
                ffn(lambda: last_tile(LAYER_COLS["g_ffn2"]), lambda: residual_tiles(LAYER_COLS["g_next"]))
                last_tile(LAYER_COLS["g_next"])
            second()

        @block.vector
        def _(dve):
            c = Count(FIRST, inner_loops)
            dve.memset(ones[:, :], 1.0)
            dve.memset(acc, 0.0).then_inc(dve_step, c.up("dve"))
            for s in range(2):
                dve.sem_inc(evac[s], 1)
            for free in (z_dve, y_done, vt_done, sc_free, wb_free, oT_done, rope_done, vm_done):
                dve.sem_inc(free, 1)
            dve.memset(eps[:, 0:1], EPS)
            dve.memset(eps[:, 1:2], 1e-5).then_inc(par_ready, 1)
            dve.memset(relb[32:33], 1.0).then_inc(par_ready, 1)
            dve.wait_ge(dve_step, c.now("dve"))

            def step(ins):
                ins.then_inc(dve_step, c.up("dve"))
                dve.wait_ge(dve_step, c.now("dve"))

            def prepare(k, gain, n=S):
                dve.wait_ge(square_done, c.next("square"))
                if c.n.get("acc", 0) or c.loops:
                    dve.wait_ge(acc_step, c.now("acc"))
                dve.tensor_tensor(acc[:, 0:n], acc[:, 0:n], xsq[:, 0:n], ALU.add).then_inc(acc_step, c.up("acc"))
                dve.wait_ge(u_hi_done, c.next("u_hi"))
                dve.scalar_tensor_tensor(out=tile(u_lo, k), in0=tile(x, k), scalar=gain, in1=tile(u_hi, k).bitcast(F32),
                                         op0=ALU.mult, op1=ALU.subtract).then_inc(u_ready, c.up("u"))

            def reciprocal_rms(n=S):
                dve.wait_ge(std_done, c.next("std"))
                step(dve.reciprocal(rs[:, 0:n], std[:, 0:n]))

            def scaled(s, dst):
                dve.wait_ge(job_done[s], c.next(f"job{s}"))
                dve.tensor_tensor(dst, ps[s][:, :], rs[:, :], ALU.mult).then_inc(evac[s], c.up(f"evac{s}"))

            def lower(k, src=None):
                dve.wait_ge(m_hi_done, c.next("m_hi"))
                dve.tensor_tensor(tile(m_lo, k), hf if src is None else src, tile(m_hi, k).bitcast(F32), ALU.subtract).then_inc(m_ready, c.up("m"))

            def ff_tile(k):
                scaled(0, gr)
                scaled(1, ur)
                dve.wait_ge(evac[1], c.now("evac1"))
                dve.wait_ge(silu_done, c.next("silu"))
                dve.tensor_tensor(hf, sg, ur, ALU.mult).then_inc(h_done, c.up("h"))
                lower(k)

            def residual(s, k, scale):
                dve.wait_ge(job_done[s], c.next(f"job{s}"))
                dve.scalar_tensor_tensor(out=tile(x, k), in0=ps[s][:, :], scalar=scale, in1=tile(x, k),
                                         op0=ALU.mult, op1=ALU.add).then_inc(evac[s], c.up(f"evac{s}"))
                dve.wait_ge(evac[s], c.now(f"evac{s}"))

            def residual_tiles(scale, gain):
                step(dve.memset(acc, 0.0))
                with c.loop(dve, 4, {**JOB, "square": 2, "u_hi": 2, "u": 2, "acc": 2}) as i:
                    for s in range(2):
                        residual(s, i * 2 + s, scale)
                        prepare(i * 2 + s, par[:, ds(i * 2 + (s + gain), 1)])

            def ffn(gain):
                reciprocal_rms()
                for part, n in enumerate(FF_PARTS):
                    with c.loop(dve, n, {**JOB, "silu": 1, "h": 1, "m_hi": 1, "m": 1}) as i:
                        ff_tile(i)
                    if part < 2:
                        with c.loop(dve, 4, JOB) as i:
                            for s in range(2):
                                residual(s, i * 2 + s, 0.5)
                    else:
                        residual_tiles(0.5, gain)

            def fourier():
                for g in range(8):
                    c.up("z_full")
                    dve.wait_ge(z_full, c.next("z_full"))
                    if g >= 2:
                        dve.wait_ge(pq_full, c.now("pq"))
                    dve.tensor_copy(T[:, 2 * (g % 2) + 1], ps[3][:, :]).then_inc(z_dve, c.up("z_dve"))
                    if g:
                        fourier_out(g - 1)
                    if 1 <= g <= 4:
                        dve.wait_ge(vt_full, c.next("vt_full"))
                        dve.tensor_copy(pt[:, VC + g - 1], ps[6][:, :]).then_inc(vt_done, c.up("vt_done"))
                    if g == 1:
                        dilated_rows()
                    if g >= 4:
                        dilated_shares(g - 4)
                fourier_out(7)

            def fourier_out(g):
                dve.wait_ge(q_copied, c.next("q_copied"))
                c.up("pq")
                if g:
                    dve.wait_ge(m_ready, c.now("m"))
                dve.tensor_tensor(T[:, 7, 0:HALF], ps[4][:, 0:HALF], T[:, 4, 0:HALF], ALU.subtract)
                dve.tensor_tensor(T[:, 7, S - 1:HALF - 1:-1], ps[4][:, 1:HALF - 1], T[:, 4, 1:HALF - 1], ALU.add).then_inc(y_done, c.up("y_done"))
                dve.wait_ge(y_done, c.now("y_done"))
                dve.sem_inc(h_done, c.up("h"))
                dve.wait_ge(m_hi_done, c.next("m_hi"))
                dve.tensor_tensor(tile(m_lo, g), T[:, 7], tile(m_hi, g).bitcast(F32), ALU.subtract).then_inc(m_ready, c.up("m"))

            def dilated(g):
                dve.wait_ge(vt_full, c.next("vt_full"))
                if g == 0:
                    dve.tensor_copy(pt[:, 29, 0:P], ps[6][:, 0:P])
                dve.tensor_copy(pt[:, VB + g], ps[5][:, :]).then_inc(vt_done, c.up("vt_done"))
                n = 256 if g == 0 else P
                l = T[:, 0:2].rearrange("p a n -> p (a n)")[:, 0:4 * n]
                l4 = l.rearrange("p (t n) -> p t n", t=4)
                for h in range(2):
                    dve.wait_ge(sc_full, c.next("sc_full"))
                    if h:
                        dve.wait_ge(tr_full, c.now("tr_full"))
                    if g == 0:
                        dve.memset(l[:, 0:64], -1e30)
                        dve.memset(l[:, 960:1024], -1e30)
                        for r in range(4):
                            lo, hi = (64 if r == 0 else 0), (192 if r == 3 else 256)
                            ins = dve.scalar_tensor_tensor(out=l4[:, r, lo:hi], in0=ps[2 + r // 2][:, (r % 2) * 256 + lo:(r % 2) * 256 + hi],
                                                           scalar=0.125, in1=bias_of(4 + h, lo, hi - lo), op0=ALU.mult, op1=ALU.add)
                    else:
                        ins = dve.scalar_tensor_tensor(out=l4, in0=ps[2][:, :].rearrange("p (t n) -> p t n", t=4), scalar=0.125,
                                                       in1=bias_of(4 + 2 * g + h, 0, P)[:, None, :].broadcast_to([P, 4, P]), op0=ALU.mult, op1=ALU.add)
                    ins.then_inc(sc_free, c.up("sc_free"))
                    dve.wait_ge(sc_free, c.now("sc_free"))
                    step(dve.tensor_reduce(nmax[:, g, :, h], l4, AX.X, ALU.max, negate=True))
                    dve.tensor_tensor(l4, l4, nmax[:, g, :, h:h + 1].broadcast_to([P, 4, n]), ALU.add).then_inc(max_done, c.up("max"))
                    scaled(0, pt[:, 18 + 4 * g + 2 * h])
                    dve.wait_ge(exp_done, c.next("exp"))
                    dve.tensor_reduce(total[:, g, :, h], l4, AX.X, ALU.add).then_inc(total_done, c.up("total"))
                    dve.wait_ge(total_done, c.now("total"))
                    scaled(1, pt[:, 19 + 4 * g + 2 * h])
                    c.up("tr_full")

            def dilated_rows():
                c.up("rows", 6)
                dve.wait_ge(rows_copied, c.now("rows") + 2)
                least = pt[0:2, 29]
                step(dve.tensor_tensor(least, rows_m[:, 0], rows_m[:, 1], ALU.min))
                step(dve.tensor_tensor(least, least, rows_m[:, 2], ALU.min))
                dve.tensor_tensor(rows_m, pt[0:2, 29:30, :].broadcast_to([2, 3, S]), rows_m, ALU.subtract).then_inc(max_done, c.up("max"))

            def dilated_shares(part):
                shared = pt[0:2, 29]
                if part == 0:
                    dve.wait_ge(mixw_exp, c.next("mixe"))
                    step(dve.tensor_tensor(rows_z, rows_z, rows_m, ALU.mult))
                elif part == 1:
                    step(dve.tensor_tensor(shared, rows_z[:, 0], rows_z[:, 1], ALU.add))
                    step(dve.tensor_tensor(shared, shared, rows_z[:, 2], ALU.add))
                elif part == 2:
                    step(dve.reciprocal(shared, shared))
                else:
                    dve.tensor_tensor(rows_m, rows_m, pt[0:2, 29:30, :].broadcast_to([2, 3, S]), ALU.mult).then_inc(mixw_done, c.up("mixw"))

            def mix_groups():
                for g in range(3):
                    dve.wait_ge(wb_full, c.next("wb_full"))
                    dst = hf if g == 0 else T[:, 5]
                    dve.tensor_tensor(dst, pt[:, QB + g], ps[7][:, :], ALU.mult).then_inc(wb_free, c.up("wb_free"))
                    dve.wait_ge(wb_free, c.now("wb_free"))
                    if g == 1:
                        step(dve.tensor_tensor(hf, hf, T[:, 5], ALU.add))
                    if g == 2:
                        step(dve.tensor_tensor(pt[:, MIX], hf, T[:, 5], ALU.add))

            def dense():
                def logits(u):
                    h, r = 3 - u // 4, u % 4
                    b = u % 2
                    if u == 4:
                        dve.wait_ge(tab_full, c.next("tab", 48))
                    dve.wait_ge(sc_full, c.next("sc_full"))
                    if u >= 2:
                        dve.wait_ge(tr_full, c.now("tr_full"))
                    for m in range(2):
                        ins = dve.scalar_tensor_tensor(out=T[:, 2 * b + m], in0=ps[2 + m][:, :], scalar=0.125,
                                                       in1=bias_of(h, 384 - r * P, S), op0=ALU.mult, op1=ALU.add)
                    ins.then_inc(sc_free, c.up("sc_free"))
                    dve.wait_ge(sc_free, c.now("sc_free"))
                    dve.tensor_reduce(stats[:, 48 + 2 * b:50 + 2 * b], T[:, 2 * b:2 * b + 2], AX.X, ALU.max, negate=True).then_inc(max_done, c.up("max"))

                def probabilities(u):
                    b = u % 2
                    dve.wait_ge(exp_done, c.next("exp"))
                    if u:
                        dve.wait_ge(prob_done, c.now("prob"))
                    step(dve.reciprocal(stats[:, 56:58], stats[:, 52 + 2 * b:54 + 2 * b]))
                    step(dve.tensor_tensor(stats[:, 58:59], stats[:, 57:58], par[:, 49:50], ALU.mult))
                    step(dve.tensor_scalar(T[:, 2 * b + 1], T[:, 2 * b + 1], stats[:, 58:59], None, ALU.mult))
                    dve.scalar_tensor_tensor(out=T[:, 2 * b + 1], in0=T[:, 2 * b], scalar=stats[:, 56:57], in1=T[:, 2 * b + 1],
                                             op0=ALU.mult, op1=ALU.add).then_inc(prob_done, c.up("prob"))

                logits(0)
                logits(1)
                for u in range(17):
                    if u < 16:
                        probabilities(u)
                        c.up("tr_full")
                    if u % 2:
                        if u > 1:
                            dve.wait_ge(evac[1], c.now("evac1"))
                        scaled(0, T[:, 7])
                    elif u:
                        dve.wait_ge(silu_done, c.next("silu"))
                        dve.wait_ge(job_done[1], c.next("job1"))
                        dve.tensor_tensor(pt[:, u // 2 - 1], T[:, 7], ps[1][:, :], ALU.mult).then_inc(evac[1], c.up("evac1"))
                    if u < 14:
                        logits(u + 2)
                dve.sem_inc(h_done, c.up("h"))
                lower(0, pt[:, MIX])
                dve.wait_ge(std_done, c.next("std"))
                step(dve.reciprocal(stats[:, 80:96], stats[:, 64:80]))
                step(dve.tensor_scalar(stats[:, 80:96], stats[:, 80:96], par[:, 50:51], None, ALU.mult))
                for h in range(4):
                    o = pt[:, OC + h].rearrange("p (t n) -> p t n", t=4)
                    dve.tensor_tensor(o, o, stats[:, 92 - 4 * h:96 - 4 * h, None].broadcast_to([P, 4, P]), ALU.mult).then_inc(oT_done, c.up("oT_done"))
                scaled(0, gr)
                scaled(1, ur)
                for h in range(4):
                    lower(1 + h)

            def mixers():
                reciprocal_rms()
                with c.loop(dve, 9, JOB) as i:
                    for s in range(2):
                        scaled(s, tile(pt, i * 2 + s))
                for s in range(2):
                    dve.wait_ge(evac[s], c.now(f"evac{s}"))
                dve.wait_ge(vec_stored, 16)
                dve.wait_ge(tab_full, c.next("tab", 128))
                for g in range(3):
                    dilated(g)
                for s in range(2):
                    dve.wait_ge(evac[s], c.now(f"evac{s}"))
                fourier()
                mix_groups()
                dense()
                c.up("pv_full", 3 + 16)
                with c.loop(dve, 4, JOB) as i:
                    for s in range(2):
                        dve.wait_ge(job_done[s], c.next(f"job{s}"))
                        dve.tensor_copy(tile(pt, i * 2 + (s + YB)), ps[2 + s][:, :])
                        dve.tensor_copy(tile(pt, i * 2 + (s + YC)), ps[s][:, :]).then_inc(evac[s], c.up(f"evac{s}"))
                for s in range(2):
                    dve.wait_ge(evac[s], c.now(f"evac{s}"))

                def merged(m):
                    dve.wait_ge(silu_done, c.next("silu"))
                    step(dve.tensor_tensor(hf, sg, tile(pt, m + YB), ALU.mult))
                    step(dve.tensor_tensor(hf, hf, tile(pt, m), ALU.add))
                    dve.wait_ge(silu_done, c.next("silu"))
                    step(dve.tensor_tensor(std, xsq, tile(pt, m + YC), ALU.mult))
                    dve.tensor_tensor(hf, hf, std, ALU.add).then_inc(h_done, c.up("h"))
                    lower(m)

                merged(0)
                with c.loop(dve, 7, {**JOB, "silu": 2, "dve": 3, "h": 1, "m_hi": 1, "m": 1}) as m:
                    scaled(0, gr)
                    scaled(1, ur)
                    merged(m + 1)
                residual_tiles(1.0, LAYER_COLS["g_ffn2"])

            def column(at, k):
                return small[:, at + k:at + k + 1] if isinstance(k, int) else small[:, ds(k + at, 1)]

            def lower_tile(k, gain):
                dve.wait_ge(u_hi_done, c.next("u_hi"))
                dve.scalar_tensor_tensor(out=u_lo[:, k], in0=x[:, k], scalar=column(TAIL[gain], k), in1=u_hi[:, k].bitcast(F32),
                                         op0=ALU.mult, op1=ALU.subtract).then_inc(u_ready, c.up("u"))

            def add_squares():
                dve.wait_ge(square_done, c.next("square"))
                dve.wait_ge(acc_step, c.now("acc"))
                dve.tensor_tensor(acc, acc, xsq, ALU.add).then_inc(acc_step, c.up("acc"))

            def normed_tile(k, at, gain):
                step(dve.tensor_tensor(pt[:, 29], tile(pt, k + at), rs[:, :], ALU.mult))
                dve.scalar_tensor_tensor(out=tile(x, k), in0=pt[:, 29], scalar=column(TAIL[gain], k), in1=tile(x, k),
                                         op0=ALU.mult, op1=ALU.add).then_inc(x_done, c.up("x"))
                dve.wait_ge(x_done, c.now("x"))

            def keep_with_squares(at):
                step(dve.memset(acc, 0.0))
                with c.loop(dve, 4, {**JOB, "square": 2, "acc": 2}) as i:
                    for s in range(2):
                        dve.wait_ge(job_done[s], c.next(f"job{s}"))
                        dve.tensor_copy(tile(pt, i * 2 + (s + at)), ps[s][:, :]).then_inc(evac[s], c.up(f"evac{s}"))
                        add_squares()

            def second():
                reciprocal_rms()
                for k in range(KT):
                    dve.scalar_tensor_tensor(out=tile(x, k), in0=tile(x, k), scalar=column(LC + LAYER_COLS["g_next"], k), in1=rs[:, :],
                                             op0=ALU.mult, op1=ALU.mult).then_inc(x_done, c.up("x"))
                    if k:
                        lower_tile(k - 1, "g_mix_pre")
                lower_tile(KT - 1, "g_mix_pre")
                reciprocal_rms()
                with c.loop(dve, 3, JOB) as i:
                    for s in range(2):
                        scaled(s, tile(pt, i * 2 + s))
                for s in range(2):
                    dve.wait_ge(evac[s], c.now(f"evac{s}"))
                window_attention()
                delta_net()
                dve.wait_ge(square_done, c.next("square"))
                dve.tensor_reduce(mem_sum, T[:, 0:4].rearrange("p a n -> p (a n)").rearrange("p (k n) -> p n k", k=KT),
                                  AX.X, ALU.add).then_inc(acc_step, c.up("acc", 8))
                for k in range(KT):
                    dve.wait_ge(u_hi_done, c.next("u_hi"))
                    dve.scalar_tensor_tensor(out=u_lo[:, k, 0:256], in0=memt[:, k], scalar=column(TAIL["g_mem"], k),
                                             in1=u_hi[:, k, 0:256].bitcast(F32), op0=ALU.mult, op1=ALU.subtract).then_inc(u_ready, c.up("u"))
                dve.wait_ge(std_done, c.next("std"))
                step(dve.reciprocal(rs_mem[:, :], std[:, 0:256]))
                keep_with_squares(0)

                def memory_pair(i):
                    for s in range(2):
                        dve.wait_ge(job_done[s], c.next(f"job{s}"))
                        k = i * 2 + (s + 8)
                        dst = pt[:, k, 0:256] if isinstance(k, int) else pt[:, ds(k, 1), 0:256].rearrange("p o n -> p (o n)")
                        dve.tensor_tensor(dst, ps[s][:, 0:256], rs_mem[:, :], ALU.mult).then_inc(evac[s], c.up(f"evac{s}"))

                def cross_input(k):
                    normed_tile(k, 0, "g_mix_post")
                    add_squares()
                    dve.wait_ge(u_hi_done, c.next("u_hi"))
                    dve.scalar_tensor_tensor(out=tile(m_lo, k), in0=tile(x, k), scalar=column(TAIL["g_cross_pre"], k),
                                             in1=tile(m_hi, k).bitcast(F32), op0=ALU.mult, op1=ALU.subtract).then_inc(m_ready, c.up("m"))

                memory_pair(0)
                reciprocal_rms()
                step(dve.memset(acc, 0.0))
                with c.loop(dve, 7, {**JOB, "square": 1, "acc": 1, "u_hi": 1, "m": 1, "x": 1, "dve": 1}) as i:
                    cross_input(i)
                    memory_pair(i + 1)
                cross_input(7)
                for i in range(4):
                    dve.wait_ge(vm_full, c.next("vm_full"))
                    dve.tensor_copy(pt[:, 24 + i], ps[7][:, :]).then_inc(vm_done, c.up("vm_done"))
                reciprocal_rms()
                for s in range(2):
                    scaled(s, pt[:, s])
                cross()
                keep_with_squares(8)
                reciprocal_rms()
                for k in range(KT):
                    normed_tile(k, 8, "g_cross_post")
                    if k:
                        lower_tile(k - 1, "g_ffn_pre")
                lower_tile(KT - 1, "g_ffn_pre")
                reciprocal_rms()
                for part, n in enumerate(FF_PARTS):
                    with c.loop(dve, n, {**JOB, "silu": 1, "h": 1, "m_hi": 1, "m": 1}) as i:
                        ff_tile(i)
                    if part == 0:
                        with c.loop(dve, 4, JOB) as i:
                            for s in range(2):
                                dve.wait_ge(job_done[s], c.next(f"job{s}"))
                                dve.tensor_copy(tile(pt, i * 2 + s), ps[s][:, :]).then_inc(evac[s], c.up(f"evac{s}"))
                    if part == 2:
                        step(dve.memset(acc, 0.0))
                    if part:
                        with c.loop(dve, 4, JOB if part == 1 else {**JOB, "square": 2, "acc": 2}) as i:
                            for s in range(2):
                                dve.wait_ge(job_done[s], c.next(f"job{s}"))
                                dst = tile(pt, i * 2 + s)
                                dve.tensor_tensor(dst, dst, ps[s][:, :], ALU.add).then_inc(evac[s], c.up(f"evac{s}"))
                                if part == 2:
                                    add_squares()
                reciprocal_rms()
                for k in range(KT):
                    normed_tile(k, 0, "g_ffn_post")

            def window_attention():
                step(dve.tensor_scalar(neg_sink, small[:, SINK:SINK + 8], -1.0, None, ALU.mult))
                ang, k, a, b = T[:, 0], T[:, 1], T[:, 2], T[:, 3]
                dve.wait_ge(tab2_in, 64)
                step(dve.tensor_copy(ang, pos_i))
                step(dve.tensor_scalar(ang, ang, small[:, INV_FREQ:INV_FREQ + 1], None, ALU.mult))
                step(dve.tensor_scalar(k, ang, float(1 / (2 * np.pi)), ROUND, ALU.mult, ALU.add))
                step(dve.tensor_scalar(k, k, ROUND, None, ALU.subtract))
                for turn in TWO_PI:
                    step(dve.scalar_tensor_tensor(out=ang, in0=k, scalar=-turn, in1=ang, op0=ALU.mult, op1=ALU.add))
                step(dve.tensor_scalar(a, ang, float(np.pi / 2), None, ALU.add))
                step(dve.tensor_scalar(b, a, float(np.pi), float(-2 * np.pi), ALU.is_gt, ALU.mult))
                step(dve.tensor_tensor(k, a, b, ALU.add))
                step(dve.tensor_scalar(ang, ang, NEAR_PI, -NEAR_PI, ALU.min, ALU.max))
                dve.tensor_scalar(k, k, NEAR_PI, -NEAR_PI, ALU.min, ALU.max).then_inc(angles_ready, 1)
                dve.wait_ge(tables_ready, 1)
                for i in range(5):
                    dve.wait_ge(rope_full, c.next("rope_full"))
                    step(dve.tensor_tensor(a, ps[2][:, :], sin, ALU.mult))
                    step(dve.tensor_tensor(pt[:, i], pt[:, i], cos, ALU.mult))
                    dve.tensor_tensor(pt[:, i], pt[:, i], a, ALU.add).then_inc(rope_done, c.up("rope_done"))
                    dve.wait_ge(rope_done, c.now("rope_done"))
                    if i in (1, 3):
                        scaled(i // 2, pt[:, 6 + i // 2])
                dve.wait_ge(vt_full, c.next("vt_full"))
                dve.tensor_copy(pt[:, AV], ps[6][:, :]).then_inc(vt_done, c.up("vt_done"))

                def logits(u):
                    j, r = divmod(u, 4)
                    b, n = u % 2, window_keys(r)
                    dve.wait_ge(sc_full, c.next("sc_full"))
                    if u >= 2:
                        dve.wait_ge(tr_full, c.now("tr_full"))
                    w = window[:, 0 if r else P:(0 if r else P) + n]
                    for m in range(2):
                        ins = dve.scalar_tensor_tensor(out=T[:, 2 * b + m, 0:n], in0=ps[2 + m][:, 0:n], scalar=0.125, in1=w,
                                                       op0=ALU.mult, op1=ALU.add)
                    ins.then_inc(sc_free, c.up("sc_free"))
                    dve.wait_ge(sc_free, c.now("sc_free"))
                    top = stats[:, 48 + 2 * b:50 + 2 * b]
                    step(dve.tensor_reduce(top, T[:, 2 * b:2 * b + 2, 0:n], AX.X, ALU.max, negate=True))
                    step(dve.tensor_tensor(top, top, neg_sink[:, j:j + 5:4], ALU.min))
                    dve.tensor_tensor(stats[:, 56 + 2 * b:58 + 2 * b], top, neg_sink[:, j:j + 5:4], ALU.subtract).then_inc(max_done, c.up("max"))

                def outputs(u):
                    j, r = divmod(u, 4)
                    b = u % 2
                    dve.wait_ge(exp_done, c.next("exp"))
                    share = stats[:, 60 + 2 * b:62 + 2 * b]
                    step(dve.tensor_tensor(share, stats[:, 52 + 2 * b:54 + 2 * b], stats[:, 56 + 2 * b:58 + 2 * b], ALU.add))
                    step(dve.reciprocal(share, share))
                    dve.wait_ge(pv_full, c.next("pv_full"))
                    o = pt[:, AO + r].rearrange("p (m n) -> p m n", m=2)[:, :, 64 * j:64 * j + 64]
                    dve.tensor_tensor(o, ps[5][:, 0:P].rearrange("p (m n) -> p m n", m=2),
                                      share[:, :, None].broadcast_to([P, 2, 64]), ALU.mult).then_inc(pv_copied, c.up("pv_copied"))

                logits(0)
                logits(1)
                for u in range(16):
                    outputs(u)
                    c.up("tr_full")
                    if u < 14:
                        logits(u + 2)
                    if u:
                        scaled((u - 1) % 2, pt[:, 7 + u])
                    if u < DN_TILES:
                        convolution(u)
                scaled(1, pt[:, 23])
                for f in range(4):
                    lower(f, ps[7 - f % 2][:, :])
                    dve.wait_ge(m_ready, c.now("m"))
                    dve.sem_inc(ut_copied, 1)

            def convolution(i):
                src, dst = pt[:, DQ + i], T[:, 6 + i % 2]
                if i >= 2:
                    dve.wait_ge(conv_silu, i - 1)
                tap = lambda t: small[:, CONV + 5 * i + t:CONV + 5 * i + t + 1]
                step(dve.tensor_scalar(dst, src, tap(2), None, ALU.mult))
                for t in (0, 1, 3, 4):
                    to, frm = (slice(2 - t, S), slice(0, S - 2 + t)) if t < 2 else (slice(0, S + 2 - t), slice(t - 2, S))
                    ins = dve.scalar_tensor_tensor(out=dst[:, to], in0=src[:, frm], scalar=tap(t), in1=dst[:, to], op0=ALU.mult, op1=ALU.add)
                    if t < 4:
                        step(ins)
                ins.then_inc(conv_done, c.up("conv_done"))

            def delta_net():
                z, e = T[0:8, 4], T[0:8, 5]
                step(dve.tensor_scalar(z, g_rows, small[0:8, DT_BIAS:DT_BIAS + 1], None, ALU.add))
                step(dve.scalar_tensor_tensor(out=e, in0=z, scalar=-1.0, in1=z, op0=ALU.mult, op1=ALU.min))
                dve.tensor_scalar(z, z, 0.0, None, ALU.max).then_inc(row_terms, c.up("terms"))
                for i in range(8):
                    dve.wait_ge(dn_copied, c.next("dn_copied"))
                    t = T[:, i] if i < 4 else ktok[:, i - 4]
                    sq = T[:, 6]
                    if i == 0:
                        dve.wait_ge(conv_silu, 11)
                    step(dve.tensor_tensor(sq, t, t, ALU.mult))
                    step(dve.tensor_reduce(stats[:, 4 * i:4 * i + 4], four(sq), AX.X, ALU.add))
                dve.sem_inc(row_terms, c.up("terms"))
                c.up("dn_copied", 12)
                dve.wait_ge(row_exps, c.next("exps", 2))
                step(dve.reciprocal(stats[:, 32:64], stats[:, 0:32]))
                step(dve.tensor_scalar(stats[:, 32:48], stats[:, 32:48], float(P ** -0.5), None, ALU.mult))
                for i in range(8):
                    t = four(T[:, i] if i < 4 else ktok[:, i - 4])
                    dve.tensor_tensor(t, t, stats[:, 32 + 4 * i:36 + 4 * i, None].broadcast_to([P, 4, P]), ALU.mult).then_inc(kq_ready, c.up("kq"))
                step(dve.tensor_tensor(z, z, e, ALU.add))
                step(dve.tensor_scalar(z, z, stats[0:8, 88:89], -1.0, ALU.mult, ALU.mult))
                ahead, back = T[0:8, 6], T[0:8, 5]
                for ch in range(4):
                    cs = slice(ch * P, ch * P + P)
                    dve.tensor_tensor_scan(ahead[:, cs], ones[0:8, :], z[:, cs], 0.0, ALU.mult, ALU.add)
                    rev = slice(ch * P + P - 1, ch * P - 1 if ch else None, -1)
                    ins = dve.tensor_tensor_scan(back[:, rev], ones[0:8, :], z[:, rev], 0.0, ALU.mult, ALU.add)
                step(ins)
                step(dve.tensor_scalar(ahead, ahead, small[0:8, FORWARD:FORWARD + 1], None, ALU.mult))
                dve.scalar_tensor_tensor(out=g_rows, in0=back, scalar=small[0:8, FORWARD + 1:FORWARD + 2], in1=ahead,
                                         op0=ALU.mult, op1=ALU.add).then_inc(rows_step, c.up("rows_step"))
                dve.wait_ge(bc_full, 1)
                dve.tensor_copy(gcol.rearrange("p c r -> p (c r)"), ps[5][:, 0:32]).then_inc(row_terms, c.up("terms"))
                step(dve.tensor_copy(bcol.rearrange("p c r -> p (c r)"), ps[4][:, 0:32]))
                dve.wait_ge(row_exps, c.next("exps"))
                dve.tensor_tensor(beg, beg, bcol, ALU.mult).then_inc(rows_step, c.up("rows_step"))
                dve.wait_ge(rows_step, c.now("rows_step"))
                dve.wait_ge(tab3_in, 16)
                def output_squares(r):
                    step(dve.tensor_tensor(T[:, 7], pt[:, AO + r], pt[:, AO + r], ALU.mult))
                    step(dve.tensor_reduce(stats[:, 4 * r:4 * r + 4], four(T[:, 7]), AX.X, ALU.add))

                for d, chunk_step, stage in lane_stages():
                    lane_dve(d, chunk_step, stage)
                    if (d, chunk_step) == (1, 3) and stage in (4, 8):
                        output_squares(stage // 4)
                for d in range(2):
                    dve.wait_ge(chunk_dve[d], c.now(f"cd{d}"))
                output_squares(0)
                output_squares(3)
                dve.sem_inc(row_terms, c.up("terms"))
                dve.wait_ge(row_exps, c.next("exps"))
                step(dve.reciprocal(stats[:, 16:32], stats[:, 0:16]))
                for r in range(4):
                    o = four(pt[:, AO + r])
                    dve.tensor_tensor(o, o, stats[:, 16 + 4 * r:20 + 4 * r, None].broadcast_to([P, 4, P]), ALU.mult).then_inc(oT_done, c.up("oT_done"))
                for h in range(4):
                    dve.wait_ge(ut_full, UT_BEFORE + h + 1)
                    dve.scalar_tensor_tensor(out=hf, in0=ps[7][:, :], scalar=small[:, G_OUT:G_OUT + 1], in1=pt[:, DG + h],
                                             op0=ALU.mult, op1=ALU.mult).then_inc(h_done, c.up("h"))
                    dve.wait_ge(h_done, c.now("h"))
                    dve.sem_inc(ut_copied, 1)
                    lower(4 + h)
                    dve.wait_ge(m_ready, c.now("m"))

            def lane_dve(d, s, stage):
                ch = s if d == 0 else 3 - s
                cs = slice(ch * P, ch * P + P)
                nt, sd, xx, xt, a1, qg, st = (four(t) for t in LANE[d])
                b0, b1, b2 = (four(ps[2 + 3 * d + i][:, :]) for i in range(3))
                eye4 = ident[:, None, :].broadcast_to([P, 4, P])
                per_head = lambda v: v[:, :, None].broadcast_to([P, 4, P])

                def products():
                    dve.wait_ge(chunk_mm[d], c.next(f"mm{d}"))

                def ready(ins):
                    ins.then_inc(chunk_dve[d], c.up(f"cd{d}"))

                if stage == 0:
                    last = P - 1 if d == 0 else 0
                    products()
                    g = gcol[:, ch, 4 * d:4 * d + 4]
                    dve.tensor_tensor(kgf[d], b0[:, :, last], g, ALU.subtract)
                    dve.tensor_copy(glast[d], b0[:, :, last])
                    for h in range(4):
                        ins = dve.scalar_tensor_tensor(out=a1[:, h], in0=b0[:, h], scalar=g[:, h:h + 1], in1=incl_mask(d),
                                                       op0=ALU.subtract, op1=ALU.add)
                    ins.then_inc(chunk_terms[d], c.up(f"terms{d}"))
                    products()
                    dve.wait_ge(chunk_act[d], c.next(f"ca{d}"))
                    dve.tensor_tensor(nt, b1, a1, ALU.mult).then_inc(dve_step, c.up("dve"))
                    dve.tensor_tensor(sd, b2, a1, ALU.mult)
                    dve.tensor_tensor(qg, qg, pt[:, DQ:DQ + 4, cs], ALU.mult)
                    dve.wait_ge(dve_step, c.now("dve"))
                    ready(dve.tensor_tensor(nt, nt, four(ps[d][:, :]), ALU.mult))
                elif stage < 15:
                    m, half = divmod(stage - 1, 2)
                    products()
                    if half == 0:
                        ready(dve.tensor_tensor(a1, b0, level_mask(d, m)[:, None, :].broadcast_to([P, 4, P]), ALU.mult))
                    elif m == 0:
                        dve.tensor_tensor(xx, eye4, a1, ALU.subtract)
                        ready(dve.tensor_tensor(xt, eye4, b2, ALU.subtract))
                    elif m < 6:
                        dve.tensor_tensor(xx, xx, b1, ALU.subtract)
                        products()
                        ready(dve.tensor_tensor(xt, xt, b2, ALU.subtract))
                    else:
                        dve.tensor_tensor(nt, pt[:, DV:DV + 4, cs], per_head(bcol[:, ch, 4 * d:4 * d + 4]), ALU.mult)
                        dve.tensor_tensor(a1, ktok[:, :, cs], per_head(beg[:, ch, 4 * d:4 * d + 4]), ALU.mult)
                        ready(dve.tensor_tensor(xt, xt, b2, ALU.subtract))
                elif stage == 15:
                    products()
                    c.up(f"ca{d}")
                elif stage == 16:
                    if s:
                        products()
                        dve.tensor_tensor(xx, xx, b2, ALU.subtract)
                    ready(dve.tensor_tensor(nt, ktok[:, :, cs], per_head(kgf[d]), ALU.mult))
                else:
                    products()
                    for h in range(4):
                        if s:
                            dve.scalar_tensor_tensor(out=st[:, h], in0=st[:, h], scalar=glast[d][:, h:h + 1], in1=b1[:, h],
                                                     op0=ALU.mult, op1=ALU.add)
                    if not s:
                        dve.tensor_copy(st, b1)
                    o = four(pt[:, AO + ch])
                    ready(dve.tensor_copy(o, b0) if s < 2 else dve.tensor_tensor(o, o, b0, ALU.add))

            def cross():
                for h in range(4):
                    for q2 in range(2):
                        dve.wait_ge(sc_full, c.next("sc_full"))
                        top, share = stats[:, 48:50], stats[:, 56:58]
                        step(dve.tensor_reduce(top, ps[2][:, :].rearrange("p (q n) -> p q n", q=2), AX.X, ALU.max, negate=True))
                        dve.tensor_scalar(top, top, 0.0625, None, ALU.mult).then_inc(max_done, c.up("max"))
                        if h < 3:
                            scaled(q2, pt[:, 2 * h + 2 + q2])
                        dve.wait_ge(exp_done, c.next("exp"))
                        dve.sem_inc(sc_free, c.up("sc_free"))
                        step(dve.reciprocal(share, stats[:, 52:54]))
                        p = T[:, 0].rearrange("p (q n) -> p q n", q=2)
                        dve.tensor_tensor(p, p, share[:, :, None].broadcast_to([P, 2, 256]), ALU.mult).then_inc(prob_done, c.up("prob"))
                    for f in range(2):
                        dve.wait_ge(u_hi_done, c.next("u_hi"))
                        dve.tensor_tensor(tile(u_lo, 2 * h + f), ps[5 + f][:, :], tile(u_hi, 2 * h + f).bitcast(F32),
                                          ALU.subtract).then_inc(u_ready, c.up("u"))
                    dve.wait_ge(u_ready, c.now("u"))
                    dve.sem_inc(pv_copied, c.up("pv_copied"))

            dve.wait_ge(setup_in, 48)
            lam4 = lamv.rearrange("p (l m j) -> p l m j", l=2, m=2)
            dve.tensor_tensor(lamp.rearrange("p (l j) -> p l j", l=2), lam4[:, :, 0], lam4[:, :, 1], ALU.mult).then_inc(par_ready, 1)
            dve.wait_ge(loaded, 16)
            for k in range(KT):
                dve.wait_ge(x_in_part[k // 2], 16)
                prepare(k, small[:, TAIL["g_first"] + k:TAIL["g_first"] + k + 1])
            dve.wait_ge(act_step, 1)
            for l in range(2):
                a = l * LC + LAYER_COLS["neg_lam"]
                step(dve.tensor_tensor(small[:, a:a + 1], stats[:, 2 * l + 1:2 * l + 2], stats[:, 2 * l:2 * l + 1], ALU.subtract))
                step(dve.tensor_tensor(small[:, a:a + 1], small[:, a:a + 1], small[:, a + 2:a + 3], ALU.subtract))
            with c.loop(dve, LAYERS, PER["dve"]) as l:
                dve.wait_ge(u_ready, c.now("u"))
                step(dve.tensor_copy(par[:, :], small[:, ds(l * LC, LC)]))
                ffn(LAYER_COLS["g_mix"])
                mixers()
                ffn(LAYER_COLS["g_next"])
            second()




def arrays_of(i):
    jobs = []
    for l in range(LAYERS):
        jobs += ffn_jobs(i["w_ffn1_gate"][l], i["w_ffn1_up"][l], i["w_ffn1_down"][l])
        gate = i["w_gate"][l]
        a = [weight_jobs(gate[:, D * j:D * j + D]) for j in range(3)]
        jobs += [weight_jobs(i["w_in"][l]), np.zeros((1, P, D), np.float32)]
        jobs.append(np.stack([a[0], weight_jobs(i["w_br_a"][l])], 1).reshape(-1, P, D))
        gates = np.stack([a[1], a[2]], 1).reshape(-1, P, D)
        jobs += [gates[:2], weight_jobs(np.concatenate([i["w_br_b"][l], i["w_br_c"][l]])), gates[2:]]
        jobs.append(weight_jobs(i["w_out"][l]))
        jobs += ffn_jobs(i["w_ffn2_gate"][l], i["w_ffn2_up"][l], i["w_ffn2_down"][l])
    w = i["w_in_2"][0]
    heads = w[:, :512].reshape(D, 2, 4, 64).transpose(0, 2, 1, 3).reshape(D, 512)
    few = np.zeros((D, P), np.float32)
    few[:, 0:8], few[:, 32:40] = w[:, 2816:2824], w[:, 2824:2832]
    jobs += [weight_jobs(heads), weight_jobs(w[:, 512:2816]), weight_jobs(few), np.zeros((1, P, D), np.float32)]
    jobs += [weight_jobs(i["w_out_2"][0]), weight_jobs(i["w_ckv_2"][0]), weight_jobs(i["w_cq_2"][0]), weight_jobs(i["w_co_2"][0])]
    jobs += ffn_jobs(i["w_gate_up_2"][0][:, :2816], i["w_gate_up_2"][0][:, 2816:], i["w_down_2"][0])
    small = np.zeros((P, NSMALL), np.float32)
    for l in range(2):
        cols = {"g_mix": i["g_mix"][l], "g_ffn2": i["g_ffn2"][l], "b_gate": i["b_gate"][l], "subln": i["subln_g"][l],
                "g_next": i["g_ffn1"][l + 1] if l + 1 < 2 else i["g_final"]}
        for n, v in cols.items():
            a = l * LC + LAYER_COLS[n]
            small[:, a:a + v.size // P] = column_major(v)
    for l in range(2):
        small[:, l * LC + LAYER_COLS["lam_init"]] = 0.8 - 0.6 * np.exp(-0.3 * l)
        small[:, l * LC + LAYER_COLS["one_less"]] = 0.2 + 0.6 * np.exp(-0.3 * l)
    tail = {"g_first": i["g_ffn1"][0]}
    for n in TAIL:
        if n != "g_first":
            tail[n] = i[n + "_2"][0]
    for n, v in tail.items():
        small[:, TAIL[n]:TAIL[n] + 8] = column_major(v)
    small[:, SINK:SINK + 8] = i["attn_sink_2"][0][None, :]
    small[:, CONV:CONV + 60] = i["conv_w_2"][0].reshape(5, DN_TILES, P).transpose(2, 1, 0).reshape(P, 60)
    small[:, G_OUT] = i["g_dn_out_2"][0]
    small[:8, A_LOG] = i["a_log_2"][0].reshape(8)
    small[:8, DT_BIAS] = i["dt_bias_2"][0].reshape(8)
    small[:, INV_FREQ] = np.tile(np.float32(10000.0) ** (-np.arange(32, dtype=np.float32) / np.float32(32)), 4)
    small[:4, FORWARD] = small[4:8, FORWARD + 1] = 1
    return {
        "jobs": np.concatenate(jobs),
        "x_in": np.ascontiguousarray(i["x"][0].T.reshape(KT, P, S).transpose(1, 0, 2)),
        "small_in": small,
        "mem_in": np.ascontiguousarray(i["mem_2"][0].T.reshape(KT, P, 256).transpose(1, 0, 2)),
        "pos_in": i["positions_2"],
        "rel_in": i["rel_bias"],
        "lam_in": np.stack([i[n][l] for l in range(2) for n in ("lam_q1", "lam_q2", "lam_k1", "lam_k2")], 1),
        **{n + "_in": v for n, v in constants().items()},
    }


def kernel(**inputs):
    import concourse.bacc as bacc
    from concourse.bass_utils import run_bass_kernel_spmd

    nc = bacc.Bacc("TRN2", target_bir_lowering=False, num_devices=1)
    arrays = arrays_of(inputs)
    aps = [nc.dram_tensor(n, a.shape, mybir.dt.from_np(a.dtype), kind="ExternalInput").ap() for n, a in arrays.items()]
    out = nc.dram_tensor("out", (P, KT, S), F32, kind="ExternalOutput").ap()
    build(nc, *aps, out)
    r = run_bass_kernel_spmd(nc, [arrays], core_ids=[0])
    y = r.results[0]["out"]
    return np.ascontiguousarray(y.transpose(1, 0, 2).reshape(D, S).T)[None]
```
